# Optimizing a Trainium2 kernel written in Bass

```python
import math
import jax, jax.numpy as jnp
from jax import lax
import numpy as np
import jax
import jax.numpy as jnp

D_MODEL = 1024
BATCH = 1
SEQ = 512
DEPTH = 2

A_HEADS = 4
A_HEAD_DIM = 256
A_WIDTH = A_HEADS * A_HEAD_DIM
A_CHUNK = 64
CONV_WIDTH = 4
B_GROUPS = 4
B_GROUP_DIM = 256
B_WIDTH = B_GROUPS * B_GROUP_DIM
POOL_WINDOWS = (2, 4, 8, 16)
C_HEADS = 16
C_HEAD_DIM = 64
C_WIDTH = C_HEADS * C_HEAD_DIM
KV_RANK = 256
IDX_HEADS = 4
IDX_DIM = 64
TOP_K_MAX = 256
Q_BLOCK = 128
NUM_BUCKETS = 32
MAX_DISTANCE = 128
EPS = 1e-6

N_EVEN = (DEPTH + 1) // 2
N_ODD = DEPTH // 2
EVEN_SPLITS = (A_WIDTH, A_WIDTH, A_WIDTH, A_WIDTH, A_WIDTH, 2 * A_HEADS, B_WIDTH, B_WIDTH)
EVEN_IN = sum(EVEN_SPLITS)
ODD_SPLITS = (C_WIDTH, KV_RANK, IDX_HEADS * IDX_DIM, IDX_DIM, IDX_HEADS, C_WIDTH)
ODD_IN = sum(ODD_SPLITS)


def _split(p, sizes):
    pts = [int(v) for v in np.cumsum(sizes)[:-1]]
    return jnp.split(p, pts, axis=-1)

def rmsnorm(x, g):
    xf = x.astype(jnp.float32)
    y = xf * lax.rsqrt(jnp.mean(xf * xf, axis=-1, keepdims=True) + EPS)
    return (y * g.astype(jnp.float32)).astype(x.dtype)

def causal_conv(u, w):
    n_taps = w.shape[0]
    s_len = u.shape[1]
    up = jnp.pad(u, ((0, 0), (n_taps - 1, 0), (0, 0)))
    out = w[0] * up[:, 0:s_len]
    for j in range(1, n_taps):
        out = out + w[j] * up[:, j:j + s_len]
    return out

def mlstm_chunkwise(q, k, v, i_pre, f_pre):
    bsz, s_len, nh, dh = q.shape
    nc = s_len // A_CHUNK
    f32 = jnp.float32

    def to_chunks(a):
        return a.astype(f32).reshape(bsz, nc, A_CHUNK, nh, -1).transpose(1, 0, 3, 2, 4)

    def gate_chunks(a):
        return a.astype(f32).reshape(bsz, nc, A_CHUNK, nh).transpose(1, 0, 3, 2)

    qc = to_chunks(q)
    kc = to_chunks(k) * (dh ** -0.5)
    vc = to_chunks(v)
    ic = gate_chunks(i_pre)
    fc = gate_chunks(f_pre)
    causal = jnp.tril(jnp.ones((A_CHUNK, A_CHUNK), dtype=bool))

    def step(carry, inp):
        c_mat, n_vec, m_prev = carry
        qb, kb, vb, ib, fb = inp
        b = jnp.cumsum(jax.nn.log_sigmoid(fb), axis=-1)
        dmat = jnp.where(causal, b[..., :, None] - b[..., None, :] + ib[..., None, :], -jnp.inf)
        inter = b + m_prev[..., None]
        m_t = jnp.maximum(inter, jnp.max(dmat, axis=-1))
        w = jnp.exp(dmat - m_t[..., None]) * jnp.einsum('bhtd,bhsd->bhts', qb, kb)
        a_inter = jnp.exp(inter - m_t)
        num = a_inter[..., None] * jnp.einsum('bhvk,bhtk->bhtv', c_mat, qb) + jnp.einsum('bhts,bhsv->bhtv', w, vb)
        nq = a_inter * jnp.einsum('bhk,bhtk->bht', n_vec, qb) + jnp.sum(w, axis=-1)
        den = jnp.maximum(jnp.abs(nq), jnp.exp(-m_t))
        h = num / den[..., None]
        b_last = b[..., -1]
        g = b_last[..., None] - b + ib
        m_new = jnp.maximum(b_last + m_prev, jnp.max(g, axis=-1))
        decay = jnp.exp(b_last + m_prev - m_new)
        sw = jnp.exp(g - m_new[..., None])
        c_new = decay[..., None, None] * c_mat + jnp.einsum('bhs,bhsv,bhsk->bhvk', sw, vb, kb)
        n_new = decay[..., None] * n_vec + jnp.einsum('bhs,bhsk->bhk', sw, kb)
        return (c_new, n_new, m_new), h

    init = (jnp.zeros((bsz, nh, dh, dh), f32), jnp.zeros((bsz, nh, dh), f32), jnp.zeros((bsz, nh), f32))
    _, hs = lax.scan(step, init, (qc, kc, vc, ic, fc))
    return hs.transpose(1, 0, 3, 2, 4).reshape(bsz, s_len, nh, dh)

def multiscale_pool(u):
    bsz, s_len, _ = u.shape
    uf = u.astype(jnp.float32)
    cs = jnp.concatenate([jnp.zeros((bsz, 1, B_WIDTH), jnp.float32), jnp.cumsum(uf, axis=1)], axis=1)
    pos = jnp.arange(s_len)
    outs = []
    for gi, win in enumerate(POOL_WINDOWS):
        sl = slice(gi * B_GROUP_DIM, (gi + 1) * B_GROUP_DIM)
        cg = cs[:, :, sl]
        hi = cg[:, 1:]
        lo = jnp.concatenate([jnp.zeros((bsz, win - 1, B_GROUP_DIM), jnp.float32), cg[:, :s_len - win + 1]], axis=1)
        cnt = jnp.minimum(pos + 1, win).astype(jnp.float32)
        outs.append((hi - lo) / cnt[None, :, None] - uf[:, :, sl])
    return jnp.stack(outs, axis=2)

def t5_bucket(rel):
    rel = jnp.maximum(rel, 0)
    max_exact = NUM_BUCKETS // 2
    rel_f = jnp.maximum(rel, 1).astype(jnp.float32)
    large = max_exact + (jnp.log(rel_f / max_exact) / math.log(MAX_DISTANCE / max_exact)
                         * (NUM_BUCKETS - max_exact)).astype(jnp.int32)
    large = jnp.minimum(large, NUM_BUCKETS - 1)
    return jnp.where(rel < max_exact, rel, large)

def even_layer(x, g_norm, w_in, conv_w, b_if, g_head, w_pool, s_pool, w_out):
    bsz, s_len, _ = x.shape
    xn = rmsnorm(x, g_norm)
    p = xn @ w_in
    q, k, v, o, z_a, gates, u, z_b = _split(p, EVEN_SPLITS)
    qk = jax.nn.silu(causal_conv(jnp.concatenate([q, k], axis=-1), conv_w))
    q, k = qk[..., :A_WIDTH], qk[..., A_WIDTH:]
    gates = gates + b_if
    i_pre, f_pre = gates[..., :A_HEADS], gates[..., A_HEADS:]
    hd = (bsz, s_len, A_HEADS, A_HEAD_DIM)
    h = mlstm_chunkwise(q.reshape(hd), k.reshape(hd), v.reshape(hd), i_pre, f_pre)
    h = jax.nn.sigmoid(o.astype(jnp.float32)).reshape(hd) * h
    h = rmsnorm(h, g_head).reshape(bsz, s_len, A_WIDTH).astype(x.dtype)
    y_a = h * jax.nn.silu(z_a)
    pooled = multiscale_pool(u).astype(x.dtype)
    y_b = jnp.einsum('bsgc,gcd->bsgd', pooled, w_pool).reshape(bsz, s_len, B_WIDTH)
    y_b = y_b * s_pool * jax.nn.silu(z_b)
    return x + jnp.concatenate([y_a, y_b], axis=-1) @ w_out

def odd_layer(x, g_norm, w_in, g_kv, w_uk, w_uv, g_q, g_k, w_out, rel_bias):
    bsz, s_len, _ = x.shape
    xn = rmsnorm(x, g_norm)
    p = xn @ w_in
    q, ckv, qi, ki, wi, z = _split(p, ODD_SPLITS)
    hd = (bsz, s_len, C_HEADS, C_HEAD_DIM)
    q = rmsnorm(q.reshape(hd), g_q)
    ckv = rmsnorm(ckv, g_kv)
    k = rmsnorm((ckv @ w_uk).reshape(hd), g_k)
    v = (ckv @ w_uv).reshape(hd)
    qi = qi.reshape(bsz, s_len, IDX_HEADS, IDX_DIM).astype(jnp.float32) * (IDX_DIM ** -0.5)
    ki = ki.astype(jnp.float32)
    wi = wi.astype(jnp.float32) * (IDX_HEADS ** -0.5)
    top_k = min(TOP_K_MAX, s_len // 4)
    n_blocks = s_len // Q_BLOCK
    key_pos = jnp.arange(s_len)

    def block(start):
        qb = lax.dynamic_slice_in_dim(q, start, Q_BLOCK, axis=1)
        qib = lax.dynamic_slice_in_dim(qi, start, Q_BLOCK, axis=1)
        wib = lax.dynamic_slice_in_dim(wi, start, Q_BLOCK, axis=1)
        t = start + jnp.arange(Q_BLOCK)
        score = jnp.einsum('bqh,bqhs->bqs', wib, jax.nn.relu(jnp.einsum('bqhd,bsd->bqhs', qib, ki)))
        score = jnp.where((key_pos[None, :] <= t[:, None])[None], score, -jnp.inf)
        _, idx = lax.top_k(score, top_k)
        valid = idx <= t[None, :, None]
        ksel = jax.vmap(lambda kk, ii: kk[ii])(k, idx)
        vsel = jax.vmap(lambda vv, ii: vv[ii])(v, idx)
        logits = jnp.einsum('bqhd,bqkhd->bqhk', qb, ksel).astype(jnp.float32) * (C_HEAD_DIM ** -0.5)
        bias = rel_bias[t5_bucket(t[None, :, None] - idx)].astype(jnp.float32)
        logits = logits + bias.transpose(0, 1, 3, 2)
        logits = jnp.where(valid[:, :, None, :], logits, -jnp.inf)
        probs = jax.nn.softmax(logits, axis=-1).astype(v.dtype)
        return jnp.einsum('bqhk,bqkhd->bqhd', probs, vsel)

    out = lax.map(block, jnp.arange(n_blocks) * Q_BLOCK)
    out = out.transpose(1, 0, 2, 3, 4).reshape(bsz, s_len, C_WIDTH)
    return x + (out * jax.nn.silu(z)) @ w_out

def first_inputs(seed: int = 0) -> dict:
    key = jax.random.key(seed)
    ks = jax.random.split(key, 20)
    nrm = jax.random.normal
    f32 = jnp.float32
    b_i = 0.1 * nrm(ks[4], (N_EVEN, A_HEADS), f32)
    b_f = jnp.linspace(3.0, 6.0, A_HEADS, dtype=f32)[None] + 0.1 * nrm(ks[5], (N_EVEN, A_HEADS), f32)
    return {
        'x': nrm(ks[0], (BATCH, SEQ, D_MODEL), f32),
        'e_norm': 1.0 + 0.02 * nrm(ks[1], (N_EVEN, D_MODEL), f32),
        'e_w_in': nrm(ks[2], (N_EVEN, D_MODEL, EVEN_IN), f32) * D_MODEL ** -0.5,
        'e_conv': nrm(ks[3], (N_EVEN, CONV_WIDTH, 2 * A_WIDTH), f32) * CONV_WIDTH ** -0.5,
        'e_b_if': jnp.concatenate([b_i, b_f], axis=-1),
        'e_g_head': 1.0 + 0.02 * nrm(ks[6], (N_EVEN, A_HEADS, A_HEAD_DIM), f32),
        'e_w_pool': nrm(ks[7], (N_EVEN, B_GROUPS, B_GROUP_DIM, B_GROUP_DIM), f32) * B_GROUP_DIM ** -0.5,
        'e_s_pool': 1.0 + 0.02 * nrm(ks[8], (N_EVEN, B_WIDTH), f32),
        'e_w_out': nrm(ks[9], (N_EVEN, A_WIDTH + B_WIDTH, D_MODEL), f32) * (A_WIDTH + B_WIDTH) ** -0.5,
        'o_norm': 1.0 + 0.02 * nrm(ks[10], (N_ODD, D_MODEL), f32),
        'o_w_in': nrm(ks[11], (N_ODD, D_MODEL, ODD_IN), f32) * D_MODEL ** -0.5,
        'o_g_kv': 1.0 + 0.02 * nrm(ks[12], (N_ODD, KV_RANK), f32),
        'o_w_uk': nrm(ks[13], (N_ODD, KV_RANK, C_WIDTH), f32) * KV_RANK ** -0.5,
        'o_w_uv': nrm(ks[14], (N_ODD, KV_RANK, C_WIDTH), f32) * KV_RANK ** -0.5,
        'o_g_q': 1.0 + 0.02 * nrm(ks[15], (N_ODD, C_HEAD_DIM), f32),
        'o_g_k': 1.0 + 0.02 * nrm(ks[16], (N_ODD, C_HEAD_DIM), f32),
        'o_w_out': nrm(ks[17], (N_ODD, C_WIDTH, D_MODEL), f32) * C_WIDTH ** -0.5,
        'rel_bias': 0.5 * nrm(ks[18], (NUM_BUCKETS, C_HEADS), f32),
    }

def first_block(x, e_norm, e_w_in, e_conv, e_b_if, e_g_head, e_w_pool, e_s_pool, e_w_out,
              o_norm, o_w_in, o_g_kv, o_w_uk, o_w_uv, o_g_q, o_g_k, o_w_out, rel_bias):
    h = x
    for layer in range(DEPTH):
        j = layer // 2
        if layer % 2 == 0:
            h = even_layer(h, e_norm[j], e_w_in[j], e_conv[j], e_b_if[j], e_g_head[j],
                           e_w_pool[j], e_s_pool[j], e_w_out[j])
        else:
            h = odd_layer(h, o_norm[j], o_w_in[j], o_g_kv[j], o_w_uk[j], o_w_uv[j],
                          o_g_q[j], o_g_k[j], o_w_out[j], rel_bias)
    return h


N_MIXERS = 2
N_HEADS = 16
HEAD_DIM = 64
ATTN_WIDTH = N_HEADS * HEAD_DIM
A_KV_HEADS = 2
A_WINDOW = 128
B_KV_HEADS = 2
CMP_BLOCK = 32
CMP_STRIDE = 16
CMP_HIDDEN = 256
SEL_BLOCK = 64
SEL_TOPK = 16
SEL_LOCAL = 2
B_WINDOW = 512
REL_BUCKETS = 32
REL_MAX_DIST = 1024
D_FF = -(-(8 * D_MODEL) // (3 * 256)) * 256
BLOCK_Q = 128
SEL_QCHUNK = 64
RMS_EPS = 1e-6
NEG_INF = -1e30
FORCE_SCORE = 1e6
N_A_LAYERS = (DEPTH + 1) // 2
N_B_LAYERS = DEPTH // 2
A_QKV_WIDTH = ATTN_WIDTH + 2 * A_KV_HEADS * HEAD_DIM
B_IN_WIDTH = ATTN_WIDTH + 6 * B_KV_HEADS * HEAD_DIM + 3 * N_HEADS


def rms_norm(x, g):
    x32 = x.astype(jnp.float32)
    y = x32 * lax.rsqrt(jnp.mean(x32 * x32, axis=-1, keepdims=True) + RMS_EPS)
    return (y * g.astype(jnp.float32)).astype(x.dtype)

def t5_bucket_2(dist):
    n = jnp.maximum(dist, 0)
    max_exact = REL_BUCKETS // 2
    nf = jnp.maximum(n, 1).astype(jnp.float32)
    log_b = max_exact + (jnp.log(nf / max_exact) / math.log(REL_MAX_DIST / max_exact)
                         * (REL_BUCKETS - max_exact)).astype(jnp.int32)
    return jnp.where(n < max_exact, n, jnp.minimum(log_b, REL_BUCKETS - 1))

def head_bias(rel_table, dist, n_kv):
    b = rel_table.astype(jnp.float32)[t5_bucket_2(dist)]
    b = b.reshape(dist.shape + (n_kv, N_HEADS // n_kv))
    return jnp.moveaxis(b, (-2, -1), (0, 1))

def banded_attention(q, k, v, window, rel_table, sinks):
    B, S, hkv, g_sz, dh = q.shape
    nb = S // BLOCK_Q
    n_prev = (window - 1) // BLOCK_Q + 1
    span = (n_prev + 1) * BLOCK_Q
    pad = ((0, 0), (n_prev * BLOCK_Q, 0), (0, 0), (0, 0))
    kp = jnp.pad(k, pad)
    vp = jnp.pad(v, pad)
    qi = jnp.arange(BLOCK_Q)[:, None]
    kj = jnp.arange(span)[None, :]
    dist = qi - kj + n_prev * BLOCK_Q
    in_win = (dist >= 0) & (dist < window)
    bias = head_bias(rel_table, dist, hkv)
    qb = jnp.moveaxis(q.reshape(B, nb, BLOCK_Q, hkv, g_sz, dh), 1, 0)

    def block(args):
        n, qn = args
        start = n * BLOCK_Q
        kn = lax.dynamic_slice_in_dim(kp, start, span, axis=1)
        vn = lax.dynamic_slice_in_dim(vp, start, span, axis=1)
        s = jnp.einsum('bqhgd,bshd->bhgqs', qn, kn).astype(jnp.float32) + bias
        mask = in_win & (start - n_prev * BLOCK_Q + kj >= 0)
        s = jnp.where(mask, s, NEG_INF)
        if sinks is None:
            p = jax.nn.softmax(s, axis=-1)
        else:
            sk = sinks.astype(jnp.float32).reshape(hkv, g_sz, 1, 1)
            m = jnp.maximum(jnp.max(s, axis=-1, keepdims=True), sk)
            e = jnp.exp(s - m)
            p = e / (jnp.sum(e, axis=-1, keepdims=True) + jnp.exp(sk - m))
        return jnp.einsum('bhgqs,bshd->bqhgd', p.astype(vn.dtype), vn)

    out = lax.map(block, (jnp.arange(nb), qb))
    return jnp.moveaxis(out, 0, 1).reshape(B, S, hkv, g_sz, dh)

def swa_sink_mixer(h, w_qkv, b_qkv, sinks, w_o, b_o, rel_table):
    B, S, _ = h.shape
    g_sz = N_HEADS // A_KV_HEADS
    kvw = A_KV_HEADS * HEAD_DIM
    qkv = h @ w_qkv + b_qkv
    q = qkv[..., :ATTN_WIDTH].reshape(B, S, A_KV_HEADS, g_sz, HEAD_DIM) * HEAD_DIM ** -0.5
    k = qkv[..., ATTN_WIDTH:ATTN_WIDTH + kvw].reshape(B, S, A_KV_HEADS, HEAD_DIM)
    v = qkv[..., ATTN_WIDTH + kvw:].reshape(B, S, A_KV_HEADS, HEAD_DIM)
    o = banded_attention(q, k, v, A_WINDOW, rel_table, sinks)
    return o.reshape(B, S, ATTN_WIDTH) @ w_o + b_o

def compress(x_tok, pos, w1, w2):
    B, S, hkv, dh = x_tok.shape
    nc = (S - CMP_BLOCK) // CMP_STRIDE + 1
    idx = jnp.arange(nc)[:, None] * CMP_STRIDE + jnp.arange(CMP_BLOCK)[None, :]
    blocks = x_tok[:, idx] + pos[:, None, :]
    flat = jnp.moveaxis(blocks, 3, 2).reshape(B, nc, hkv, CMP_BLOCK * dh)
    return jax.nn.gelu(flat @ w1) @ w2

def nsa_mixer(h, w_in, cmp_pos, cmp_w1, cmp_w2, w_o, rel_table):
    B, S, _ = h.shape
    hkv, g_sz, dh = B_KV_HEADS, N_HEADS // B_KV_HEADS, HEAD_DIM
    kvw = hkv * dh
    proj = h @ w_in
    q = proj[..., :ATTN_WIDTH].reshape(B, S, hkv, g_sz, dh) * dh ** -0.5
    kv = proj[..., ATTN_WIDTH:ATTN_WIDTH + 6 * kvw].reshape(B, S, 6, hkv, dh)
    k_cmp, v_cmp, k_slc, v_slc, k_win, v_win = [kv[:, :, i] for i in range(6)]
    gates = jax.nn.sigmoid(proj[..., ATTN_WIDTH + 6 * kvw:].astype(jnp.float32))
    gates = gates.reshape(B, S, hkv, g_sz, 3).astype(h.dtype)

    kc = compress(k_cmp, cmp_pos[0], cmp_w1[0], cmp_w2[0])
    vc = compress(v_cmp, cmp_pos[1], cmp_w1[1], cmp_w2[1])
    nc = kc.shape[1]
    t = jnp.arange(S)[:, None]
    c_start = jnp.arange(nc) * CMP_STRIDE
    c_end = c_start + CMP_BLOCK - 1
    c_valid = c_end[None, :] <= t
    s_c = jnp.einsum('bshgd,bchd->bhgsc', q, kc).astype(jnp.float32)
    s_c = s_c + head_bias(rel_table, t - c_end[None, :], hkv)
    s_c = jnp.where(c_valid, s_c, NEG_INF)
    p_c = jax.nn.softmax(s_c, axis=-1) * c_valid
    o_cmp = jnp.einsum('bhgsc,bchd->bshgd', p_c.astype(h.dtype), vc)

    n_sel = S // SEL_BLOCK
    top_k = min(SEL_TOPK, n_sel)
    s_start = jnp.arange(n_sel) * SEL_BLOCK
    overlap = ((c_start[:, None] < s_start[None, :] + SEL_BLOCK)
               & (c_start[:, None] + CMP_BLOCK > s_start[None, :])).astype(jnp.float32)
    imp = jnp.einsum('bhgsc,cj->bhsj', p_c, overlap)
    cur = t // SEL_BLOCK
    jb = jnp.arange(n_sel)[None, :]
    forced = (jb == 0) | ((cur - jb >= 0) & (cur - jb < SEL_LOCAL))
    score = jnp.where(forced, FORCE_SCORE, jnp.where(jb <= cur, imp, -1.0))
    _, sel_idx = lax.top_k(score, top_k)

    ksb = jnp.moveaxis(k_slc.reshape(B, n_sel, SEL_BLOCK, hkv, dh), 3, 1)
    vsb = jnp.moveaxis(v_slc.reshape(B, n_sel, SEL_BLOCK, hkv, dh), 3, 1)
    n_ch = S // SEL_QCHUNK
    q_ch = jnp.moveaxis(q.reshape(B, n_ch, SEL_QCHUNK, hkv, g_sz, dh), 1, 0)
    idx_ch = jnp.moveaxis(sel_idx.reshape(B, hkv, n_ch, SEL_QCHUNK, top_k), 2, 0)
    bi = jnp.arange(B)[:, None, None, None]
    hi = jnp.arange(hkv)[None, :, None, None]
    table_h = rel_table.astype(jnp.float32).reshape(REL_BUCKETS, hkv, g_sz).transpose(1, 0, 2)
    n_keys = top_k * SEL_BLOCK

    def sel_chunk(args):
        c, qc, ic = args
        kg = ksb[bi, hi, ic].reshape(B, hkv, SEL_QCHUNK, n_keys, dh)
        vg = vsb[bi, hi, ic].reshape(B, hkv, SEL_QCHUNK, n_keys, dh)
        key_pos = (ic[..., None] * SEL_BLOCK + jnp.arange(SEL_BLOCK)).reshape(B, hkv, SEL_QCHUNK, n_keys)
        q_pos = c * SEL_QCHUNK + jnp.arange(SEL_QCHUNK)
        dist = q_pos[:, None] - key_pos
        bias = jnp.moveaxis(table_h[hi, t5_bucket_2(dist)], -1, 2)
        s = jnp.einsum('bqhgd,bhqkd->bhgqk', qc, kg).astype(jnp.float32) + bias
        s = jnp.where((dist >= 0)[:, :, None], s, NEG_INF)
        p = jax.nn.softmax(s, axis=-1)
        return jnp.einsum('bhgqk,bhqkd->bqhgd', p.astype(vg.dtype), vg)

    o_slc = lax.map(sel_chunk, (jnp.arange(n_ch), q_ch, idx_ch))
    o_slc = jnp.moveaxis(o_slc, 0, 1).reshape(B, S, hkv, g_sz, dh)

    o_win = banded_attention(q, k_win, v_win, B_WINDOW, rel_table, None)

    o = gates[..., 0:1] * o_cmp + gates[..., 1:2] * o_slc + gates[..., 2:3] * o_win
    return o.reshape(B, S, ATTN_WIDTH) @ w_o

def swiglu(h, w_gu, w_down):
    gate, up = jnp.split(h @ w_gu, 2, axis=-1)
    return (jax.nn.silu(gate) * up) @ w_down

def second_inputs(seed: int = 0) -> dict:
    key = jax.random.key(seed)
    ks = jax.random.split(key, 18)
    f32 = jnp.float32

    def nrm(k, shape, scale):
        return jax.random.normal(k, shape, f32) * scale

    res_scale = (2 * DEPTH) ** -0.5
    return {
        'x': nrm(ks[0], (BATCH, SEQ, D_MODEL), 1.0),
        'rel_table': nrm(ks[1], (REL_BUCKETS, N_HEADS), 0.5),
        'attn_norm': 1.0 + nrm(ks[2], (DEPTH, D_MODEL), 0.05),
        'ffn_norm': 1.0 + nrm(ks[3], (DEPTH, D_MODEL), 0.05),
        'final_norm': 1.0 + nrm(ks[4], (D_MODEL,), 0.05),
        'a_w_qkv': nrm(ks[5], (N_A_LAYERS, D_MODEL, A_QKV_WIDTH), D_MODEL ** -0.5),
        'a_b_qkv': nrm(ks[6], (N_A_LAYERS, A_QKV_WIDTH), 0.02),
        'a_sinks': nrm(ks[7], (N_A_LAYERS, N_HEADS), 1.0),
        'a_w_o': nrm(ks[8], (N_A_LAYERS, ATTN_WIDTH, D_MODEL), ATTN_WIDTH ** -0.5 * res_scale),
        'a_b_o': nrm(ks[9], (N_A_LAYERS, D_MODEL), 0.02),
        'b_w_in': nrm(ks[10], (N_B_LAYERS, D_MODEL, B_IN_WIDTH), D_MODEL ** -0.5),
        'b_cmp_pos': nrm(ks[11], (N_B_LAYERS, 2, CMP_BLOCK, HEAD_DIM), 0.1),
        'b_cmp_w1': nrm(ks[12], (N_B_LAYERS, 2, CMP_BLOCK * HEAD_DIM, CMP_HIDDEN), (CMP_BLOCK * HEAD_DIM) ** -0.5),
        'b_cmp_w2': nrm(ks[13], (N_B_LAYERS, 2, CMP_HIDDEN, HEAD_DIM), CMP_HIDDEN ** -0.5),
        'b_w_o': nrm(ks[14], (N_B_LAYERS, ATTN_WIDTH, D_MODEL), ATTN_WIDTH ** -0.5 * res_scale),
        'ffn_w_gu': nrm(ks[15], (DEPTH, D_MODEL, 2 * D_FF), D_MODEL ** -0.5),
        'ffn_w_down': nrm(ks[16], (DEPTH, D_FF, D_MODEL), D_FF ** -0.5 * res_scale),
    }

def second_block(x, rel_table, attn_norm, ffn_norm, final_norm, a_w_qkv, a_b_qkv, a_sinks, a_w_o, a_b_o,
              b_w_in, b_cmp_pos, b_cmp_w1, b_cmp_w2, b_w_o, ffn_w_gu, ffn_w_down):
    h = x
    for layer in range(DEPTH):
        hn = rms_norm(h, attn_norm[layer])
        j = layer // N_MIXERS
        if layer % N_MIXERS == 0:
            h = h + swa_sink_mixer(hn, a_w_qkv[j], a_b_qkv[j], a_sinks[j], a_w_o[j], a_b_o[j], rel_table)
        else:
            h = h + nsa_mixer(hn, b_w_in[j], b_cmp_pos[j], b_cmp_w1[j], b_cmp_w2[j], b_w_o[j], rel_table)
        h = h + swiglu(rms_norm(h, ffn_norm[layer]), ffn_w_gu[layer], ffn_w_down[layer])
    return rms_norm(h, final_norm)


def setup_inputs(seed=0):
    out = dict(first_inputs(seed))
    for name, value in second_inputs(seed + 1).items():
        if name != "x":
            out[name + "_2"] = value
    return out


def reference(
    x, e_norm, e_w_in, e_conv, e_b_if, e_g_head, e_w_pool, e_s_pool, e_w_out, o_norm, o_w_in,
    o_g_kv, o_w_uk, o_w_uv, o_g_q, o_g_k, o_w_out, rel_bias, rel_table_2, attn_norm_2,
    ffn_norm_2, final_norm_2, a_w_qkv_2, a_b_qkv_2, a_sinks_2, a_w_o_2, a_b_o_2, b_w_in_2,
    b_cmp_pos_2, b_cmp_w1_2, b_cmp_w2_2, b_w_o_2, ffn_w_gu_2, ffn_w_down_2,
):
    x = first_block(
        x, e_norm, e_w_in, e_conv, e_b_if, e_g_head, e_w_pool, e_s_pool, e_w_out, o_norm,
        o_w_in, o_g_kv, o_w_uk, o_w_uv, o_g_q, o_g_k, o_w_out, rel_bias,
    )
    return second_block(
        x, rel_table_2, attn_norm_2, ffn_norm_2, final_norm_2, a_w_qkv_2, a_b_qkv_2, a_sinks_2,
        a_w_o_2, a_b_o_2, b_w_in_2, b_cmp_pos_2, b_cmp_w1_2, b_cmp_w2_2, b_w_o_2, ffn_w_gu_2,
        ffn_w_down_2,
    )


_drawn_inputs = setup_inputs


def setup_inputs(seed=0):
    import zlib

    import numpy as np

    out = dict(_drawn_inputs(seed))
    spreads = {}
    factors = {'e_g_head': 5.278,
     'e_s_pool': 6.232,
     'o_norm': 4.941,
     'o_g_kv': 8.0,
     'o_g_q': 8.0,
     'o_g_k': 8.0,
     'attn_norm_2': 6.037,
     'a_b_qkv_2': 24.584,
     'a_sinks_2': 64.0,
     'a_b_o_2': 22.432,
     'b_cmp_pos_2': 200.0,
     'rel_table_2': 4.307,
     'ffn_norm_2': 8.0,
     'ffn_w_gu_2': 3.24,
     'ffn_w_down_2': 3.22,
     'b_w_in_2': 8.0,
     'b_cmp_w1_2': 8.0,
     'b_cmp_w2_2': 8.0,
     'b_w_o_2': 8.0}
    for name, (base, spread) in spreads.items():
        noise = np.random.default_rng([zlib.crc32(name.encode()), seed]).standard_normal(out[name].shape)
        drawn = base * np.exp(spread * noise) if base else spread * noise
        out[name] = jnp.asarray(drawn.astype(out[name].dtype))
    for name, factor in factors.items():
        out[name] = (out[name] * factor).astype(out[name].dtype)
    return out
```

```python
import math
from contextlib import ExitStack

import numpy as np

import concourse.bass as bass
from concourse import mybir

F32 = mybir.dt.float32
F32R = mybir.dt.float32r
ALU = mybir.AluOpType
ACT = mybir.ActivationFunctionType
AX_X = mybir.AxisListType.X

P = 128
SEQ = 512
DM = 1024
MT = DM // P
QT = SEQ // P
EPS = 1e-6
NEG = -1e30
CUT = -3e38
BEYOND = -1e38
CREDIT = 64
HD = 64
NH = 16
TOPK = 128
DFF = 2816
NCMP = 31
CREDITED = ["small_loads", "tile_turned", "tile_kept", "norm_squared", "norm_summed", "norm_var", "norm_std",
            "norm_inv", "norm_scaled", "norm_high", "norm_low", "weights_landed0", "weights_landed1",
            "weights_high", "weights_low", "tile_summed", "tile_steps",
            "gate_rows_spread", "mem_k_staged", "mem_v_staged", "mem_scores", "mem_gaps", "mem_decays", "mem_weighed",
            "mem_masked", "mem_read", "mem_tail", "bias_landed0", "bias_landed1", "bias_flipped", "bias_out", "att_staged", "att_scores", "att_logits", "att_peaks", "att_shifts", "att_probs", "att_sunk",
            "att_turned", "att_kept", "att_mixed", "att_dens", "att_outs"]
BIAS_L = 640


class Signal:

    def __init__(self, sem, base):
        self.sem = sem
        self.base = base

    def at(self, n):
        return n + self.base

    def advance(self, n):
        self.base += n


def rows(i, n=1):
    return bass.ds(i, n)


def flat(ap):
    return ap.rearrange("p a b -> p (a b)")


class Kernel:
    def __init__(self, nc, dram, ctx):
        self.nc, self.d, self.ctx = nc, dram, ctx
        self.signals = {}
        self.stage_n = 0
        self.ps = [ctx.enter_context(nc.psum_tensor(f"bank{i}", [P, 512], F32)) for i in range(8)]

    def sb(self, ctx, name, shape, dt=F32):
        return ctx.enter_context(self.nc.sbuf_tensor(name, shape, dt))

    def sig(self, name):
        if name not in self.signals:
            credit = CREDIT if name in CREDITED else 0
            self.signals[name] = Signal(self.ctx.enter_context(self.nc.semaphore(name)), credit)
        return self.signals[name]

    def block(self):
        return self.nc.Block(no_gpsimd_drain=True)

    def load(self, pairs):
        nc, arrived = self.nc, self.sig("small_loads")
        with self.block() as block:
            @block.sync
            def _(sp):
                for dst, src in pairs:
                    sp.dma_start(dst, src, allow_slow_non_contiguous=True).then_inc(arrived.sem, 16)
                sp.wait_ge(arrived.sem, arrived.at(16 * len(pairs)))
        arrived.advance(16 * len(pairs))

    def turn(self, tiles, src, dst):
        nc, turned, kept = self.nc, self.sig("tile_turned"), self.sig("tile_kept")
        with self.block() as block:
            @block.tensor
            def _(pe):
                for m in range(tiles):
                    pe.wait_ge(kept.sem, kept.at(m - 1))
                    for t in range(4):
                        ins = nc.tensor.transpose(self.ps[m % 2][:, t * P:(t + 1) * P], src(m, t), self.ident[:, :])
                    ins.then_inc(turned.sem, 1)

            @block.vector
            def _(dve):
                for m in range(tiles):
                    dve.wait_ge(turned.sem, turned.at(m + 1))
                    nc.vector.tensor_copy(dst(m), self.ps[m % 2][:, :].rearrange("p (t c) -> p t c", t=4)).then_inc(kept.sem, 1)
        turned.advance(tiles)
        kept.advance(tiles)

    def norm(self, groups, per, src, gain, out, hi=None, lo=None, mat=None, width=None):
        nc = self.nc
        n = groups * per
        mat = self.ones if mat is None else mat
        width = per * P if width is None else width
        squared, summed = self.sig("norm_squared"), self.sig("norm_summed")
        var, std, inv = self.sig("norm_var"), self.sig("norm_std"), self.sig("norm_inv")
        scaled, high, low = self.sig("norm_scaled"), self.sig("norm_high"), self.sig("norm_low")
        with ExitStack() as ctx:
            sq = self.sb(ctx, f"sq{self.stage_n}", [P, 2, 512])
            rs = self.sb(ctx, f"rs{self.stage_n}", [P, 2, 3, 512])
            self.stage_n += 1
            block = ctx.enter_context(self.block())

            @block.scalar
            def _(act):
                def squares(g):
                    for t in range(per):
                        m = g * per + t
                        act.wait_ge(summed.sem, summed.at(m - 1))
                        nc.scalar.activation(sq[:, m % 2, :], src(m), ACT.Square).then_inc(squared.sem, 1)

                squares(0)
                for g in range(groups):
                    if g + 1 < groups:
                        squares(g + 1)
                    act.wait_ge(var.sem, var.at(g + 1))
                    act.wait_ge(inv.sem, inv.at(g - 1))
                    nc.scalar.activation(rs[:, g % 2, 1, :], rs[:, g % 2, 0, :], ACT.Sqrt).then_inc(std.sem, 1)
                    if hi is not None:
                        for t in range(per):
                            m = g * per + t
                            act.wait_ge(scaled.sem, scaled.at(m + 1))
                            nc.scalar.activation(hi(m), out(m), ACT.Copy).then_inc(high.sem, 1)

            @block.tensor
            def _(pe):
                for g in range(groups):
                    pe.wait_ge(var.sem, var.at(g - 1))
                    for t in range(per):
                        m = g * per + t
                        pe.wait_ge(squared.sem, squared.at(m + 1))
                        nc.tensor.matmul(self.ps[g % 2][:, :], mat[:, :], sq[:, m % 2, :], start=(t == 0),
                                         stop=(t == per - 1)).then_inc(summed.sem, 1)

            @block.vector
            def _(dve):
                for g in range(groups):
                    dve.wait_ge(summed.sem, summed.at((g + 1) * per))
                    dve.wait_ge(std.sem, std.at(g - 1))
                    nc.vector.tensor_scalar(rs[:, g % 2, 0, :], self.ps[g % 2][:, :], 1.0 / width, EPS, ALU.mult,
                                            ALU.add).then_inc(var.sem, 1)
                    dve.wait_ge(std.sem, std.at(g + 1))
                    dve.wait_ge(scaled.sem, scaled.at((g - 1) * per))
                    nc.vector.reciprocal(rs[:, g % 2, 2, :], rs[:, g % 2, 1, :]).then_inc(inv.sem, 1)
                    dve.wait_ge(inv.sem, inv.at(g + 1))
                    for t in range(per):
                        m = g * per + t
                        if hi is not None:
                            dve.wait_ge(high.sem, high.at(m - 1))
                            dve.wait_ge(low.sem, low.at(m - 1))
                        nc.vector.scalar_tensor_tensor(out(m), src(m), gain(m), rs[:, g % 2, 2, :], ALU.mult,
                                                       ALU.mult).then_inc(scaled.sem, 1)
                        if hi is not None and m >= 1:
                            dve.wait_ge(high.sem, high.at(m))
                            nc.vector.tensor_tensor(lo(m - 1), out(m - 1), hi(m - 1).bitcast(F32),
                                                    ALU.subtract).then_inc(low.sem, 1)
                    if hi is not None and g == groups - 1:
                        dve.wait_ge(high.sem, high.at(n))
                        nc.vector.tensor_tensor(lo(n - 1), out(n - 1), hi(n - 1).bitcast(F32),
                                                ALU.subtract).then_inc(low.sem, 1)
        squared.advance(n)
        summed.advance(n)
        for s in (var, std, inv):
            s.advance(groups)
        scaled.advance(n)
        if hi is not None:
            high.advance(n)
            low.advance(n)

    def dense(self, pairs, kc, cpt, weights, x_hi, x_lo, steps, rolled=True):
        nc = self.nc
        U = 2 * cpt
        L = [len(steps[0]), len(steps[1])]
        LB = L[0] + L[1]
        raw, whi, wlo = self.raw, self.whi, self.wlo
        landed = [self.sig("weights_landed0"), self.sig("weights_landed1")]
        high, low = self.sig("weights_high"), self.sig("weights_low")
        summed, evac = self.sig("tile_summed"), self.sig("tile_steps")
        pieces = len(weights(0, 0, 0))

        def done_steps(i, j, k):
            return evac.at(i * LB + (L[0] if j else 0) + k)

        def wait_chunk(i, j, half):
            return i * U + j * cpt + half

        def loop(eng, n, body):
            if rolled and n > 1:
                with eng.Fori(0, n) as i:
                    body(i)
            else:
                for i in range(n):
                    body(i)

        with self.block() as block:
            @block.sync
            def _(sp):
                def body(i):
                    for j in range(2):
                        for half in range(cpt):
                            c = wait_chunk(i, j, half)
                            slot = (j * cpt + half) % 2
                            sp.wait_ge(low.sem, low.at(c - 1))
                            for c0, n, ap in weights(i, j, half):
                                sp.dma_start(raw[:, slot, 0:kc, c0:c0 + n], ap).then_inc(landed[slot].sem, 16)

                loop(sp, pairs, body)

            def split(eng, i, j):
                for half in range(cpt):
                    c = wait_chunk(i, j, half)
                    slot = (j * cpt + half) % 2
                    a = raw[:, slot, 0:kc, :]
                    h, lw = whi[:, slot, 0:kc, :], wlo[:, slot, 0:kc, :]
                    if eng is scalar_engine[0]:
                        nth = i * cpt + ((j * cpt + half) // 2 + 1)
                        eng.wait_ge(landed[slot].sem, landed[slot].at(nth * 16 * pieces))
                        eng.wait_ge(summed.sem, summed.at(c - 1))
                        nc.scalar.activation(h, a, ACT.Copy).then_inc(high.sem, 1)
                    else:
                        eng.wait_ge(high.sem, high.at(c + 1))
                        nc.vector.tensor_tensor(lw, a, h.bitcast(F32), ALU.subtract).then_inc(low.sem, 1)

            scalar_engine = [None]

            def after(eng, who, i, j):
                for k, (engine, step) in enumerate(steps[j]):
                    if engine != who:
                        continue
                    if k == 0:
                        eng.wait_ge(summed.sem, summed.at(i * U + (j + 1) * cpt))
                    eng.wait_ge(evac.sem, done_steps(i, j, k))
                    step(i, self.ps[j][:, :]).then_inc(evac.sem, 1)

            def splitter(eng, who):
                def body(i):
                    split(eng, i, 1)
                    after(eng, who, i, 0)
                    split(eng, i + 1, 0)
                    after(eng, who, i, 1)

                split(eng, 0, 0)
                if pairs > 1:
                    loop(eng, pairs - 1, body)
                split(eng, pairs - 1, 1)
                after(eng, who, pairs - 1, 0)
                after(eng, who, pairs - 1, 1)

            @block.scalar
            def _(act):
                scalar_engine[0] = act
                splitter(act, "act")

            @block.vector
            def _(dve):
                splitter(dve, "dve")

            @block.tensor
            def _(pe):
                def body(i):
                    for j in range(2):
                        pe.wait_ge(evac.sem, done_steps(i, j, -L[1 - j]))
                        for half in range(cpt):
                            slot = (j * cpt + half) % 2
                            pe.wait_ge(low.sem, low.at(wait_chunk(i, j, half) + 1))
                            for k in range(kc):
                                kt = half * kc + k
                                first, last = kt == 0, kt == cpt * kc - 1
                                out = self.ps[j][:, :]
                                nc.tensor.matmul(out, wlo[:, slot, k, :], x_hi(kt), start=first, stop=False)
                                nc.tensor.matmul(out, whi[:, slot, k, :], x_lo(kt), start=False, stop=False)
                                ins = nc.tensor.matmul(out, whi[:, slot, k, :], x_hi(kt), start=False, stop=last)
                            ins.then_inc(summed.sem, 1)

                loop(pe, pairs, body)
        for s in landed:
            s.advance(pairs * cpt * 16 * pieces)
        for s in (high, low, summed):
            s.advance(pairs * U)
        evac.advance(pairs * LB)

    def columns(self, w, kc, first, stride, pair_stride):
        def of(i, j, half):
            src = w[half * kc * P:(half + 1) * kc * P, :]
            return [(0, P, src[:, rows(i * pair_stride + (first + j * stride), P)].rearrange("(k p) c -> p k c", p=P))]
        return of

    def listed(self, w, kc, tiles):
        def of(i, j, half):
            out, at = [], 0
            for c, n in tiles[2 * i + j]:
                out.append((at, n, w[half * kc * P:(half + 1) * kc * P, c:c + n].rearrange("(k p) c -> p k c", p=P)))
                at += n
            return out
        return of

    def keep(self, dst, engine="act"):
        nc = self.nc

        def step(j):
            if engine == "act":
                return [("act", lambda i, ps: nc.scalar.activation(dst(i, j), ps, ACT.Copy))]
            return [("dve", lambda i, ps: nc.vector.tensor_copy(dst(i, j), ps))]
        return [step(0), step(1)]

    def add_residual(self, bias=None):
        nc, hT = self.nc, self.hT

        def step(j):
            if bias is None:
                return [("dve", lambda i, ps: nc.vector.tensor_tensor(
                    flat(hT[:, rows(i * 2 + j), :]), ps, flat(hT[:, rows(i * 2 + j), :]), ALU.add))]
            return [("dve", lambda i, ps: nc.vector.scalar_tensor_tensor(
                flat(hT[:, rows(i * 2 + j), :]), ps, bias[:, rows(i * 2 + j)], flat(hT[:, rows(i * 2 + j), :]),
                ALU.add, ALU.add))]
        return [step(0), step(1)]

    def norm_stream(self, gain, x_hi, x_lo, tmp):
        self.norm(1, MT, lambda m: self.hT[:, m, :], lambda m: gain[:, m:m + 1], lambda m: tmp[:, m % 2, :],
                  lambda m: x_hi[:, m, :], lambda m: x_lo[:, m, :])

    def setup(self):
        nc, d, ctx = self.nc, self.d, self.ctx
        self.hT = self.sb(ctx, "hT", [P, MT, 512])
        self.ident = self.sb(ctx, "ident", [P, P])
        self.ones = self.sb(ctx, "ones", [P, P])
        self.raw = self.sb(ctx, "raw", [P, 2, 11, P])
        self.whi = self.sb(ctx, "whi", [P, 2, 11, P], F32R)
        self.wlo = self.sb(ctx, "wlo", [P, 2, 11, P], F32R)
        self.gains = self.sb(ctx, "gains", [P, 6, MT])
        self.xs_hi = self.sb(ctx, "x_hi", [P, MT, 512], F32R)
        self.xs_lo = self.sb(ctx, "x_lo", [P, MT, 512], F32R)
        self.xtmp = self.sb(ctx, "x_tmp", [P, 2, 512])

        for n in CREDITED:
            self.sig(n)
        started = self.ctx.enter_context(nc.semaphore("started"))
        with self.block() as block:
            @block.gpsimd
            def _(pool):
                for n in CREDITED:
                    pool.sem_inc(self.signals[n].sem, CREDIT)
                nc.gpsimd.memset(self.ones[:, :], 1.0).then_inc(started, 1)
                pool.wait_ge(started, 1)

        gain = lambda ap: ap.rearrange("(m p) -> p m", p=P)
        with ExitStack() as c:
            xin = self.sb(c, "xin", [P, QT, DM])
            self.load([(self.ident[:, :], d["c_ident"]), (xin[:, :, :], d["x"][0].rearrange("(t p) c -> p t c", p=P)),
                       (self.gains[:, 0, :], gain(d["e_norm"][0])), (self.gains[:, 1, :], gain(d["o_norm"][0])),
                       (self.gains[:, 2, :], gain(d["attn_norm_2"][0])), (self.gains[:, 3, :], gain(d["attn_norm_2"][1])),
                       (self.gains[:, 4, :], gain(d["ffn_norm_2"][0])), (self.gains[:, 5, :], gain(d["ffn_norm_2"][1]))])
            self.turn(MT, lambda m, t: xin[:, t, m * P:(m + 1) * P],
                      lambda m: self.hT[:, m, :].rearrange("p (t c) -> p t c", t=4))

    def even(self):
        nc, d = self.nc, self.d
        w = d["e_w_in"][0]
        hi, lo = self.xs_hi, self.xs_lo
        xh, xl = (lambda k: hi[:, k, :]), (lambda k: lo[:, k, :])
        self.norm_stream(self.gains[:, 0, :], hi, lo, self.xtmp)
        with ExitStack() as c:
            yb = self.sb(c, "yb", [P, MT, 512])
            ha = self.sb(c, "ha", [P, MT, 512])
            tmp = self.sb(c, "even_tmp", [P, 3, 512])
            small = self.sb(c, "even_small", [P, 96])
            conv, ghead, spool = small[:, 0:64], small[:, 64:72], small[:, 72:80]
            bif = small[0:4, 80:82]
            gain = lambda ap: ap.rearrange("(m p) -> p m", p=P)
            self.load([(conv.rearrange("p (m j) -> p m j", j=4)[:, :, j], gain(d["e_conv"][0, j])) for j in range(4)]
                      + [(ghead, gain(d["e_g_head"][0].rearrange("a b -> (a b)"))), (spool, gain(d["e_s_pool"][0])),
                         (bif, d["e_b_if"][0].rearrange("(k h) -> h k", h=4))])

            with ExitStack() as c2:
                u = self.sb(c2, "u", [P, MT, 512])
                self.dense(4, 8, 1, self.columns(w, 8, 5128, P, 256), xh, xl,
                           self.keep(lambda i, j: flat(u[:, rows(i * 2 + j), :])))
                self.pool(u, yb)
            gate = lambda j: [
                ("act", lambda i, ps: nc.scalar.activation(tmp[:, j, :], ps, ACT.Silu)),
                ("dve", lambda i, ps: nc.vector.scalar_tensor_tensor(
                    flat(yb[:, rows(i * 2 + j), :]), flat(yb[:, rows(i * 2 + j), :]), spool[:, rows(i * 2 + j)],
                    tmp[:, j, :], ALU.mult, ALU.mult))]
            self.dense(4, 8, 1, self.columns(w, 8, 6152, P, 256), xh, xl, [gate(0), gate(1)])

            with ExitStack() as c2:
                vt = self.sb(c2, "vt", [P, QT, DM])
                self.dense(4, 8, 1, self.columns(w, 8, 2048, P, 256), xh, xl,
                           self.keep(lambda i, j: flat(ha[:, rows(i * 2 + j), :])))
                self.turn(MT, lambda m, t: ha[:, m, t * P:(t + 1) * P], lambda m: vt[:, :, m * P:(m + 1) * P])

                qk = self.sb(c2, "qk", [P, 16, 512])
                acol = self.sb(c2, "acol", [P, QT, 4])
                with ExitStack() as c3:
                    pad = self.sb(c3, "pad", [P, 2, 516])
                    self.clear(pad[:, :, 0:4])

                    def conv_steps(j):
                        def tap(t):
                            def f(i, ps):
                                wt = conv[:, rows(i * 8 + (4 * j + t))]
                                if t == 0:
                                    return nc.vector.tensor_scalar(tmp[:, j, :], pad[:, j, 1:513], wt, None, ALU.mult)
                                return nc.vector.scalar_tensor_tensor(tmp[:, j, :], pad[:, j, 1 + t:513 + t], wt,
                                                                      tmp[:, j, :], ALU.mult, ALU.add)
                            return ("dve", f)
                        return ([("act", lambda i, ps: nc.scalar.activation(pad[:, j, 4:516], ps, ACT.Copy))]
                                + [tap(t) for t in range(4)]
                                + [("act", lambda i, ps: nc.scalar.activation(flat(qk[:, rows(i * 2 + j), :]),
                                                                              tmp[:, j, :], ACT.Silu))])
                    self.dense(8, 8, 1, self.columns(w, 8, 0, P, 256), xh, xl, [conv_steps(0), conv_steps(1)])

                with ExitStack() as c3:
                    gi = self.sb(c3, "gates", [4, 2, 512])
                    gk = [[("act", lambda i, ps, j=j: nc.scalar.activation(gi[:, j, :], ps[0:4, :], ACT.Identity,
                                                                           bias=bif[:, j:j + 1]))] for j in range(2)]
                    self.dense(1, 8, 1, self.columns(w, 8, 5120, 4, 8), xh, xl, gk, rolled=False)
                    self.stabilize(c3, gi, acol)
                self.recall(c2, qk, vt, acol, ha)

            gate_o = lambda j: [
                ("act", lambda i, ps: nc.scalar.activation(tmp[:, j, :], ps, ACT.Sigmoid)),
                ("dve", lambda i, ps: nc.vector.tensor_tensor(flat(ha[:, rows(i * 2 + j), :]), tmp[:, j, :],
                                                              flat(ha[:, rows(i * 2 + j), :]), ALU.mult))]
            self.dense(4, 8, 1, self.columns(w, 8, 3072, P, 256), xh, xl, [gate_o(0), gate_o(1)])
            self.norm(4, 2, lambda m: ha[:, m, :], lambda m: ghead[:, m:m + 1], lambda m: ha[:, m, :])
            gate_z = lambda j: [
                ("act", lambda i, ps: nc.scalar.activation(tmp[:, j, :], ps, ACT.Silu)),
                ("dve", lambda i, ps: nc.vector.tensor_tensor(flat(ha[:, rows(i * 2 + j), :]), tmp[:, j, :],
                                                              flat(ha[:, rows(i * 2 + j), :]), ALU.mult))]
            self.dense(4, 8, 1, self.columns(w, 8, 4096, P, 256), xh, xl, [gate_z(0), gate_z(1)])

            y_hi, y_lo = self.sb(c, "y_hi", [P, 16, 512], F32R), self.sb(c, "y_lo", [P, 16, 512], F32R)
            self.split_tiles(16, lambda m: (ha if m < 8 else yb)[:, m % 8, :], lambda m: y_hi[:, m, :],
                             lambda m: y_lo[:, m, :])
            self.dense(4, 8, 2, self.columns(d["e_w_out"][0], 8, 0, P, 256), lambda k: y_hi[:, k, :],
                       lambda k: y_lo[:, k, :], self.add_residual())

    def clear(self, ap):
        nc, cleared = self.nc, self.sig("cleared")
        with self.block() as block:
            @block.vector
            def _(dve):
                nc.vector.memset(ap, 0.0).then_inc(cleared.sem, 1)

    def split_tiles(self, n, src, hi, lo):
        nc, high = self.nc, self.sig("norm_high")
        with self.block() as block:
            @block.scalar
            def _(act):
                for m in range(n):
                    nc.scalar.activation(hi(m), src(m), ACT.Copy).then_inc(high.sem, 1)

            @block.vector
            def _(dve):
                for m in range(n):
                    dve.wait_ge(high.sem, high.at(m + 1))
                    nc.vector.tensor_tensor(lo(m), src(m), hi(m).bitcast(F32), ALU.subtract)
        high.advance(n)

    def pool(self, u, yb):
        nc, d = self.nc, self.d
        step, mixed, kept = self.sig("pool_step"), self.sig("pool_mixed"), self.sig("pool_kept")
        with ExitStack() as c:
            win = self.sb(c, "win", [P, 2, 2, 512])
            pooled = self.sb(c, "pooled", [P, MT, 512])
            wp = self.sb(c, "wp", [P, 4, 2, 256])
            cnt = self.sb(c, "cnt", [P, 4, 512])
            self.load([(wp[:, g], d["e_w_pool"][0, g].rearrange("(k p) c -> p k c", p=P)) for g in range(4)]
                      + [(cnt[:, :, :], d["c_pool"])])
            with self.block() as block:
                @block.vector
                def _(dve):
                    n = 0

                    def link(ins):
                        nonlocal n
                        n += 1
                        ins.then_inc(step.sem, 1)
                        dve.wait_ge(step.sem, n)

                    for g in range(4):
                        src = u[:, 2 * g:2 * g + 2, :]
                        cur = src
                        for b in range(g + 1):
                            w = 1 << b
                            nxt = win[:, b % 2]
                            link(nc.vector.tensor_copy(nxt[:, :, 0:w], cur[:, :, 0:w]))
                            link(nc.vector.tensor_tensor(nxt[:, :, w:512], cur[:, :, w:512], cur[:, :, 0:512 - w], ALU.add))
                            cur = nxt
                        for t in range(2):
                            link(nc.vector.tensor_tensor(pooled[:, 2 * g + t, :], cur[:, t, :], cnt[:, g, :], ALU.mult))
                        link(nc.vector.tensor_tensor(pooled[:, 2 * g:2 * g + 2, :], pooled[:, 2 * g:2 * g + 2, :], src,
                                                     ALU.subtract))
                    step.base = n
            with self.block() as block:
                @block.tensor
                def _(pe):
                    for m in range(MT):
                        g, t = m // 2, m % 2
                        if m >= 2:
                            pe.wait_ge(kept.sem, m - 1)
                        for k in range(2):
                            ins = nc.tensor.matmul(self.ps[m % 2][:, :], wp[:, g, k, t * P:(t + 1) * P],
                                                   pooled[:, 2 * g + k, :], start=(k == 0), stop=(k == 1))
                        ins.then_inc(mixed.sem, 1)

                @block.scalar
                def _(act):
                    for m in range(MT):
                        act.wait_ge(mixed.sem, m + 1)
                        nc.scalar.activation(yb[:, m, :], self.ps[m % 2][:, :], ACT.Copy).then_inc(kept.sem, 1)

    def stabilize(self, c, gi, acol):
        nc, d = self.nc, self.d
        row, colsum = self.sig("gate_step"), self.sig("gate_turned")
        stored = self.sig("gate_rows_stored")
        rowsT = self.sb(c, "gate_rows", [4, 8, 512])
        scratch = d["s_rows"]
        i_pre, f_pre = gi[:, 0, :], gi[:, 1, :]
        t0, t1, F, a, M, m, one, em = [rowsT[:, k, :] for k in range(8)]
        with self.block() as block:
            @block.scalar
            def _(act):
                nc.scalar.activation(t0, f_pre, ACT.Abs).then_inc(row.sem, 1)
                act.wait_ge(row.sem, 1)
                nc.scalar.activation(t0, t0, ACT.Exp, scale=-1.0).then_inc(row.sem, 1)
                act.wait_ge(row.sem, 2)
                nc.scalar.activation(t0, t0, ACT.Ln, bias=1.0).then_inc(row.sem, 1)
                act.wait_ge(row.sem, 11)
                nc.scalar.activation(em, m, ACT.Exp, scale=-1.0).then_inc(row.sem, 1)

            @block.vector
            def _(dve):
                dve.wait_ge(row.sem, 3)
                nc.vector.memset(one, 1.0).then_inc(row.sem, 1)
                dve.wait_ge(row.sem, 4)
                nc.vector.tensor_scalar(t1, f_pre, 0.0, None, ALU.min).then_inc(row.sem, 1)
                dve.wait_ge(row.sem, 5)
                nc.vector.tensor_tensor(t1, t1, t0, ALU.subtract).then_inc(row.sem, 1)
                dve.wait_ge(row.sem, 6)
                nc.vector.tensor_tensor_scan(F, one, t1, 0.0, ALU.mult, ALU.add).then_inc(row.sem, 1)
                dve.wait_ge(row.sem, 7)
                nc.vector.tensor_tensor(a, i_pre, F, ALU.subtract).then_inc(row.sem, 1)
                dve.wait_ge(row.sem, 8)
                nc.vector.memset(t0, 0.0).then_inc(row.sem, 1)
                dve.wait_ge(row.sem, 9)
                nc.vector.tensor_tensor_scan(M, a, t0, 0.0, ALU.max, ALU.add).then_inc(row.sem, 1)
                dve.wait_ge(row.sem, 10)
                nc.vector.tensor_tensor(m, F, M, ALU.add).then_inc(row.sem, 1)
                dve.wait_ge(colsum.sem, 1)
                nc.vector.tensor_copy(acol[:, :, :], self.ps[0][:, 0:16].rearrange("p (t h) -> p t h", t=4))

            @block.tensor
            def _(pe):
                pe.wait_ge(row.sem, 8)
                for t in range(4):
                    ins = nc.tensor.transpose(self.ps[0][:, 4 * t:4 * t + 4], a[:, t * P:(t + 1) * P], self.ident[0:4, 0:4])
                ins.then_inc(colsum.sem, 1)

            @block.sync
            def _(sp):
                sp.wait_ge(row.sem, 12)
                sp.dma_start(scratch[0], M).then_inc(stored.sem, 16)
                sp.dma_start(scratch[1], em).then_inc(stored.sem, 16)
                sp.wait_ge(stored.sem, 32)

    def recall(self, c, qk, vt, acol, ha):
        nc, scratch = self.nc, self.d["s_rows"]
        spread = self.sig("gate_rows_spread")
        kh = self.sb(c, "kh", [P, 2, 512])
        vh = self.sb(c, "vh", [P, QT, 256])
        W = self.sb(c, "Wst", [P, QT, 512])
        Mb = self.sb(c, "Mb", [P, 2, 512])
        D = self.sb(c, "Dst", [P, 2, 512])
        den = self.sb(c, "den", [P, 2, 512])
        tri = self.sb(c, "tri", [P, P])
        self.load([(tri[:, :], self.d["c_tri"])])
        k_staged, v_staged = self.sig("mem_k_staged"), self.sig("mem_v_staged")
        scores, gaps, decays = self.sig("mem_scores"), self.sig("mem_gaps"), self.sig("mem_decays")
        weighed, masked = self.sig("mem_weighed"), self.sig("mem_masked")
        read, tail = self.sig("mem_read"), self.sig("mem_tail")
        with self.block() as block:
            @block.sync
            def _(sp):
                with sp.Fori(0, 4) as h:
                    sp.wait_ge(tail.sem, h * 5 + CREDIT)
                    sp.dma_start(Mb[:, 0, :], scratch[0, rows(h), :].broadcast_to([P, 512])).then_inc(spread.sem, 16)
                    sp.dma_start(Mb[:, 1, :], scratch[1, rows(h), :].broadcast_to([P, 512])).then_inc(spread.sem, 16)

            @block.scalar
            def _(act):
                with act.Fori(0, 4) as h:
                    act.wait_ge(tail.sem, h * 5 + CREDIT)
                    nc.scalar.activation(kh[:, :, :], qk[:, rows(h * 2 + 8, 2), :], ACT.Copy,
                                         scale=256 ** -0.5).then_inc(k_staged.sem, 1)
                    for s in range(QT):
                        n = 512 - s * P
                        act.wait_ge(gaps.sem, h * 4 + (s + 1 + CREDIT))
                        nc.scalar.activation(D[:, s % 2, 0:n], D[:, s % 2, 0:n], ACT.Exp, scale=-1.0).then_inc(decays.sem, 1)

            @block.vector
            def _(dve):
                with dve.Fori(0, 4) as h:
                    dve.wait_ge(tail.sem, h * 5 + CREDIT)
                    nc.vector.tensor_copy(vh[:, :, :], vt[:, :, rows(h * 256, 256)]).then_inc(v_staged.sem, 1)
                    dve.wait_ge(spread.sem, h * 32 + (32 + CREDIT))
                    for s in range(QT):
                        n, t = 512 - s * P, s * P
                        dve.wait_ge(weighed.sem, h * 4 + (s - 1 + CREDIT))
                        nc.vector.tensor_scalar(D[:, s % 2, 0:n], Mb[:, 0, t:512], acol[:, s, rows(h)], 0.0, ALU.subtract,
                                                ALU.max).then_inc(gaps.sem, 1)
                        dve.wait_ge(decays.sem, h * 4 + (s + 1 + CREDIT))
                        dve.wait_ge(scores.sem, h * 4 + (s + 1 + CREDIT))
                        nc.vector.tensor_tensor(W[:, s, 0:n], D[:, s % 2, 0:n], self.ps[s % 2][:, 0:n],
                                                ALU.mult).then_inc(weighed.sem, 1)
                    dve.wait_ge(read.sem, h * 3 + (1 + CREDIT))
                    nc.vector.scalar_tensor_tensor(den[:, 0, :], self.ps[4][:, :], -1.0, Mb[:, 1, :], ALU.mult,
                                                   ALU.max).then_inc(tail.sem, 1)
                    dve.wait_ge(tail.sem, h * 5 + (1 + CREDIT))
                    nc.vector.tensor_tensor(den[:, 0, :], self.ps[4][:, :], den[:, 0, :], ALU.max).then_inc(tail.sem, 1)
                    dve.wait_ge(tail.sem, h * 5 + (2 + CREDIT))
                    nc.vector.reciprocal(den[:, 1, :], den[:, 0, :]).then_inc(tail.sem, 1)
                    dve.wait_ge(tail.sem, h * 5 + (3 + CREDIT))
                    for v in range(2):
                        dve.wait_ge(read.sem, h * 3 + (2 + v + CREDIT))
                        nc.vector.tensor_tensor(flat(ha[:, rows(h * 2 + v), :]), self.ps[2 + v][:, :], den[:, 1, :],
                                                ALU.mult).then_inc(tail.sem, 1)

            @block.gpsimd
            def _(pool):
                with pool.Fori(0, 4) as h:
                    for s in range(QT):
                        pool.wait_ge(weighed.sem, h * 4 + (s + 1 + CREDIT))
                        nc.gpsimd.tensor_tensor(W[:, s, 0:P], W[:, s, 0:P], tri[:, :], ALU.mult).then_inc(masked.sem, 1)

            @block.tensor
            def _(pe):
                with pe.Fori(0, 4) as h:
                    pe.wait_ge(k_staged.sem, h + (1 + CREDIT))
                    for s in range(QT):
                        n, t = 512 - s * P, s * P
                        pe.wait_ge(weighed.sem, h * 4 + (s - 1 + CREDIT))
                        for k in range(2):
                            ins = nc.tensor.matmul(self.ps[s % 2][:, 0:n], kh[:, k, s * P:(s + 1) * P],
                                                   flat(qk[:, rows(h * 2 + k), t:512]), start=(k == 0), stop=(k == 1))
                        ins.then_inc(scores.sem, 1)
                    pe.wait_ge(masked.sem, h * 4 + (4 + CREDIT))
                    pe.wait_ge(v_staged.sem, h + (1 + CREDIT))
                    pe.wait_ge(tail.sem, h * 5 + CREDIT)
                    for o, lhs in ((4, None), (2, 0), (3, 1)):
                        for s in range(QT):
                            n, t = 512 - s * P, s * P
                            st = self.ones[:, :] if lhs is None else vh[:, s, lhs * P:(lhs + 1) * P]
                            ins = nc.tensor.matmul(self.ps[o][:, t:512], st, W[:, s, 0:n], start=(s == 0),
                                                   stop=(s == QT - 1))
                        ins.then_inc(read.sem, 1)

    def bias_tiles(self, table, onehot, dst, n):
        nc, d = self.nc, self.d
        made, kept, stored = self.sig("bias_made"), self.sig("bias_kept"), self.sig("bias_stored")
        scratch = d["s_bias"]
        with ExitStack() as c:
            tab = self.sb(c, f"tab{self.stage_n}", [33, NH])
            hot = self.sb(c, f"hot{self.stage_n}", [33, BIAS_L])
            vec = self.sb(c, f"vec{self.stage_n}", [NH, BIAS_L])
            self.stage_n += 1
            self.load([(tab[0:32, :], table), (tab[32:33, :], d["c_one"]), (hot[:, :], onehot)])
            with self.block() as block:
                @block.tensor
                def _(pe):
                    nc.tensor.matmul(self.ps[0][0:NH, :], tab[:, :], hot[:, 0:512], start=True, stop=True)
                    nc.tensor.matmul(self.ps[1][0:NH, 0:P], tab[:, :], hot[:, 512:640], start=True,
                                     stop=True).then_inc(made.sem, 1)

                @block.scalar
                def _(act):
                    act.wait_ge(made.sem, made.at(1))
                    nc.scalar.activation(vec[:, 0:512], self.ps[0][0:NH, :], ACT.Copy).then_inc(kept.sem, 1)
                    nc.scalar.activation(vec[:, 512:640], self.ps[1][0:NH, 0:P], ACT.Copy).then_inc(kept.sem, 1)

                @block.sync
                def _(sp):
                    sp.wait_ge(kept.sem, kept.at(2))
                    sp.dma_start(scratch, vec[:, :]).then_inc(stored.sem, 16)
                    sp.wait_ge(stored.sem, stored.at(16))
            made.advance(1)
            kept.advance(2)
            stored.advance(16)
            flip = self.sb(c, f"flip{self.stage_n}", [P, P])
            skew = self.sb(c, f"skew{self.stage_n}", [P, 2, 2, n])
            self.load([(flip[:, :], d["c_flip"])])
            chunks = NH // 2
            landed = [self.sig("bias_landed0"), self.sig("bias_landed1")]
            flipped, out = self.sig("bias_flipped"), self.sig("bias_out")
            with self.block() as block:
                @block.sync
                def _(sp):
                    for g in range(chunks):
                        sp.wait_ge(flipped.sem, flipped.at(2 * (g - 1)))
                        src = bass.AP(tensor=scratch.tensor, offset=scratch.offset + 2 * g * BIAS_L + 512 - n,
                                      ap=[[1, P], [BIAS_L, 2], [1, n]])
                        sp.dma_start(skew[:, g % 2], src).then_inc(landed[g % 2].sem, 16)

                @block.tensor
                def _(pe):
                    for g in range(chunks):
                        pe.wait_ge(landed[g % 2].sem, landed[g % 2].at(16 * (g // 2 + 1)))
                        for h in range(2):
                            pe.wait_ge(out.sem, out.at(2 * g + h - 1))
                            nc.tensor.matmul(self.ps[h][:, 0:n], flip[:, :], skew[:, g % 2, h, :], start=True,
                                             stop=True).then_inc(flipped.sem, 1)

                @block.scalar
                def _(act):
                    for h in range(NH):
                        act.wait_ge(flipped.sem, flipped.at(h + 1))
                        nc.scalar.activation(dst[:, h, :], self.ps[h % 2][:, 0:n], ACT.Copy).then_inc(out.sem, 1)
            for q in landed:
                q.advance(16 * chunks // 2)
            flipped.advance(NH)
            out.advance(NH)

    def attention(self, q, k, k_shape, v, per_loop, keys, bias, out, add=False, mask=None, sink=None, gate=None,
                  few=False):
        nc = self.nc
        loops = NH // per_loop
        units = [(pp, t, half) for pp in range(per_loop // 2) for t in range(QT) for half in range(2)]
        NU = len(units)
        sg = self.sig
        staged, scores, logits, peaks = sg("att_staged"), sg("att_scores"), sg("att_logits"), sg("att_peaks")
        shifts, probs, sunk = sg("att_shifts"), sg("att_probs"), sg("att_sunk")
        turned, kept, mixed = sg("att_turned"), sg("att_kept"), sg("att_mixed")
        dens, outs = sg("att_dens"), sg("att_outs")
        n_logits = 2 if mask is not None else 1
        n_staged = 2 + few
        n_dens = 1 + (sink is not None) + (gate is not None)
        with ExitStack() as c:
            n = self.stage_n
            self.stage_n += 1
            qs = self.sb(c, f"qs{n}", [P, per_loop // 2, 512])
            ks = self.sb(c, f"ks{n}", [P, *k_shape])
            vs = self.sb(c, f"vs{n}", [32, HD]) if few else None
            prob = self.sb(c, f"prob{n}", [P, 2, 512])
            pT = self.sb(c, f"pT{n}", [P, 2, 4, P])
            st = self.sb(c, f"stat{n}", [P, 4, 8])
            S, T, O = self.ps[0:2], self.ps[2:4], self.ps[4:6]
            block = c.enter_context(self.block())

            def head(i, u):
                return i * per_loop + (2 * units[u][0] + units[u][2])

            def stat(u, k):
                return st[:, u % 4, k:k + 1]

            @block.tensor
            def _(pe):
                def score(i, u):
                    pp, t, half = units[u]
                    k0, nk, _ = keys(t)
                    if u == 0:
                        pe.wait_ge(staged.sem, staged.at(i * n_staged + n_staged))
                    pe.wait_ge(logits.sem, logits.at((i * NU + (u - 1)) * n_logits))
                    nc.tensor.matmul(S[u % 2][:, 0:nk], qs[64 * half:64 * half + 64, pp, t * P:(t + 1) * P],
                                     ks[64 * half:64 * half + 64, pp % k_shape[0], k0:k0 + nk], start=True, stop=True).then_inc(scores.sem, 1)

                def turn(i, u):
                    _, nk, blocks = keys(units[u][1])
                    pe.wait_ge(probs.sem, probs.at(i * NU + (u + 1)))
                    pe.wait_ge(kept.sem, kept.at(i * NU + (u - 1)))
                    for b, (_, r) in enumerate(blocks):
                        ins = nc.tensor.transpose(T[u % 2][0:r, b * P:(b + 1) * P], prob[:, u % 2, b * P:b * P + r],
                                                  self.ident[:, :])
                    ins.then_inc(turned.sem, 1)

                def mix(i, u):
                    _, _, blocks = keys(units[u][1])
                    pe.wait_ge(outs.sem, outs.at(i * NU + (u - 1)))
                    pe.wait_ge(kept.sem, kept.at(i * NU + (u + 1)))
                    for b, (kb, r) in enumerate(blocks):
                        val = vs[0:r, :] if few else v(i, units[u], kb, r)
                        ins = nc.tensor.matmul(O[u % 2][:, 0:HD], pT[0:r, u % 2, b, :], val,
                                               start=(b == 0), stop=(b == len(blocks) - 1))
                    ins.then_inc(mixed.sem, 1)

                with pe.Fori(0, loops) as i:
                    for j in range(NU + 2):
                        if j < NU:
                            score(i, j)
                        if j >= 2:
                            mix(i, j - 2)
                        if 1 <= j <= NU:
                            turn(i, j - 1)

            @block.vector
            def _(dve):
                def logit(i, u):
                    _, t, _ = units[u]
                    k0, nk, _ = keys(t)
                    pr = prob[:, u % 2, 0:nk]
                    dve.wait_ge(turned.sem, turned.at(i * NU + (u - 1)))
                    dve.wait_ge(scores.sem, scores.at(i * NU + (u + 1)))
                    nc.vector.scalar_tensor_tensor(pr, S[u % 2][:, 0:nk], HD ** -0.5, bias(head(i, u), t, nk),
                                                   ALU.mult, ALU.add).then_inc(logits.sem, 1)
                    if mask is not None:
                        dve.wait_ge(logits.sem, logits.at((i * NU + u) * 2 + 1))
                        nc.vector.tensor_tensor(pr, pr, mask(t, nk), ALU.add).then_inc(logits.sem, 1)
                    dve.wait_ge(logits.sem, logits.at((i * NU + (u + 1)) * n_logits))
                    nc.vector.tensor_reduce(stat(u, 0), pr, AX_X, ALU.max).then_inc(peaks.sem, 1)
                    dve.wait_ge(peaks.sem, peaks.at(i * NU + (u + 1)))
                    if sink is None:
                        nc.vector.tensor_scalar(stat(u, 1), stat(u, 0), -1.0, None, ALU.mult).then_inc(shifts.sem, 1)
                    else:
                        nc.vector.tensor_scalar(stat(u, 1), stat(u, 0), sink[:, rows(head(i, u))], -1.0, ALU.max,
                                                ALU.mult).then_inc(shifts.sem, 1)

                def finish(i, u):
                    _, t, _ = units[u]
                    h = head(i, u)
                    b = (i * NU + u) * n_dens
                    k = 0
                    dve.wait_ge(mixed.sem, mixed.at(i * NU + (u + 1)))
                    if sink is not None:
                        dve.wait_ge(sunk.sem, sunk.at(i * NU + (u + 1)))
                        nc.vector.tensor_tensor(stat(u, 2), stat(u, 2), stat(u, 3), ALU.add).then_inc(dens.sem, 1)
                        k += 1
                        dve.wait_ge(dens.sem, dens.at(b + k))
                    nc.vector.reciprocal(stat(u, 4), stat(u, 2)).then_inc(dens.sem, 1)
                    k += 1
                    dve.wait_ge(dens.sem, dens.at(b + k))
                    if gate is not None:
                        nc.vector.tensor_tensor(stat(u, 4), stat(u, 4), gate(h, t), ALU.mult).then_inc(dens.sem, 1)
                        k += 1
                        dve.wait_ge(dens.sem, dens.at(b + k))
                    o = out[:, t, rows(h * HD, HD)]
                    if add:
                        nc.vector.scalar_tensor_tensor(o, O[u % 2][:, 0:HD], stat(u, 4), o, ALU.mult,
                                                       ALU.add).then_inc(outs.sem, 1)
                    else:
                        nc.vector.tensor_scalar(o, O[u % 2][:, 0:HD], stat(u, 4), None, ALU.mult).then_inc(outs.sem, 1)

                with dve.Fori(0, loops) as i:
                    for j in range(NU + 2):
                        if j < NU:
                            logit(i, j)
                        if j >= 2:
                            finish(i, j - 2)

            @block.scalar
            def _(act):
                def exp(i, u):
                    _, nk, _ = keys(units[u][1])
                    pr = prob[:, u % 2, 0:nk]
                    act.wait_ge(shifts.sem, shifts.at(i * NU + (u + 1)))
                    nc.scalar.activation(pr, pr, ACT.Exp, bias=stat(u, 1), accum_out=stat(u, 2)).then_inc(probs.sem, 1)
                    if sink is not None:
                        nc.scalar.activation(stat(u, 3), sink[:, rows(head(i, u))], ACT.Exp,
                                             bias=stat(u, 1)).then_inc(sunk.sem, 1)

                def keep(i, u):
                    _, _, blocks = keys(units[u][1])
                    r, nb = blocks[0][1], len(blocks)
                    act.wait_ge(mixed.sem, mixed.at(i * NU + (u - 1)))
                    act.wait_ge(turned.sem, turned.at(i * NU + (u + 1)))
                    nc.scalar.activation(pT[0:r, u % 2, 0:nb, :].rearrange("p b q -> p (b q)"),
                                         T[u % 2][0:r, 0:nb * P], ACT.Copy).then_inc(kept.sem, 1)

                with act.Fori(0, loops) as i:
                    act.wait_ge(scores.sem, scores.at(i * NU))
                    nc.scalar.activation(qs[:, :, :], q(i), ACT.Copy).then_inc(staged.sem, 1)
                    nc.scalar.activation(ks[:, :, :], k(i), ACT.Copy).then_inc(staged.sem, 1)
                    if few:
                        act.wait_ge(mixed.sem, mixed.at(i * NU))
                        nc.scalar.activation(vs[0:NCMP, :], v(i), ACT.Copy).then_inc(staged.sem, 1)
                    for j in range(NU + 1):
                        if j < NU:
                            exp(i, j)
                        if j >= 1:
                            keep(i, j - 1)
        total = loops * NU
        staged.advance(n_staged * loops)
        logits.advance(total * n_logits)
        dens.advance(total * n_dens)
        if sink is not None:
            sunk.advance(total)
        for s in (scores, peaks, shifts, probs, turned, kept, mixed, outs):
            s.advance(total)

    @staticmethod
    def causal(t):
        return 0, (t + 1) * P, [(b, P) for b in range(t + 1)]

    def odd(self):
        nc, d = self.nc, self.d
        w = d["o_w_in"][0]
        hi, lo = self.xs_hi, self.xs_lo
        xh, xl = (lambda k: hi[:, k, :]), (lambda k: lo[:, k, :])
        self.norm_stream(self.gains[:, 1, :], hi, lo, self.xtmp)
        with ExitStack() as c:
            otok = self.sb(c, "otok", [P, QT, DM])
            with ExitStack() as c2:
                qT = self.sb(c2, "qT", [P, MT, 512])
                kT = self.sb(c2, "kT", [P, MT, 512])
                vt = self.sb(c2, "vt2", [P, QT, DM])
                mask = self.sb(c2, "mask", [P, QT, 512])
                with ExitStack() as c3:
                    ckv = self.sb(c3, "ckv", [P, 2, 512])
                    qi = self.sb(c3, "qi", [P, 2, 512])
                    ki = self.sb(c3, "ki", [P, 512])
                    wi = self.sb(c3, "wi", [P, 512])
                    wit = self.sb(c3, "wit", [P, QT, P])
                    small = self.sb(c3, "odd_small", [P, 4])
                    halves = self.sb(c3, "halves", [P, P])
                    gq, gk, gkv = small[:, 0:1], small[:, 1:2], small[:, 2:4]
                    one = lambda ap: ap.rearrange("(p a) -> p a", a=1)
                    self.load([(small[64 * s:64 * s + 64, k:k + 1], one(d[nm][0])) for s in range(2)
                               for k, nm in enumerate(("o_g_q", "o_g_k"))]
                              + [(gkv, d["o_g_kv"][0].rearrange("(m p) -> p m", p=P)), (halves[:, :], d["c_halves"])])
                    self.dense(4, 8, 1, self.columns(w, 8, 0, P, 256), xh, xl,
                               self.keep(lambda i, j: flat(qT[:, rows(i * 2 + j), :])))
                    dsts = [ckv[:, 0, :], ckv[:, 1, :], qi[:, 0, :], qi[:, 1, :]]
                    self.dense(2, 8, 1, self.columns(w, 8, 1024, P, 256), xh, xl,
                               self.keep(lambda i, j: dsts[2 * i + j]), rolled=False)
                    tiles = [[(1536, 64), (1536, 64)], [(1600, 64), (1664, 64)]]
                    self.dense(1, 8, 1, self.listed(w, 8, tiles), xh, xl,
                               self.keep(lambda i, j: (ki, wi)[j][:, :]), rolled=False)
                    self.norm(8, 1, lambda m: qT[:, m, :], lambda m: gq, lambda m: qT[:, m, :], mat=halves, width=HD)
                    ch = self.sb(c3, "ckv_hi", [P, 2, 512], F32R)
                    cl = self.sb(c3, "ckv_lo", [P, 2, 512], F32R)
                    self.norm(1, 2, lambda m: ckv[:, m, :], lambda m: gkv[:, m:m + 1], lambda m: self.xtmp[:, m % 2, :],
                              lambda m: ch[:, m, :], lambda m: cl[:, m, :])
                    self.dense(4, 2, 1, self.columns(d["o_w_uk"][0], 2, 0, P, 256), lambda k: ch[:, k, :],
                               lambda k: cl[:, k, :], self.keep(lambda i, j: flat(kT[:, rows(i * 2 + j), :])))
                    self.norm(8, 1, lambda m: kT[:, m, :], lambda m: gk, lambda m: kT[:, m, :], mat=halves, width=HD)
                    vF = otok[:, :, :].rearrange("p t (a b) -> p (t a) b", b=512)
                    self.dense(4, 2, 1, self.columns(d["o_w_uv"][0], 2, 0, P, 256), lambda k: ch[:, k, :],
                               lambda k: cl[:, k, :], self.keep(lambda i, j: flat(vF[:, rows(i * 2 + j), :])))
                    self.turn(MT, lambda m, t: vF[:, m, t * P:(t + 1) * P], lambda m: vt[:, :, m * P:(m + 1) * P])
                    self.turn(1, lambda m, t: wi[:, t * P:(t + 1) * P], lambda m: wit[:, :, :])
                    self.choose(c3, qi, ki, wit, mask)
                bias = self.sb(c2, "bias_o", [P, NH, 512])
                self.bias_tiles(d["rel_bias"], d["c_hot_o"], bias[:, :, :], 512)
                self.attention(lambda i: qT[:, rows(i * 2, 2), :],
                               lambda i: kT[:, rows(i * 2, 2), :], (2, 512),
                               lambda i, u, kb, r: vt[0:r, kb, rows(i * 256 + (2 * u[0] + u[2]) * HD, HD)],
                               4, self.causal, lambda h, t, nk: flat(bias[:, rows(h), 512 - nk:512]), otok,
                               mask=lambda t, nk: mask[:, t, 0:nk])
            self.project_out(c, otok, d["o_w_out"][0], z=(w, 1604, xh, xl))

    def choose(self, c, qi, ki, wit, mask):
        nc, d = self.nc, self.d
        dots, acts, acc = self.sig("idx_dots"), self.sig("idx_relu"), self.sig("idx_step")
        sc = self.sb(c, "idx_score", [P, 512])
        rl = self.sb(c, "idx_relu_buf", [P, 2, 512])
        top = self.sb(c, "idx_top", [P, 8])
        later = self.sb(c, "idx_later", [P, P])
        self.load([(later[:, :], d["c_later"])])
        nrel = 12
        with self.block() as block:
            @block.tensor
            def _(pe):
                for n in range(nrel):
                    t, h = 1 + n // 4, n % 4
                    nk = (t + 1) * P
                    if n >= 2:
                        pe.wait_ge(acts.sem, n - 1)
                    s = 64 * (h % 2)
                    nc.tensor.matmul(self.ps[n % 2][:, 0:nk], qi[s:s + 64, h // 2, t * P:(t + 1) * P],
                                     ki[s:s + 64, 0:nk], start=True, stop=True).then_inc(dots.sem, 1)

            per_tile = 4 + 1 + 2 * (TOPK // 8) + 2

            def head_done(n):
                return (n // 4) * per_tile + n % 4 + 1 + 1

            @block.scalar
            def _(act):
                for n in range(nrel):
                    t = 1 + n // 4
                    nk = (t + 1) * P
                    act.wait_ge(dots.sem, n + 1)
                    if n >= 2:
                        act.wait_ge(acc.sem, head_done(n - 2))
                    nc.scalar.activation(rl[:, n % 2, 0:nk], self.ps[n % 2][:, 0:nk], ACT.Relu,
                                         scale=(64 ** -0.5) * (4 ** -0.5)).then_inc(acts.sem, 1)

            @block.vector
            def _(dve):
                n = 0

                def link(ins):
                    nonlocal n
                    n += 1
                    ins.then_inc(acc.sem, 1)
                    dve.wait_ge(acc.sem, n)

                link(nc.vector.memset(mask[:, 0, :], 0.0))
                for t in range(1, QT):
                    nk = (t + 1) * P
                    s = sc[:, 0:nk]
                    for h in range(4):
                        k = (t - 1) * 4 + h
                        dve.wait_ge(acts.sem, k + 1)
                        wt = wit[:, t, h:h + 1]
                        if h == 0:
                            link(nc.vector.tensor_scalar(s, rl[:, k % 2, 0:nk], wt, None, ALU.mult))
                        else:
                            link(nc.vector.scalar_tensor_tensor(s, rl[:, k % 2, 0:nk], wt, s, ALU.mult, ALU.add))
                    link(nc.vector.tensor_tensor(sc[:, t * P:nk], sc[:, t * P:nk], later[:, :], ALU.add))
                    for _ in range(TOPK // 8):
                        link(nc.vector.max(top[:, :], s))
                        link(nc.vector.match_replace(s, top[:, :], s, CUT))
                    link(nc.vector.tensor_scalar(s, s, CUT, 1.0, ALU.is_equal, ALU.subtract))
                    link(nc.vector.tensor_scalar(mask[:, t, 0:nk], s, -NEG, None, ALU.mult))

    def project_out(self, c, otok, w_out, z=None, bias=None):
        nc = self.nc
        oT = self.sb(c, f"oT{self.stage_n}", [P, MT, 512])
        o_hi = self.sb(c, f"o_hi{self.stage_n}", [P, MT, 512], F32R)
        o_lo = self.sb(c, f"o_lo{self.stage_n}", [P, MT, 512], F32R)
        tmp = self.sb(c, f"o_tmp{self.stage_n}", [P, 2, 512])
        self.stage_n += 1
        self.turn(MT, lambda m, t: otok[:, t, m * P:(m + 1) * P], lambda m: oT[:, m, :].rearrange("p (t c) -> p t c", t=4))
        if z is not None:
            w, col, xh, xl = z
            gate = lambda j: [
                ("act", lambda i, ps: nc.scalar.activation(tmp[:, j, :], ps, ACT.Silu)),
                ("dve", lambda i, ps: nc.vector.tensor_tensor(flat(oT[:, rows(i * 2 + j), :]), tmp[:, j, :],
                                                              flat(oT[:, rows(i * 2 + j), :]), ALU.mult))]
            self.dense(4, 8, 1, self.columns(w, 8, col, P, 256), xh, xl, [gate(0), gate(1)])
        self.split_tiles(MT, lambda m: oT[:, m, :], lambda m: o_hi[:, m, :], lambda m: o_lo[:, m, :])
        self.dense(4, 8, 1, self.columns(w_out, 8, 0, P, 256), lambda k: o_hi[:, k, :], lambda k: o_lo[:, k, :],
                   self.add_residual(bias))

    def windowed(self):
        nc, d = self.nc, self.d
        w = d["a_w_qkv_2"][0]
        hi, lo = self.xs_hi, self.xs_lo
        xh, xl = (lambda k: hi[:, k, :]), (lambda k: lo[:, k, :])
        self.norm_stream(self.gains[:, 2, :], hi, lo, self.xtmp)
        with ExitStack() as c:
            otok = self.sb(c, "otok_w", [P, QT, DM])
            small = self.sb(c, "win_small", [P, 40])
            bq, bk, bv, bo, sink = small[:, 0:8], small[:, 8:10], small[:, 10:11], small[:, 11:19], small[:, 20:36]
            b = d["a_b_qkv_2"][0]
            col = lambda ap: ap.rearrange("(m p) -> p m", p=ap.shape[0] if ap.shape[0] < P else P)
            self.load([(bq, col(b[0:1024])), (bv, col(b[1152:1280])), (bo, col(d["a_b_o_2"][0])),
                       (sink, d["a_sinks_2"].broadcast_to([P, NH]))]
                      + [(small[64 * s:64 * s + 64, 8 + g:9 + g], col(b[1024 + 64 * g:1088 + 64 * g]))
                         for s in range(2) for g in range(2)])
            with ExitStack() as c2:
                qT = self.sb(c2, "qT_w", [P, MT, 512])
                kT = self.sb(c2, "kT_w", [P, 2, 512])
                vF = self.sb(c2, "vF_w", [P, 512])
                vt = self.sb(c2, "vt_w", [P, QT, P])
                bias = self.sb(c2, "bias_w", [P, NH, 256])
                step = lambda j: [("act", lambda i, ps: nc.scalar.activation(
                    flat(qT[:, rows(i * 2 + j), :]), ps, ACT.Identity, bias=bq[:, rows(i * 2 + j)]))]
                self.dense(4, 8, 1, self.columns(w, 8, 0, P, 256), xh, xl, [step(0), step(1)])
                dst = [(kT[:, 0, :], bk[:, 0:1]), (kT[:, 1, :], bk[:, 1:2]), (vF[:, :], bv), (vF[:, :], bv)]
                tiles = [[(1024, 64), (1024, 64)], [(1088, 64), (1088, 64)], [(1152, 64), (1216, 64)],
                         [(1152, 64), (1216, 64)]]
                step2 = lambda j: [("act", lambda i, ps: nc.scalar.activation(dst[2 * i + j][0], ps, ACT.Identity,
                                                                              bias=dst[2 * i + j][1]))]
                self.dense(2, 8, 1, self.listed(w, 8, tiles), xh, xl, [step2(0), step2(1)], rolled=False)
                self.turn(1, lambda m, t: vF[:, t * P:(t + 1) * P], lambda m: vt[:, :, :])
                self.bias_tiles(d["rel_table_2"], d["c_hot_w"], bias[:, :, :], 256)

                def keys(t):
                    return (0, P, [(0, P)]) if t == 0 else ((t - 1) * P, 2 * P, [(t - 1, P), (t, P)])
                self.attention(lambda i: qT[:, rows(i * 4, 4), :],
                               lambda i: kT[:, rows(i), :], (1, 512),
                               lambda i, u, kb, r: vt[0:r, kb, rows(i * HD, HD)],
                               8, keys, lambda h, t, nk: flat(bias[:, rows(h), 256 - nk:256]), otok, sink=sink)
            self.project_out(c, otok, d["a_w_o_2"][0], bias=bo)

    def feed_forward(self, layer):
        nc, d = self.nc, self.d
        w, wd = d["ffn_w_gu_2"][layer], d["ffn_w_down_2"][layer]
        hi, lo = self.xs_hi, self.xs_lo
        self.norm_stream(self.gains[:, 4 + layer, :], hi, lo, self.xtmp)
        T = DFF // P
        with ExitStack() as c:
            a_hi = self.sb(c, f"a_hi{layer}", [P, T, 512], F32R)
            a_lo = self.sb(c, f"a_lo{layer}", [P, T, 512], F32R)
            tmp = self.sb(c, f"ff_tmp{layer}", [P, 2, 512])
            gate = [("act", lambda i, ps: nc.scalar.activation(tmp[:, 0, :], ps, ACT.Silu))]
            up = [("dve", lambda i, ps: nc.vector.tensor_tensor(tmp[:, 1, :], ps, tmp[:, 0, :], ALU.mult)),
                  ("act", lambda i, ps: nc.scalar.activation(flat(a_hi[:, rows(i), :]), tmp[:, 1, :], ACT.Copy)),
                  ("dve", lambda i, ps: nc.vector.tensor_tensor(flat(a_lo[:, rows(i), :]), tmp[:, 1, :],
                                                                flat(a_hi[:, rows(i), :]).bitcast(F32), ALU.subtract))]
            self.dense(T, 8, 1, self.columns(w, 8, 0, DFF, P), lambda k: hi[:, k, :], lambda k: lo[:, k, :], [gate, up])
            self.dense(4, 11, 2, self.columns(wd, 11, 0, P, 256), lambda k: a_hi[:, k, :], lambda k: a_lo[:, k, :],
                       self.add_residual())

    def sparse(self):
        nc, d = self.nc, self.d
        w = d["b_w_in_2"][0]
        hi, lo = self.xs_hi, self.xs_lo
        xh, xl = (lambda k: hi[:, k, :]), (lambda k: lo[:, k, :])
        self.norm_stream(self.gains[:, 3, :], hi, lo, self.xtmp)
        with ExitStack() as c:
            otok = self.sb(c, "otok_s", [P, QT, DM])
            with ExitStack() as c2:
                qT = self.sb(c2, "qT_s", [P, MT, 512])
                kT = self.sb(c2, "kT_s", [P, 2, 2, 512])
                vt = self.sb(c2, "vt_s", [P, 2, QT, P])
                gt = self.sb(c2, "gt_s", [P, QT, P])
                kcT = self.sb(c2, "kcT", [P, 2, 32])
                vc = self.sb(c2, "vc", [32, 2, HD])
                seen = self.sb(c2, "seen", [P, 1])
                self.dense(4, 8, 1, self.columns(w, 8, 0, P, 256), xh, xl,
                           self.keep(lambda i, j: flat(qT[:, rows(i * 2 + j), :])))
                with ExitStack() as c3:
                    cT = self.sb(c3, "cmpT", [P, 2, 2, 512])
                    vF = self.sb(c3, "vF_s", [P, 3, 512])
                    kv = lambda i, h: (1024 + P * i + 64 * h, 64)
                    tiles, dsts = [], []
                    for i, dst in ((0, cT[:, 0]), (1, cT[:, 1]), (2, kT[:, 0]), (4, kT[:, 1])):
                        for h in range(2):
                            tiles.append([kv(i, h), kv(i, h)])
                            dsts.append(dst[:, h, :])
                    for n, i in enumerate((3, 5)):
                        tiles.append([kv(i, 0), kv(i, 1)])
                        dsts.append(vF[:, n, :])
                    for n in range(2):
                        tiles.append([(1712, 64), (1776, 64)])
                        dsts.append(vF[:, 2, :])
                    def step(j):
                        def f(i, ps):
                            return nc.scalar.activation(dsts[2 * i + j], ps, ACT.Sigmoid if 2 * i + j >= 10 else ACT.Copy)
                        return [("act", f)]
                    self.dense(6, 8, 1, self.listed(w, 8, tiles), xh, xl, [step(0), step(1)], rolled=False)
                    outs = [vt[:, 0], vt[:, 1], gt[:, :, :]]
                    self.turn(3, lambda m, t: vF[:, m, t * P:(t + 1) * P], lambda m: outs[m])
                    self.compress(c3, cT, kcT, vc)
                bias = self.sb(c2, "bias_s", [P, NH, 512])
                self.bias_tiles(d["rel_table_2"], d["c_hot_s"], bias[:, :, :], 512)
                self.load([(seen[:, :], d["c_seen"])])
                self.scale_rows(gt[:, 0, :], seen)
                gate = lambda g: lambda h, t: gt[:, t, rows(h * 3 + (80 + g))]
                qs = lambda i: qT[:, rows(i * 4, 4), :]

                def cmp_keys(t):
                    n = 8 * t + 7
                    return 0, n, [(0, n)]
                self.attention(qs, lambda i: kcT[:, rows(i), 0:NCMP], (1, NCMP),
                               lambda i: flat(vc[0:NCMP, rows(i), :]), 8, cmp_keys,
                               lambda h, t, nk: flat(bias[:, rows(h), 415 - P * t:416 - P * t + 16 * (nk - 1):16]), otok,
                               gate=gate(0), few=True)
                for b, (s, g) in enumerate(((0, 1), (1, 2))):
                    self.attention(qs, lambda i: kT[:, s, rows(i), :], (1, 512),
                                   lambda i, u, kb, r: vt[0:r, s, kb, rows(i * HD, HD)], 8, self.causal,
                                   lambda h, t, nk: flat(bias[:, rows(h), 512 - nk:512]), otok, add=True, gate=gate(g))
            self.project_out(c, otok, d["b_w_o_2"][0])

    def scale_rows(self, gt, seen):
        nc, done = self.nc, self.sig("rows_scaled")
        with self.block() as block:
            @block.vector
            def _(dve):
                g = gt[:, 80:128].rearrange("p (h g) -> p h g", g=3)[:, :, 0]
                nc.vector.tensor_scalar(g, g, seen[:, 0:1], None, ALU.mult).then_inc(done.sem, 1)

    def compress(self, c, cT, kcT, vc):
        nc, d = self.nc, self.d
        N = 2 * NCMP
        blk = self.sb(c, "cmp_blk", [P, 16, N])
        w1 = self.sb(c, "cmp_w1", [P, 16, 256])
        w2 = self.sb(c, "cmp_w2", [P, 2, P])
        pos = self.sb(c, "cmp_pos", [P, 16])
        hid = self.sb(c, "cmp_hid", [P, 2, N])
        arg = self.sb(c, "cmp_arg", [P, 2, N])
        built, made, step = self.sig("cmp_built"), self.sig("cmp_made"), self.sig("cmp_step")
        second, kept = self.sig("cmp_second"), self.sig("cmp_kept")
        for s in range(2):
            w2d = d["b_cmp_w2_2"][0, s].rearrange("(m p) c -> p m c", p=P)
            self.load([(w1[:, :, :], d["b_cmp_w1_2"][0, s].rearrange("(j p) c -> p j c", p=P)),
                       (w2[:, :, 0:HD], w2d), (w2[:, :, HD:P], w2d),
                       (pos[:, :], d["b_cmp_pos_2"][0, s].rearrange("(j e) c -> (e c) j", e=2))])
            with self.block() as block:
                @block.vector
                def _(dve):
                    for half in range(2):
                        r = slice(64 * half, 64 * half + 64)
                        for h in range(2):
                            x = cT[r, s, h, :].rearrange("p (b j e) -> p e j b", j=8, e=2)
                            for b in range(2):
                                ins = nc.vector.tensor_tensor(
                                    blk[r, 8 * b:8 * b + 8, NCMP * h:NCMP * (h + 1)], x[:, half, :, b:b + NCMP],
                                    pos[r, 8 * b:8 * b + 8].rearrange("p (j a) -> p j a", a=1).broadcast_to([64, 8, NCMP]),
                                    ALU.add)
                    ins.then_inc(built.sem, 1)
                    dve.wait_ge(made.sem, s + 1)
                    h0 = hid[:, :, :].rearrange("p m n -> p (m n)")
                    a0 = arg[:, :, :].rearrange("p m n -> p (m n)")
                    ps = self.ps[0][:, 0:2 * N]
                    b0 = 6 * s
                    nc.vector.tensor_copy(h0, ps).then_inc(step.sem, 1)
                    dve.wait_ge(step.sem, b0 + 1)
                    nc.vector.tensor_tensor(a0, h0, h0, ALU.mult).then_inc(step.sem, 1)
                    dve.wait_ge(step.sem, b0 + 2)
                    nc.vector.tensor_scalar(a0, a0, 0.044715, 1.0, ALU.mult, ALU.add).then_inc(step.sem, 1)
                    dve.wait_ge(step.sem, b0 + 3)
                    nc.vector.tensor_tensor(a0, a0, h0, ALU.mult).then_inc(step.sem, 1)
                    dve.wait_ge(step.sem, b0 + 5)
                    nc.vector.tensor_tensor(h0, a0, h0, ALU.mult).then_inc(step.sem, 1)
                    dve.wait_ge(second.sem, s + 1)
                    if s == 0:
                        nc.vector.tensor_copy(kcT[:, :, 0:NCMP], self.ps[1][:, 0:N].rearrange("p (h n) -> p h n", h=2))
                    else:
                        nc.vector.tensor_copy(vc[0:NCMP, :, :], self.ps[1][0:NCMP, 0:2 * HD].rearrange("p (h n) -> p h n", h=2))

                @block.scalar
                def _(act):
                    a0 = arg[:, :, :].rearrange("p m n -> p (m n)")
                    act.wait_ge(step.sem, 6 * s + 4)
                    nc.scalar.activation(a0, a0, ACT.Sigmoid, scale=2 * math.sqrt(2 / math.pi)).then_inc(step.sem, 1)

                @block.tensor
                def _(pe):
                    pe.wait_ge(built.sem, s + 1)
                    for m in range(2):
                        for j in range(16):
                            ins = nc.tensor.matmul(self.ps[0][:, m * N:(m + 1) * N], w1[:, j, m * P:(m + 1) * P], blk[:, j, :],
                                                   start=(j == 0), stop=(j == 15))
                    ins.then_inc(made.sem, 1)
                    pe.wait_ge(step.sem, 6 * s + 6)
                    if s == 0:
                        for m in range(2):
                            ins = nc.tensor.matmul(self.ps[1][:, 0:N], w2[:, m, :], hid[:, m, :], start=(m == 0), stop=(m == 1))
                    else:
                        for h in range(2):
                            for m in range(2):
                                ins = nc.tensor.matmul(self.ps[1][0:NCMP, HD * h:HD * (h + 1)],
                                                       hid[:, m, NCMP * h:NCMP * (h + 1)], w2[:, m, 0:HD],
                                                       start=(m == 0), stop=(m == 1))
                    ins.then_inc(second.sem, 1)

    def finish(self, out, final=True):
        nc, d = self.nc, self.d
        stored = self.sig("stored")
        with ExitStack() as c:
            y = self.sb(c, "y", [P, MT, 512])
            tok = self.sb(c, "tok", [P, QT, DM])
            g = self.sb(c, "final_gain", [P, MT])
            self.load([(g[:, :], d["final_norm_2"].rearrange("(m p) -> p m", p=P))])
            if final:
                self.norm(1, MT, lambda m: self.hT[:, m, :], lambda m: g[:, m:m + 1], lambda m: y[:, m, :])
            src = y if final else self.hT
            self.turn(MT, lambda m, t: src[:, m, t * P:(t + 1) * P], lambda m: tok[:, :, m * P:(m + 1) * P])
            with self.block() as block:
                @block.sync
                def _(sp):
                    sp.dma_start(out[0].rearrange("(t p) c -> p t c", p=P), tok[:, :, :]).then_inc(stored.sem, 16)
                    sp.wait_ge(stored.sem, 16)


def build(nc, dram, out, layers=6):
    with ExitStack() as ctx:
        k = Kernel(nc, dram, ctx)
        k.setup()
        for stage in (k.even, k.odd, k.windowed, lambda: k.feed_forward(0), k.sparse, lambda: k.feed_forward(1))[:layers]:
            stage()
        k.finish(out, layers == 6)


def _buckets(dist, max_dist):
    rel = np.maximum(dist, 0)
    f = np.maximum(rel, 1).astype(np.float32)
    large = 16 + (np.log(f / np.float32(16)) / np.float32(math.log(max_dist / 16)) * np.float32(16)).astype(np.int32)
    return np.where(rel < 16, rel, np.minimum(large, 31))


def _one_hot(max_dist, valid):
    dist = 511 - np.arange(BIAS_L)
    hot = np.zeros((33, BIAS_L), np.float32)
    ok = valid(dist)
    hot[_buckets(dist, max_dist)[ok], np.nonzero(ok)[0]] = 1.0
    hot[32, ~ok] = NEG
    return hot


def _constants():
    pos = np.arange(SEQ)
    cnt = np.stack([1.0 / np.minimum(pos + 1, w).astype(np.float32) for w in (2, 4, 8, 16)]).astype(np.float32)
    half = np.arange(P) // 64
    return {
        "c_ident": np.eye(P, dtype=np.float32),
        "c_one": np.ones((1, NH), np.float32),
        "c_halves": (half[:, None] == half[None, :]).astype(np.float32),
        "c_pool": np.broadcast_to(cnt, (P, 4, SEQ)).copy(),
        "c_flip": np.eye(P, dtype=np.float32)[::-1].copy(),
        "c_tri": np.triu(np.ones((P, P), np.float32)),
        "c_later": np.where(np.arange(P)[None, :] > np.arange(P)[:, None], BEYOND, 0).astype(np.float32),
        "c_seen": (np.arange(P) >= 31).astype(np.float32).reshape(P, 1),
        "c_hot_o": _one_hot(128, lambda x: x >= 0),
        "c_hot_w": _one_hot(1024, lambda x: (x >= 0) & (x < 128)),
        "c_hot_s": _one_hot(1024, lambda x: x >= 0),
    }


def kernel(**inputs):
    import concourse.bacc as bacc
    from concourse.bass_utils import run_bass_kernel_spmd as run

    nc = bacc.Bacc("TRN2", target_bir_lowering=False, num_devices=1)
    arrays = {n: np.ascontiguousarray(a) for n, a in inputs.items()}
    arrays.update(_constants())
    dram = {n: nc.dram_tensor(f"in_{n}", a.shape, F32, kind="ExternalInput").ap() for n, a in arrays.items()}
    dram["s_rows"] = nc.dram_tensor("s_rows", (2, 4, 512), F32, kind="Internal").ap()
    dram["s_bias"] = nc.dram_tensor("s_bias", (NH, BIAS_L), F32, kind="Internal").ap()
    out = nc.dram_tensor("out", (1, SEQ, DM), F32, kind="ExternalOutput").ap()
    build(nc, dram, out, LAYERS)
    r = run(nc, [{f"in_{n}": a for n, a in arrays.items()}], core_ids=[0])
    return r.results[0]["out"]


LAYERS = 6
```

```python
import math
from contextlib import ExitStack

import numpy as np

import concourse.bass as bass
from concourse import mybir

F32 = mybir.dt.float32
F32R = mybir.dt.float32r
ALU = mybir.AluOpType
ACT = mybir.ActivationFunctionType
AX_X = mybir.AxisListType.X

P = 128
SEQ = 512
DM = 1024
MT = DM // P
QT = SEQ // P
EPS = 1e-6
NEG = -1e30
CUT = -3e38
BEYOND = -1e38
CREDIT = 64
HD = 64
NH = 16
TOPK = 128
DFF = 2816
NCMP = 31
CREDITED = ["small_loads", "tile_turned", "tile_kept", "norm_squared", "norm_summed", "norm_var", "norm_std",
            "norm_inv", "norm_scaled", "norm_high", "norm_low", "weights_landed0", "weights_landed1",
            "weights_high", "weights_low", "tile_summed", "tile_steps",
            "gate_rows_spread", "mem_k_staged", "mem_v_staged", "mem_scores", "mem_gaps", "mem_decays", "mem_weighed",
            "mem_masked", "mem_read", "mem_tail", "att_bias", "att_staged", "att_scores", "att_logits", "att_peaks", "att_shifts", "att_probs", "att_dens",
            "att_ready", "att_turned", "att_kept", "att_mixed", "att_outs", "heads_squared", "heads_summed",
            "heads_root", "heads_spread", "heads_scaled"]
BIAS_L = 640


class Signal:

    def __init__(self, sem, base):
        self.sem = sem
        self.base = base

    def at(self, n):
        return n + self.base

    def advance(self, n):
        self.base += n


def rows(i, n=1):
    return bass.ds(i, n)


def flat(ap):
    return ap.rearrange("p a b -> p (a b)")


class Kernel:
    def __init__(self, nc, dram, ctx):
        self.nc, self.d, self.ctx = nc, dram, ctx
        self.signals = {}
        self.stage_n = 0
        self.banks = ctx.enter_context(nc.psum_tensor("banks", [P, 8, 512], F32))
        self.ps = [self.banks[:, i, :] for i in range(8)]
        self.plan = self.weight_plan()
        self.planned = 0

    def sb(self, ctx, name, shape, dt=F32):
        return ctx.enter_context(self.nc.sbuf_tensor(name, shape, dt))

    def sig(self, name):
        if name not in self.signals:
            credit = CREDIT if name in CREDITED else 0
            self.signals[name] = Signal(self.ctx.enter_context(self.nc.semaphore(name)), credit)
        return self.signals[name]

    def block(self):
        return self.nc.Block(no_gpsimd_drain=True)

    def load(self, pairs):
        nc, arrived = self.nc, self.sig("small_loads")
        with self.block() as block:
            @block.sync
            def _(sp):
                for dst, src in pairs:
                    sp.dma_start(dst, src, allow_slow_non_contiguous=True).then_inc(arrived.sem, 16)
                sp.wait_ge(arrived.sem, arrived.at(16 * len(pairs)))
        arrived.advance(16 * len(pairs))

    def turn(self, tiles, src, dst):
        nc, turned, kept = self.nc, self.sig("tile_turned"), self.sig("tile_kept")
        with self.block() as block:
            @block.tensor
            def _(pe):
                for m in range(tiles):
                    pe.wait_ge(kept.sem, kept.at(m - 1))
                    for t in range(4):
                        ins = nc.tensor.transpose(self.banks[:, m % 2, t * P:(t + 1) * P], src(m, t), self.ident[:, :])
                    ins.then_inc(turned.sem, 1)

            @block.vector
            def _(dve):
                for m in range(tiles):
                    dve.wait_ge(turned.sem, turned.at(m + 1))
                    nc.vector.tensor_copy(dst(m), self.ps[m % 2][:, :].rearrange("p (t c) -> p t c", t=4)).then_inc(kept.sem, 1)
        turned.advance(tiles)
        kept.advance(tiles)

    def norm(self, groups, per, src, gain, out, hi=None, lo=None, mat=None, width=None):
        nc = self.nc
        n = groups * per
        mat = self.ones if mat is None else mat
        width = per * P if width is None else width
        squared, summed = self.sig("norm_squared"), self.sig("norm_summed")
        var, std, inv = self.sig("norm_var"), self.sig("norm_std"), self.sig("norm_inv")
        scaled, high, low = self.sig("norm_scaled"), self.sig("norm_high"), self.sig("norm_low")
        with ExitStack() as ctx:
            sq = self.sb(ctx, f"sq{self.stage_n}", [P, 2, 512])
            rs = self.sb(ctx, f"rs{self.stage_n}", [P, 2, 3, 512])
            self.stage_n += 1
            block = ctx.enter_context(self.block())

            @block.scalar
            def _(act):
                def squares(g):
                    for t in range(per):
                        m = g * per + t
                        act.wait_ge(summed.sem, summed.at(m - 1))
                        nc.scalar.activation(sq[:, m % 2, :], src(m), ACT.Square).then_inc(squared.sem, 1)

                squares(0)
                for g in range(groups):
                    if g + 1 < groups:
                        squares(g + 1)
                    act.wait_ge(var.sem, var.at(g + 1))
                    act.wait_ge(inv.sem, inv.at(g - 1))
                    nc.scalar.activation(rs[:, g % 2, 1, :], rs[:, g % 2, 0, :], ACT.Sqrt).then_inc(std.sem, 1)
                    if hi is not None:
                        for t in range(per):
                            m = g * per + t
                            act.wait_ge(scaled.sem, scaled.at(m + 1))
                            nc.scalar.activation(hi(m), out(m), ACT.Copy).then_inc(high.sem, 1)

            @block.tensor
            def _(pe):
                for g in range(groups):
                    pe.wait_ge(var.sem, var.at(g - 1))
                    for t in range(per):
                        m = g * per + t
                        pe.wait_ge(squared.sem, squared.at(m + 1))
                        nc.tensor.matmul(self.ps[g % 2][:, :], mat[:, :], sq[:, m % 2, :], start=(t == 0),
                                         stop=(t == per - 1)).then_inc(summed.sem, 1)

            @block.vector
            def _(dve):
                for g in range(groups):
                    dve.wait_ge(summed.sem, summed.at((g + 1) * per))
                    dve.wait_ge(std.sem, std.at(g - 1))
                    nc.vector.tensor_scalar(rs[:, g % 2, 0, :], self.ps[g % 2][:, :], 1.0 / width, EPS, ALU.mult,
                                            ALU.add).then_inc(var.sem, 1)
                    dve.wait_ge(std.sem, std.at(g + 1))
                    dve.wait_ge(scaled.sem, scaled.at((g - 1) * per))
                    nc.vector.reciprocal(rs[:, g % 2, 2, :], rs[:, g % 2, 1, :]).then_inc(inv.sem, 1)
                    dve.wait_ge(inv.sem, inv.at(g + 1))
                    for t in range(per):
                        m = g * per + t
                        if hi is not None:
                            dve.wait_ge(high.sem, high.at(m - 1))
                            dve.wait_ge(low.sem, low.at(m - 1))
                        nc.vector.scalar_tensor_tensor(out(m), src(m), gain(m), rs[:, g % 2, 2, :], ALU.mult,
                                                       ALU.mult).then_inc(scaled.sem, 1)
                        if hi is not None and m >= 1:
                            dve.wait_ge(high.sem, high.at(m))
                            nc.vector.tensor_tensor(lo(m - 1), out(m - 1), hi(m - 1).bitcast(F32),
                                                    ALU.subtract).then_inc(low.sem, 1)
                    if hi is not None and g == groups - 1:
                        dve.wait_ge(high.sem, high.at(n))
                        nc.vector.tensor_tensor(lo(n - 1), out(n - 1), hi(n - 1).bitcast(F32),
                                                ALU.subtract).then_inc(low.sem, 1)
        squared.advance(n)
        summed.advance(n)
        for s in (var, std, inv):
            s.advance(groups)
        scaled.advance(n)
        if hi is not None:
            high.advance(n)
            low.advance(n)

    def norm_heads(self, x, heads, width, member, spread, gain):
        nc = self.nc
        squared, summed, root = self.sig("heads_squared"), self.sig("heads_summed"), self.sig("heads_root")
        out, scaled = self.sig("heads_spread"), self.sig("heads_scaled")
        with ExitStack() as ctx:
            sq = self.sb(ctx, f"hsq{self.stage_n}", [P, 2, 512])
            rs = self.sb(ctx, f"hrs{self.stage_n}", [heads, 3, 512])
            self.stage_n += 1
            block = ctx.enter_context(self.block())

            @block.scalar
            def _(act):
                for m in range(MT):
                    act.wait_ge(summed.sem, summed.at(m - 1))
                    nc.scalar.activation(sq[:, m % 2, :], x[:, m, :], ACT.Square).then_inc(squared.sem, 1)
                act.wait_ge(root.sem, root.at(1))
                nc.scalar.activation(rs[:, 1, :], rs[:, 0, :], ACT.Sqrt).then_inc(root.sem, 1)

            @block.tensor
            def _(pe):
                for m in range(MT):
                    pe.wait_ge(squared.sem, squared.at(m + 1))
                    nc.tensor.matmul(self.ps[0][0:heads, :], member[:, m, :], sq[:, m % 2, :], start=(m == 0),
                                     stop=(m == MT - 1)).then_inc(summed.sem, 1)
                pe.wait_ge(root.sem, root.at(3))
                for m in range(MT):
                    pe.wait_ge(scaled.sem, scaled.at(m - 1))
                    nc.tensor.matmul(self.ps[1 + m % 2][:, :], spread[:, m, :], rs[:, 2, :], start=True,
                                     stop=True).then_inc(out.sem, 1)

            @block.vector
            def _(dve):
                dve.wait_ge(summed.sem, summed.at(MT))
                nc.vector.tensor_scalar(rs[:, 0, :], self.ps[0][0:heads, :], 1.0 / width, EPS, ALU.mult,
                                        ALU.add).then_inc(root.sem, 1)
                dve.wait_ge(root.sem, root.at(2))
                nc.vector.reciprocal(rs[:, 2, :], rs[:, 1, :]).then_inc(root.sem, 1)
                for m in range(MT):
                    dve.wait_ge(out.sem, out.at(m + 1))
                    nc.vector.scalar_tensor_tensor(x[:, m, :], x[:, m, :], gain(m), self.ps[1 + m % 2][:, :], ALU.mult,
                                                   ALU.mult).then_inc(scaled.sem, 1)
        for s in (squared, summed, out, scaled):
            s.advance(MT)
        root.advance(3)

    def dense(self, name, x_hi, x_lo, steps):
        nc = self.nc
        spec = self.plan[self.planned]
        assert spec[0] == name, (spec[0], name)
        self.planned += 1
        after_this = self.plan[self.planned] if self.planned < len(self.plan) else None
        _, kc, cpt, pairs, weights, rolled = spec
        U = 2 * cpt
        L = [len(steps[0]), len(steps[1])]
        LB = L[0] + L[1]
        raw, whi, wlo = self.raw, self.whi, self.wlo
        landed = [self.sig("weights_landed0"), self.sig("weights_landed1")]
        high, low = self.sig("weights_high"), self.sig("weights_low")
        summed, evac = self.sig("tile_summed"), self.sig("tile_steps")
        pieces = len(weights(0, 0, 0))

        def done_steps(i, j, k):
            return evac.at(i * LB + (L[0] if j else 0) + k)

        def wait_chunk(i, j, half):
            return i * U + j * cpt + half

        def loop(eng, n, body):
            if rolled and n > 1:
                with eng.Fori(0, n) as i:
                    body(i)
            else:
                for i in range(n):
                    body(i)

        with self.block() as block:
            @block.sync
            def _(sp):
                def load(i, q):
                    sp.wait_ge(low.sem, low.at(i * U + (q - 1)))
                    self.load_chunk(sp, spec, landed, i, q // cpt, q % cpt)

                def body(i):
                    for q in range(2, U + 2):
                        load(i + q // U, q % U)

                if pairs > 1:
                    loop(sp, pairs - 1, body)
                for q in range(2, U):
                    load(pairs - 1, q)
                if after_this is not None:
                    sp.wait_ge(low.sem, low.at(pairs * U))
                    self.load_first(sp, after_this, landed)

            def split(eng, i, j):
                for half in range(cpt):
                    c = wait_chunk(i, j, half)
                    slot = (j * cpt + half) % 2
                    a = raw[:, slot, 0:kc, :]
                    h, lw = whi[:, slot, 0:kc, :], wlo[:, slot, 0:kc, :]
                    if eng is scalar_engine[0]:
                        nth = i * cpt + ((j * cpt + half) // 2 + 1)
                        eng.wait_ge(landed[slot].sem, landed[slot].at(nth * 16 * pieces))
                        eng.wait_ge(summed.sem, summed.at(c - 1))
                        nc.scalar.activation(h, a, ACT.Copy).then_inc(high.sem, 1)
                    else:
                        eng.wait_ge(high.sem, high.at(c + 1))
                        nc.vector.tensor_tensor(lw, a, h.bitcast(F32), ALU.subtract).then_inc(low.sem, 1)

            scalar_engine = [None]

            def after(eng, who, i, j):
                for k, (engine, step) in enumerate(steps[j]):
                    if engine != who:
                        continue
                    if k == 0:
                        eng.wait_ge(summed.sem, summed.at(i * U + (j + 1) * cpt))
                    eng.wait_ge(evac.sem, done_steps(i, j, k))
                    step(i, self.ps[j][:, :]).then_inc(evac.sem, 1)

            def splitter(eng, who):
                def body(i):
                    split(eng, i, 1)
                    after(eng, who, i, 0)
                    split(eng, i + 1, 0)
                    after(eng, who, i, 1)

                split(eng, 0, 0)
                if pairs > 1:
                    loop(eng, pairs - 1, body)
                split(eng, pairs - 1, 1)
                after(eng, who, pairs - 1, 0)
                after(eng, who, pairs - 1, 1)

            @block.scalar
            def _(act):
                scalar_engine[0] = act
                splitter(act, "act")

            @block.vector
            def _(dve):
                splitter(dve, "dve")

            @block.tensor
            def _(pe):
                def body(i):
                    for j in range(2):
                        pe.wait_ge(evac.sem, done_steps(i, j, -L[1 - j]))
                        for half in range(cpt):
                            slot = (j * cpt + half) % 2
                            pe.wait_ge(low.sem, low.at(wait_chunk(i, j, half) + 1))
                            for k in range(kc):
                                kt = half * kc + k
                                first, last = kt == 0, kt == cpt * kc - 1
                                out = self.ps[j][:, :]
                                nc.tensor.matmul(out, wlo[:, slot, k, :], x_hi(kt), start=first, stop=False)
                                nc.tensor.matmul(out, whi[:, slot, k, :], x_lo(kt), start=False, stop=False)
                                ins = nc.tensor.matmul(out, whi[:, slot, k, :], x_hi(kt), start=False, stop=last)
                            ins.then_inc(summed.sem, 1)

                loop(pe, pairs, body)
        for s in landed:
            s.advance(pairs * cpt * 16 * pieces)
        for s in (high, low, summed):
            s.advance(pairs * U)
        evac.advance(pairs * LB)

    def weight_plan(self):
        d = self.d
        ew, ow, aw, bw = d["e_w_in"][0], d["o_w_in"][0], d["a_w_qkv_2"][0], d["b_w_in_2"][0]
        plain = lambda name, w, first: (name, 8, 1, 4, self.columns(w, 8, first, P, 256), True)
        key = lambda c: [(c, 64), (c, 64)]
        plan = [
            plain("e_u", ew, 5128), plain("e_zb", ew, 6152), plain("e_v", ew, 2048),
            ("e_qk", 8, 1, 8, self.columns(ew, 8, 0, P, 256), True),
            ("e_gates", 8, 1, 1, self.columns(ew, 8, 5120, 4, 8), False),
            plain("e_o", ew, 3072), plain("e_za", ew, 4096),
            ("e_out", 8, 2, 4, self.columns(d["e_w_out"][0], 8, 0, P, 256), True),
            plain("o_q", ow, 0),
            ("o_ckv_qi", 8, 1, 2, self.columns(ow, 8, 1024, P, 256), False),
            ("o_ki_wi", 8, 1, 1, self.listed(ow, 8, [key(1536), [(1600, 64), (1664, 64)]]), False),
            ("o_uk", 2, 1, 4, self.columns(d["o_w_uk"][0], 2, 0, P, 256), True),
            ("o_uv", 2, 1, 4, self.columns(d["o_w_uv"][0], 2, 0, P, 256), True),
            plain("o_z", ow, 1604), plain("o_out", d["o_w_out"][0], 0),
            plain("a_q", aw, 0),
            ("a_kv", 8, 1, 2, self.listed(aw, 8, [key(1024), key(1088), [(1152, 64), (1216, 64)],
                                                  [(1152, 64), (1216, 64)]]), False),
            plain("a_out", d["a_w_o_2"][0], 0)]
        ffn = lambda n: [
            (f"ff_gu{n}", 8, 1, DFF // P, self.columns(d["ffn_w_gu_2"][n], 8, 0, DFF, P), True),
            (f"ff_down{n}", 11, 2, 4, self.columns(d["ffn_w_down_2"][n], 11, 0, P, 256), True)]
        kv = lambda n: 1024 + P * n
        tiles = [key(kv(n) + 64 * h) for n in (0, 1, 2, 4) for h in range(2)]
        tiles += [[(kv(n), 64), (kv(n) + 64, 64)] for n in (3, 5)] + [[(1712, 64), (1776, 64)]] * 2
        return (plan + ffn(0) + [plain("b_q", bw, 0), ("b_rest", 8, 1, 6, self.listed(bw, 8, tiles), False),
                                 plain("b_out", d["b_w_o_2"][0], 0)] + ffn(1))

    def load_chunk(self, sp, spec, landed, i, j, half):
        _, kc, cpt, _, weights, _ = spec
        slot = (j * cpt + half) % 2
        for c0, n, ap in weights(i, j, half):
            sp.dma_start(self.raw[:, slot, 0:kc, c0:c0 + n], ap).then_inc(landed[slot].sem, 16)

    def load_first(self, sp, spec, landed):
        for q in range(2):
            self.load_chunk(sp, spec, landed, 0, q // spec[2], q % spec[2])

    def columns(self, w, kc, first, stride, pair_stride):
        def of(i, j, half):
            src = w[half * kc * P:(half + 1) * kc * P, :]
            return [(0, P, src[:, rows(i * pair_stride + (first + j * stride), P)].rearrange("(k p) c -> p k c", p=P))]
        return of

    def listed(self, w, kc, tiles):
        def of(i, j, half):
            out, at = [], 0
            for c, n in tiles[2 * i + j]:
                out.append((at, n, w[half * kc * P:(half + 1) * kc * P, c:c + n].rearrange("(k p) c -> p k c", p=P)))
                at += n
            return out
        return of

    def keep(self, dst, engine="act"):
        nc = self.nc

        def step(j):
            if engine == "act":
                return [("act", lambda i, ps: nc.scalar.activation(dst(i, j), ps, ACT.Copy))]
            return [("dve", lambda i, ps: nc.vector.tensor_copy(dst(i, j), ps))]
        return [step(0), step(1)]

    def add_residual(self, bias=None):
        nc, hT = self.nc, self.hT

        def step(j):
            if bias is None:
                return [("dve", lambda i, ps: nc.vector.tensor_tensor(
                    flat(hT[:, rows(i * 2 + j), :]), ps, flat(hT[:, rows(i * 2 + j), :]), ALU.add))]
            return [("dve", lambda i, ps: nc.vector.scalar_tensor_tensor(
                flat(hT[:, rows(i * 2 + j), :]), ps, bias[:, rows(i * 2 + j)], flat(hT[:, rows(i * 2 + j), :]),
                ALU.add, ALU.add))]
        return [step(0), step(1)]

    def norm_stream(self, gain, x_hi, x_lo, tmp):
        self.norm(1, MT, lambda m: self.hT[:, m, :], lambda m: gain[:, m:m + 1], lambda m: tmp[:, m % 2, :],
                  lambda m: x_hi[:, m, :], lambda m: x_lo[:, m, :])

    def setup(self):
        nc, d, ctx = self.nc, self.d, self.ctx
        self.hT = self.sb(ctx, "hT", [P, MT, 512])
        self.ident = self.sb(ctx, "ident", [P, P])
        self.ones = self.sb(ctx, "ones", [P, P])
        self.raw = self.sb(ctx, "raw", [P, 2, 11, P])
        self.whi = self.sb(ctx, "whi", [P, 2, 11, P], F32R)
        self.wlo = self.sb(ctx, "wlo", [P, 2, 11, P], F32R)
        self.gains = self.sb(ctx, "gains", [P, 6, MT])
        self.xs = self.sb(ctx, "xs", [P, 2, MT, 512], F32R)
        self.xs_hi, self.xs_lo = self.xs[:, 0], self.xs[:, 1]
        self.xtmp = self.sb(ctx, "x_tmp", [P, 2, 512])

        for n in CREDITED:
            self.sig(n)
        started = self.ctx.enter_context(nc.semaphore("started"))
        with self.block() as block:
            @block.sync
            def _(sp):
                self.load_first(sp, self.plan[0], [self.sig("weights_landed0"), self.sig("weights_landed1")])

            @block.gpsimd
            def _(pool):
                for n in CREDITED:
                    pool.sem_inc(self.signals[n].sem, CREDIT)
                nc.gpsimd.memset(self.ones[:, :], 1.0).then_inc(started, 1)
                pool.wait_ge(started, 1)

        gain = lambda ap: ap.rearrange("(m p) -> p m", p=P)
        with ExitStack() as c:
            xin = self.sb(c, "xin", [P, QT, DM])
            self.load([(self.ident[:, :], d["c_ident"]), (xin[:, :, :], d["x"][0].rearrange("(t p) c -> p t c", p=P)),
                       (self.gains[:, 0, :], gain(d["e_norm"][0])), (self.gains[:, 1, :], gain(d["o_norm"][0])),
                       (self.gains[:, 2, :], gain(d["attn_norm_2"][0])), (self.gains[:, 3, :], gain(d["attn_norm_2"][1])),
                       (self.gains[:, 4, :], gain(d["ffn_norm_2"][0])), (self.gains[:, 5, :], gain(d["ffn_norm_2"][1]))])
            self.turn(MT, lambda m, t: xin[:, t, m * P:(m + 1) * P],
                      lambda m: self.hT[:, m, :].rearrange("p (t c) -> p t c", t=4))

        self.bias_tables()

    def even(self):
        nc, d = self.nc, self.d
        w = d["e_w_in"][0]
        hi, lo = self.xs_hi, self.xs_lo
        xh, xl = (lambda k: hi[:, k, :]), (lambda k: lo[:, k, :])
        self.norm_stream(self.gains[:, 0, :], hi, lo, self.xtmp)
        with ExitStack() as c:
            yb = self.sb(c, "yb", [P, MT, 512])
            ha = self.sb(c, "ha", [P, MT, 512])
            tmp = self.sb(c, "even_tmp", [P, 3, 512])
            small = self.sb(c, "even_small", [P, 96])
            conv, ghead, spool = small[:, 0:64], small[:, 64:72], small[:, 72:80]
            bif = small[0:4, 80:82]
            gain = lambda ap: ap.rearrange("(m p) -> p m", p=P)
            self.load([(conv.rearrange("p (m j) -> p m j", j=4)[:, :, j], gain(d["e_conv"][0, j])) for j in range(4)]
                      + [(ghead, gain(d["e_g_head"][0].rearrange("a b -> (a b)"))), (spool, gain(d["e_s_pool"][0])),
                         (bif, d["e_b_if"][0].rearrange("(k h) -> h k", h=4))])

            with ExitStack() as c2:
                u = self.sb(c2, "u", [P, MT, 512])
                self.dense("e_u", xh, xl,
                           self.keep(lambda i, j: flat(u[:, rows(i * 2 + j), :])))
                self.pool(u, yb)
            gate = lambda j: [
                ("act", lambda i, ps: nc.scalar.activation(tmp[:, j, :], ps, ACT.Silu)),
                ("dve", lambda i, ps: nc.vector.scalar_tensor_tensor(
                    flat(yb[:, rows(i * 2 + j), :]), flat(yb[:, rows(i * 2 + j), :]), spool[:, rows(i * 2 + j)],
                    tmp[:, j, :], ALU.mult, ALU.mult))]
            self.dense("e_zb", xh, xl, [gate(0), gate(1)])

            with ExitStack() as c2:
                vt = self.sb(c2, "vt", [P, QT, DM])
                self.dense("e_v", xh, xl,
                           self.keep(lambda i, j: flat(ha[:, rows(i * 2 + j), :])))
                self.turn(MT, lambda m, t: ha[:, m, t * P:(t + 1) * P], lambda m: vt[:, :, m * P:(m + 1) * P])

                qk = self.sb(c2, "qk", [P, 16, 512])
                acol = self.sb(c2, "acol", [P, QT, 4])
                with ExitStack() as c3:
                    pad = self.sb(c3, "pad", [P, 2, 516])
                    self.clear(pad[:, :, 0:4])

                    def conv_steps(j):
                        def tap(t):
                            def f(i, ps):
                                wt = conv[:, rows(i * 8 + (4 * j + t))]
                                if t == 0:
                                    return nc.vector.tensor_scalar(tmp[:, j, :], pad[:, j, 1:513], wt, None, ALU.mult)
                                return nc.vector.scalar_tensor_tensor(tmp[:, j, :], pad[:, j, 1 + t:513 + t], wt,
                                                                      tmp[:, j, :], ALU.mult, ALU.add)
                            return ("dve", f)
                        return ([("act", lambda i, ps: nc.scalar.activation(pad[:, j, 4:516], ps, ACT.Copy))]
                                + [tap(t) for t in range(4)]
                                + [("act", lambda i, ps: nc.scalar.activation(flat(qk[:, rows(i * 2 + j), :]),
                                                                              tmp[:, j, :], ACT.Silu))])
                    self.dense("e_qk", xh, xl, [conv_steps(0), conv_steps(1)])

                with ExitStack() as c3:
                    gi = self.sb(c3, "gates", [4, 2, 512])
                    gk = [[("act", lambda i, ps, j=j: nc.scalar.activation(gi[:, j, :], ps[0:4, :], ACT.Identity,
                                                                           bias=bif[:, j:j + 1]))] for j in range(2)]
                    self.dense("e_gates", xh, xl, gk)
                    self.stabilize(c3, gi, acol)
                self.recall(c2, qk, vt, acol, ha)

            gate_o = lambda j: [
                ("act", lambda i, ps: nc.scalar.activation(tmp[:, j, :], ps, ACT.Sigmoid)),
                ("dve", lambda i, ps: nc.vector.tensor_tensor(flat(ha[:, rows(i * 2 + j), :]), tmp[:, j, :],
                                                              flat(ha[:, rows(i * 2 + j), :]), ALU.mult))]
            self.dense("e_o", xh, xl, [gate_o(0), gate_o(1)])
            with ExitStack() as c2:
                member, spread = self.sb(c2, "member4", [P, MT, 4]), self.sb(c2, "spread4", [4, MT, P])
                self.load([(member[:, :, :], d["c_member4"]), (spread[:, :, :], d["c_spread4"])])
                self.norm_heads(ha, 4, 256, member, spread, lambda m: ghead[:, m:m + 1])
            gate_z = lambda j: [
                ("act", lambda i, ps: nc.scalar.activation(tmp[:, j, :], ps, ACT.Silu)),
                ("dve", lambda i, ps: nc.vector.tensor_tensor(flat(ha[:, rows(i * 2 + j), :]), tmp[:, j, :],
                                                              flat(ha[:, rows(i * 2 + j), :]), ALU.mult))]
            self.dense("e_za", xh, xl, [gate_z(0), gate_z(1)])

            y_hi, y_lo = self.sb(c, "y_hi", [P, 16, 512], F32R), self.sb(c, "y_lo", [P, 16, 512], F32R)
            self.split_tiles(16, lambda m: (ha if m < 8 else yb)[:, m % 8, :], lambda m: y_hi[:, m, :],
                             lambda m: y_lo[:, m, :])
            self.dense("e_out", lambda k: y_hi[:, k, :],
                       lambda k: y_lo[:, k, :], self.add_residual())

    def clear(self, ap):
        nc, cleared = self.nc, self.sig("cleared")
        with self.block() as block:
            @block.vector
            def _(dve):
                nc.vector.memset(ap, 0.0).then_inc(cleared.sem, 1)

    def split_tiles(self, n, src, hi, lo):
        nc, high = self.nc, self.sig("norm_high")
        with self.block() as block:
            @block.scalar
            def _(act):
                for m in range(n):
                    nc.scalar.activation(hi(m), src(m), ACT.Copy).then_inc(high.sem, 1)

            @block.vector
            def _(dve):
                for m in range(n):
                    dve.wait_ge(high.sem, high.at(m + 1))
                    nc.vector.tensor_tensor(lo(m), src(m), hi(m).bitcast(F32), ALU.subtract)
        high.advance(n)

    def pool(self, u, yb):
        nc, d = self.nc, self.d
        step, mixed, kept = self.sig("pool_step"), self.sig("pool_mixed"), self.sig("pool_kept")
        with ExitStack() as c:
            win = self.sb(c, "win", [P, 2, 2, 512])
            pooled = self.sb(c, "pooled", [P, MT, 512])
            wp = self.sb(c, "wp", [P, 4, 2, 256])
            cnt = self.sb(c, "cnt", [P, 4, 512])
            self.load([(wp[:, g], d["e_w_pool"][0, g].rearrange("(k p) c -> p k c", p=P)) for g in range(4)]
                      + [(cnt[:, :, :], d["c_pool"])])
            with self.block() as block:
                @block.vector
                def _(dve):
                    n = 0

                    def link(ins):
                        nonlocal n
                        n += 1
                        ins.then_inc(step.sem, 1)
                        dve.wait_ge(step.sem, n)

                    for g in range(4):
                        src = u[:, 2 * g:2 * g + 2, :]
                        cur = src
                        for b in range(g + 1):
                            w = 1 << b
                            nxt = win[:, b % 2]
                            link(nc.vector.tensor_copy(nxt[:, :, 0:w], cur[:, :, 0:w]))
                            link(nc.vector.tensor_tensor(nxt[:, :, w:512], cur[:, :, w:512], cur[:, :, 0:512 - w], ALU.add))
                            cur = nxt
                        for t in range(2):
                            link(nc.vector.tensor_tensor(pooled[:, 2 * g + t, :], cur[:, t, :], cnt[:, g, :], ALU.mult))
                        link(nc.vector.tensor_tensor(pooled[:, 2 * g:2 * g + 2, :], pooled[:, 2 * g:2 * g + 2, :], src,
                                                     ALU.subtract))
                    step.base = n
            with self.block() as block:
                @block.tensor
                def _(pe):
                    for m in range(MT):
                        g, t = m // 2, m % 2
                        if m >= 2:
                            pe.wait_ge(kept.sem, m - 1)
                        for k in range(2):
                            ins = nc.tensor.matmul(self.ps[m % 2][:, :], wp[:, g, k, t * P:(t + 1) * P],
                                                   pooled[:, 2 * g + k, :], start=(k == 0), stop=(k == 1))
                        ins.then_inc(mixed.sem, 1)

                @block.scalar
                def _(act):
                    for m in range(MT):
                        act.wait_ge(mixed.sem, m + 1)
                        nc.scalar.activation(yb[:, m, :], self.ps[m % 2][:, :], ACT.Copy).then_inc(kept.sem, 1)

    def stabilize(self, c, gi, acol):
        nc, d = self.nc, self.d
        row, colsum = self.sig("gate_step"), self.sig("gate_turned")
        stored = self.sig("gate_rows_stored")
        rowsT = self.sb(c, "gate_rows", [4, 8, 512])
        scratch = d["s_rows"]
        i_pre, f_pre = gi[:, 0, :], gi[:, 1, :]
        t0, t1, F, a, M, m, one, em = [rowsT[:, k, :] for k in range(8)]
        with self.block() as block:
            @block.scalar
            def _(act):
                nc.scalar.activation(t0, f_pre, ACT.Abs).then_inc(row.sem, 1)
                act.wait_ge(row.sem, 1)
                nc.scalar.activation(t0, t0, ACT.Exp, scale=-1.0).then_inc(row.sem, 1)
                act.wait_ge(row.sem, 2)
                nc.scalar.activation(t0, t0, ACT.Ln, bias=1.0).then_inc(row.sem, 1)
                act.wait_ge(row.sem, 11)
                nc.scalar.activation(em, m, ACT.Exp, scale=-1.0).then_inc(row.sem, 1)

            @block.vector
            def _(dve):
                dve.wait_ge(row.sem, 3)
                nc.vector.memset(one, 1.0).then_inc(row.sem, 1)
                dve.wait_ge(row.sem, 4)
                nc.vector.tensor_scalar(t1, f_pre, 0.0, None, ALU.min).then_inc(row.sem, 1)
                dve.wait_ge(row.sem, 5)
                nc.vector.tensor_tensor(t1, t1, t0, ALU.subtract).then_inc(row.sem, 1)
                dve.wait_ge(row.sem, 6)
                nc.vector.tensor_tensor_scan(F, one, t1, 0.0, ALU.mult, ALU.add).then_inc(row.sem, 1)
                dve.wait_ge(row.sem, 7)
                nc.vector.tensor_tensor(a, i_pre, F, ALU.subtract).then_inc(row.sem, 1)
                dve.wait_ge(row.sem, 8)
                nc.vector.memset(t0, 0.0).then_inc(row.sem, 1)
                dve.wait_ge(row.sem, 9)
                nc.vector.tensor_tensor_scan(M, a, t0, 0.0, ALU.max, ALU.add).then_inc(row.sem, 1)
                dve.wait_ge(row.sem, 10)
                nc.vector.tensor_tensor(m, F, M, ALU.add).then_inc(row.sem, 1)
                dve.wait_ge(colsum.sem, 1)
                nc.vector.tensor_copy(acol[:, :, :], self.ps[0][:, 0:16].rearrange("p (t h) -> p t h", t=4))

            @block.tensor
            def _(pe):
                pe.wait_ge(row.sem, 8)
                for t in range(4):
                    ins = nc.tensor.transpose(self.ps[0][:, 4 * t:4 * t + 4], a[:, t * P:(t + 1) * P], self.ident[0:4, 0:4])
                ins.then_inc(colsum.sem, 1)

            @block.sync
            def _(sp):
                sp.wait_ge(row.sem, 12)
                sp.dma_start(scratch[0], M).then_inc(stored.sem, 16)
                sp.dma_start(scratch[1], em).then_inc(stored.sem, 16)
                sp.wait_ge(stored.sem, 32)

    def recall(self, c, qk, vt, acol, ha):
        nc, scratch = self.nc, self.d["s_rows"]
        spread = self.sig("gate_rows_spread")
        kh = self.sb(c, "kh", [P, 2, 512])
        vh = self.sb(c, "vh", [P, QT, 256])
        W = self.sb(c, "Wst", [P, QT, 512])
        Mb = self.sb(c, "Mb", [P, 2, 512])
        D = self.sb(c, "Dst", [P, 2, 512])
        den = self.sb(c, "den", [P, 2, 512])
        tri = self.sb(c, "tri", [P, P])
        self.load([(tri[:, :], self.d["c_tri"])])
        k_staged, v_staged = self.sig("mem_k_staged"), self.sig("mem_v_staged")
        scores, gaps, decays = self.sig("mem_scores"), self.sig("mem_gaps"), self.sig("mem_decays")
        weighed, masked = self.sig("mem_weighed"), self.sig("mem_masked")
        read, tail = self.sig("mem_read"), self.sig("mem_tail")
        with self.block() as block:
            @block.sync
            def _(sp):
                with sp.Fori(0, 4) as h:
                    sp.wait_ge(tail.sem, h * 5 + CREDIT)
                    sp.dma_start(Mb[:, 0, :], scratch[0, rows(h), :].broadcast_to([P, 512])).then_inc(spread.sem, 16)
                    sp.dma_start(Mb[:, 1, :], scratch[1, rows(h), :].broadcast_to([P, 512])).then_inc(spread.sem, 16)

            @block.scalar
            def _(act):
                with act.Fori(0, 4) as h:
                    act.wait_ge(tail.sem, h * 5 + CREDIT)
                    nc.scalar.activation(kh[:, :, :], qk[:, rows(h * 2 + 8, 2), :], ACT.Copy,
                                         scale=256 ** -0.5).then_inc(k_staged.sem, 1)
                    for s in range(QT):
                        n = 512 - s * P
                        act.wait_ge(gaps.sem, h * 4 + (s + 1 + CREDIT))
                        nc.scalar.activation(D[:, s % 2, 0:n], D[:, s % 2, 0:n], ACT.Exp, scale=-1.0).then_inc(decays.sem, 1)

            @block.vector
            def _(dve):
                with dve.Fori(0, 4) as h:
                    dve.wait_ge(tail.sem, h * 5 + CREDIT)
                    nc.vector.tensor_copy(vh[:, :, :], vt[:, :, rows(h * 256, 256)]).then_inc(v_staged.sem, 1)
                    dve.wait_ge(spread.sem, h * 32 + (32 + CREDIT))
                    for s in range(QT):
                        n, t = 512 - s * P, s * P
                        dve.wait_ge(weighed.sem, h * 4 + (s - 1 + CREDIT))
                        nc.vector.tensor_scalar(D[:, s % 2, 0:n], Mb[:, 0, t:512], acol[:, s, rows(h)], 0.0, ALU.subtract,
                                                ALU.max).then_inc(gaps.sem, 1)
                        dve.wait_ge(decays.sem, h * 4 + (s + 1 + CREDIT))
                        dve.wait_ge(scores.sem, h * 4 + (s + 1 + CREDIT))
                        nc.vector.tensor_tensor(W[:, s, 0:n], D[:, s % 2, 0:n], self.ps[s % 2][:, 0:n],
                                                ALU.mult).then_inc(weighed.sem, 1)
                    dve.wait_ge(read.sem, h * 3 + (1 + CREDIT))
                    nc.vector.scalar_tensor_tensor(den[:, 0, :], self.ps[4][:, :], -1.0, Mb[:, 1, :], ALU.mult,
                                                   ALU.max).then_inc(tail.sem, 1)
                    dve.wait_ge(tail.sem, h * 5 + (1 + CREDIT))
                    nc.vector.tensor_tensor(den[:, 0, :], self.ps[4][:, :], den[:, 0, :], ALU.max).then_inc(tail.sem, 1)
                    dve.wait_ge(tail.sem, h * 5 + (2 + CREDIT))
                    nc.vector.reciprocal(den[:, 1, :], den[:, 0, :]).then_inc(tail.sem, 1)
                    dve.wait_ge(tail.sem, h * 5 + (3 + CREDIT))
                    for v in range(2):
                        dve.wait_ge(read.sem, h * 3 + (2 + v + CREDIT))
                        nc.vector.tensor_tensor(flat(ha[:, rows(h * 2 + v), :]), self.ps[2 + v][:, :], den[:, 1, :],
                                                ALU.mult).then_inc(tail.sem, 1)

            @block.gpsimd
            def _(pool):
                with pool.Fori(0, 4) as h:
                    for s in range(QT):
                        pool.wait_ge(weighed.sem, h * 4 + (s + 1 + CREDIT))
                        nc.gpsimd.tensor_tensor(W[:, s, 0:P], W[:, s, 0:P], tri[:, :], ALU.mult).then_inc(masked.sem, 1)

            @block.tensor
            def _(pe):
                with pe.Fori(0, 4) as h:
                    pe.wait_ge(k_staged.sem, h + (1 + CREDIT))
                    for s in range(QT):
                        n, t = 512 - s * P, s * P
                        pe.wait_ge(weighed.sem, h * 4 + (s - 1 + CREDIT))
                        for k in range(2):
                            ins = nc.tensor.matmul(self.ps[s % 2][:, 0:n], kh[:, k, s * P:(s + 1) * P],
                                                   flat(qk[:, rows(h * 2 + k), t:512]), start=(k == 0), stop=(k == 1))
                        ins.then_inc(scores.sem, 1)
                    pe.wait_ge(masked.sem, h * 4 + (4 + CREDIT))
                    pe.wait_ge(v_staged.sem, h + (1 + CREDIT))
                    pe.wait_ge(tail.sem, h * 5 + CREDIT)
                    for o, lhs in ((4, None), (2, 0), (3, 1)):
                        for s in range(QT):
                            n, t = 512 - s * P, s * P
                            st = self.ones[:, :] if lhs is None else vh[:, s, lhs * P:(lhs + 1) * P]
                            ins = nc.tensor.matmul(self.ps[o][:, t:512], st, W[:, s, 0:n], start=(s == 0),
                                                   stop=(s == QT - 1))
                        ins.then_inc(read.sem, 1)

    def bias_tables(self):
        nc, d = self.nc, self.d
        made, kept, stored = self.sig("bias_made"), self.sig("bias_kept"), self.sig("bias_spread")
        with ExitStack() as c:
            tab = self.sb(c, "tab", [33, 2, NH])
            hot = self.sb(c, "hot", [33, 3, BIAS_L])
            vec = self.sb(c, "vec", [NH, 3, BIAS_L])
            tables = [d["rel_bias"], d["rel_table_2"]]
            self.load([(tab[0:32, i, :], tables[i]) for i in range(2)] + [(tab[32:33, i, :], d["c_one"]) for i in range(2)]
                      + [(hot[:, :, :], d["c_hot"].rearrange("a b e -> b a e"))])
            with self.block() as block:
                @block.tensor
                def _(pe):
                    for a in range(3):
                        w = tab[:, min(a, 1), :]
                        nc.tensor.matmul(self.banks[0:NH, 2 * a, :], w, hot[:, a, 0:512], start=True, stop=True)
                        ins = nc.tensor.matmul(self.banks[0:NH, 2 * a + 1, 0:P], w, hot[:, a, 512:BIAS_L], start=True, stop=True)
                    ins.then_inc(made.sem, 1)

                @block.scalar
                def _(act):
                    act.wait_ge(made.sem, 1)
                    for a in range(3):
                        nc.scalar.activation(vec[:, a, 0:512], self.banks[0:NH, 2 * a, :], ACT.Copy).then_inc(kept.sem, 1)
                        nc.scalar.activation(vec[:, a, 512:BIAS_L], self.banks[0:NH, 2 * a + 1, 0:P], ACT.Copy).then_inc(kept.sem, 1)
                    act.wait_ge(kept.sem, 6)
                    act.dma_start(d["s_bias"].rearrange("a h e -> h a e"), vec[:, :, :]).then_inc(stored.sem, 16)
                    act.wait_ge(stored.sem, 16)
                    for a in range(3):
                        src = bass.AP(tensor=d["s_bias"].tensor, offset=a * NH * BIAS_L, ap=[[BIAS_L, NH], [0, P], [1, BIAS_L]])
                        act.dma_start(d["s_skew"][a], src).then_inc(stored.sem, 16)

    def attention(self, q, k, k_shape, v, v_shape, per_loop, keys, n_bias, table, out, add=False, mask=None, sink=None,
                  gate=None, bias_at=None):
        nc = self.nc
        loops = NH // per_loop
        pairs = per_loop // 2
        shared = k_shape[0] == 1
        steps = [(2 * g, half, t) for g in range(pairs // 2) for half in range(2) for t in range(QT)]
        NS = len(steps)
        sg = self.sig
        landed, staged, scores, logits = sg("att_bias"), sg("att_staged"), sg("att_scores"), sg("att_logits")
        peaks, shifts, probs, dens = sg("att_peaks"), sg("att_shifts"), sg("att_probs"), sg("att_dens")
        ready, turned, kept, mixed = sg("att_ready"), sg("att_turned"), sg("att_kept"), sg("att_mixed")
        outs = sg("att_outs")
        n_logits = 2 if mask is not None else 1
        n_peaks = 2 if sink is not None else 1
        n_shifts = 2 if sink is not None else 1
        n_probs = 3 if sink is not None else 2
        n_dens = 1 + (sink is not None) + (gate is not None)
        bias = self.xs[:, :, :, :].bitcast(F32).rearrange("p a b c -> p (a b c)")[:, 0:NH * n_bias]
        bias_heads = bias.rearrange("p (h x) -> p h x", h=NH)
        bias_pairs = bias.rearrange("p (a e x) -> p a e x", e=2, x=n_bias)
        with ExitStack() as c:
            n = self.stage_n
            self.stage_n += 1
            qs = self.sb(c, f"qs{n}", [P, pairs, 512])
            ks = self.sb(c, f"ks{n}", [P, *k_shape])
            vs = self.sb(c, f"vs{n}", v_shape)
            prob = self.sb(c, f"prob{n}", [P, 3, 2, 512])
            pT = self.sb(c, f"pT{n}", [P, 2, QT * 2 * P])
            st = self.sb(c, f"stat{n}", [P, 4, 6, 2])
            S = [self.banks[:, 2 * b:2 * b + 2, :] for b in range(2)]
            T = self.banks[:, 4:6, :].rearrange("p a b -> p (a b)")
            O = [self.banks[:, 6 + b, 0:2 * P] for b in range(2)]
            block = c.enter_context(self.block())

            def stat(s, k):
                return st[:, s % 4, k, :]

            def pair0(i, s):
                return i * pairs + steps[s][0]

            if table is not None:
                @block.sync
                def _(sp):
                    sp.wait_ge(self.sig("bias_spread").sem, 16 * (1 + 3))
                    for i in range(loops):
                        h = i * per_loop
                        src = bass.AP(tensor=self.d["s_skew"].tensor,
                                      offset=(table * NH + h) * P * BIAS_L + 127 + 512 - n_bias,
                                      ap=[[BIAS_L - 1, P], [P * BIAS_L, per_loop], [1, n_bias]])
                        sp.dma_start(bias_heads[:, h:h + per_loop, :], src).then_inc(landed.sem, 16)
                        sp.wait_ge(landed.sem, landed.at(16 * i + 16))

            @block.tensor
            def _(pe):
                def score(i, s):
                    p, half, t = steps[s]
                    k0, nk, _ = keys(t)
                    if s == 0:
                        pe.wait_ge(staged.sem, staged.at(i * 3 + 3))
                    pe.wait_ge(logits.sem, logits.at((i * NS + (s - 1)) * n_logits))
                    r = slice(64 * half, 64 * half + 64)
                    for x in range(2):
                        ins = nc.tensor.matmul(S[s % 2][:, x, 0:nk], qs[r, p + x, t * P:(t + 1) * P],
                                               ks[r, (p + x) % k_shape[0], k0:k0 + nk], start=True, stop=True)
                    ins.then_inc(scores.sem, 1)

                def turn(i, s):
                    _, _, blocks = keys(steps[s][2])
                    pe.wait_ge(kept.sem, kept.at(i * NS + s))
                    pe.wait_ge(ready.sem, ready.at((i * NS + (s + 1)) * 2))
                    for b, (_, r) in enumerate(blocks):
                        for x in range(2):
                            ins = nc.tensor.transpose(T[0:r, (2 * b + x) * P:(2 * b + x + 1) * P],
                                                      prob[:, s % 3, x, b * P:b * P + r], self.ident[:, :])
                    ins.then_inc(turned.sem, 1)

                def mix(i, s):
                    p, half, t = steps[s]
                    _, _, blocks = keys(t)
                    o = O[s % 2][64 * half:64 * half + 64, :]
                    pe.wait_ge(outs.sem, outs.at(i * NS + (s - 1)))
                    pe.wait_ge(kept.sem, kept.at(i * NS + (s + 1)))
                    last = len(blocks) - 1
                    if shared:
                        for b, (kb, r) in enumerate(blocks):
                            ins = nc.tensor.matmul(o, vs[0:r, kb, :], pT[0:r, s % 2, 2 * b * P:2 * (b + 1) * P],
                                                   start=(b == 0), stop=(b == last))
                    else:
                        for x in range(2):
                            lane = (2 * (p + x) + half) * HD
                            for b, (kb, r) in enumerate(blocks):
                                ins = nc.tensor.matmul(o[:, x * P:(x + 1) * P], vs[0:r, kb, lane:lane + HD],
                                                       pT[0:r, s % 2, (2 * b + x) * P:(2 * b + x + 1) * P],
                                                       start=(b == 0), stop=(b == last))
                    ins.then_inc(mixed.sem, 1)

                with pe.Fori(0, loops) as i:
                    for j in range(NS + 3):
                        if j < NS:
                            score(i, j)
                        if j >= 3:
                            mix(i, j - 3)
                        if 2 <= j < NS + 2:
                            turn(i, j - 2)

            @block.vector
            def _(dve):
                def logit(i, s):
                    _, half, t = steps[s]
                    _, nk, _ = keys(t)
                    at = i * NS + s
                    pr = prob[:, s % 3, :, 0:nk]
                    if table is not None and s == 0:
                        dve.wait_ge(landed.sem, landed.at(i * 16 + 16))
                    dve.wait_ge(turned.sem, turned.at(at - 2))
                    dve.wait_ge(scores.sem, scores.at(at + 1))
                    b = bias_pairs[:, rows(pair0(i, s), 2), half]
                    b = b[:, :, n_bias - nk:n_bias] if bias_at is None else b[:, :, bias_at(t, nk)]
                    nc.vector.scalar_tensor_tensor(pr, S[s % 2][:, :, 0:nk], HD ** -0.5, b, ALU.mult,
                                                   ALU.add).then_inc(logits.sem, 1)
                    if mask is not None:
                        dve.wait_ge(logits.sem, logits.at(at * 2 + 1))
                        nc.vector.tensor_tensor(pr, pr, mask(t, nk), ALU.add).then_inc(logits.sem, 1)
                    dve.wait_ge(logits.sem, logits.at((at + 1) * n_logits))
                    nc.vector.tensor_reduce(stat(s, 0), pr, AX_X, ALU.max).then_inc(peaks.sem, 1)
                    if sink is not None:
                        sk = sink[:, rows(pair0(i, s), 2), half]
                        dve.wait_ge(peaks.sem, peaks.at(at * 2 + 1))
                        nc.vector.tensor_tensor(stat(s, 0), stat(s, 0), sk, ALU.max).then_inc(peaks.sem, 1)
                    dve.wait_ge(peaks.sem, peaks.at((at + 1) * n_peaks))
                    nc.vector.tensor_scalar(stat(s, 1), stat(s, 0), -1.0, None, ALU.mult).then_inc(shifts.sem, 1)
                    if sink is not None:
                        dve.wait_ge(shifts.sem, shifts.at(at * 2 + 1))
                        nc.vector.tensor_tensor(stat(s, 3), sk, stat(s, 1), ALU.add).then_inc(shifts.sem, 1)

                def divide(i, s):
                    _, half, t = steps[s]
                    _, nk, _ = keys(t)
                    at = i * NS + s
                    dve.wait_ge(probs.sem, probs.at((at + 1) * n_probs))
                    done = 0
                    if sink is not None:
                        nc.vector.tensor_tensor(stat(s, 2), stat(s, 2), stat(s, 4), ALU.add).then_inc(dens.sem, 1)
                        done += 1
                        dve.wait_ge(dens.sem, dens.at(at * n_dens + done))
                    nc.vector.reciprocal(stat(s, 5), stat(s, 2)).then_inc(dens.sem, 1)
                    done += 1
                    dve.wait_ge(dens.sem, dens.at(at * n_dens + done))
                    if gate is not None:
                        nc.vector.tensor_tensor(stat(s, 5), stat(s, 5), gate(pair0(i, s), half, t),
                                                ALU.mult).then_inc(dens.sem, 1)
                        done += 1
                        dve.wait_ge(dens.sem, dens.at(at * n_dens + done))
                    for x in range(2):
                        pr = prob[:, s % 3, x, 0:nk]
                        nc.vector.tensor_scalar(pr, pr, st[:, s % 4, 5, x:x + 1], None, ALU.mult).then_inc(ready.sem, 1)

                def finish(i, s):
                    _, half, t = steps[s]
                    r = slice(64 * half, 64 * half + 64)
                    o = out[r, rows(pair0(i, s), 2), t * P:(t + 1) * P]
                    got = O[s % 2][r, :].rearrange("p (x q) -> p x q", x=2)
                    dve.wait_ge(mixed.sem, mixed.at(i * NS + (s + 1)))
                    if add:
                        nc.vector.tensor_tensor(o, got, o, ALU.add).then_inc(outs.sem, 1)
                    else:
                        nc.vector.tensor_copy(o, got).then_inc(outs.sem, 1)

                with dve.Fori(0, loops) as i:
                    for j in range(NS + 4):
                        if j < NS:
                            logit(i, j)
                        if 1 <= j <= NS:
                            divide(i, j - 1)
                        if j >= 4:
                            finish(i, j - 4)

            @block.scalar
            def _(act):
                def exp(i, s):
                    _, nk, _ = keys(steps[s][2])
                    at = i * NS + s
                    act.wait_ge(shifts.sem, shifts.at((at + 1) * n_shifts))
                    for x in range(2):
                        pr = prob[:, s % 3, x, 0:nk]
                        nc.scalar.activation(pr, pr, ACT.Exp, bias=st[:, s % 4, 1, x:x + 1],
                                             accum_out=st[:, s % 4, 2, x:x + 1]).then_inc(probs.sem, 1)
                    if sink is not None:
                        nc.scalar.activation(stat(s, 4), stat(s, 3), ACT.Exp).then_inc(probs.sem, 1)

                def keep(i, s):
                    _, _, blocks = keys(steps[s][2])
                    r, w = blocks[0][1], 2 * P * len(blocks)
                    act.wait_ge(mixed.sem, mixed.at(i * NS + (s - 1)))
                    act.wait_ge(turned.sem, turned.at(i * NS + (s + 1)))
                    nc.scalar.activation(pT[0:r, s % 2, 0:w], T[0:r, 0:w], ACT.Copy).then_inc(kept.sem, 1)

                with act.Fori(0, loops) as i:
                    act.wait_ge(mixed.sem, mixed.at(i * NS))
                    nc.scalar.activation(qs[:, :, :], q(i), ACT.Copy).then_inc(staged.sem, 1)
                    nc.scalar.activation(ks[:, :, :], k(i), ACT.Copy).then_inc(staged.sem, 1)
                    nc.scalar.activation(vs[0:v(i).shape[0]], v(i), ACT.Copy).then_inc(staged.sem, 1)
                    for j in range(NS + 2):
                        if j < NS:
                            exp(i, j)
                        if j >= 2:
                            keep(i, j - 2)
        total = loops * NS
        staged.advance(3 * loops)
        if table is not None:
            landed.advance(16 * loops)
        for sgn, k in ((logits, n_logits), (peaks, n_peaks), (shifts, n_shifts), (probs, n_probs), (dens, n_dens),
                       (ready, 2), (scores, 1), (turned, 1), (kept, 1), (mixed, 1), (outs, 1)):
            sgn.advance(total * k)

    @staticmethod
    def causal(t):
        return 0, (t + 1) * P, [(b, P) for b in range(t + 1)]

    def odd(self):
        nc, d = self.nc, self.d
        w = d["o_w_in"][0]
        hi, lo = self.xs_hi, self.xs_lo
        xh, xl = (lambda k: hi[:, k, :]), (lambda k: lo[:, k, :])
        self.norm_stream(self.gains[:, 1, :], hi, lo, self.xtmp)
        with ExitStack() as c:
            oT = self.sb(c, "oT_o", [P, MT, 512])
            with ExitStack() as c2:
                qT = self.sb(c2, "qT", [P, MT, 512])
                kT = self.sb(c2, "kT", [P, MT, 512])
                vt = self.sb(c2, "vt2", [P, QT, DM])
                mask = self.sb(c2, "mask", [P, QT, 512])
                with ExitStack() as c3:
                    ckv = self.sb(c3, "ckv", [P, 2, 512])
                    qi = self.sb(c3, "qi", [P, 2, 512])
                    ki = self.sb(c3, "ki", [P, 512])
                    wi = self.sb(c3, "wi", [P, 512])
                    wit = self.sb(c3, "wit", [P, QT, P])
                    small = self.sb(c3, "odd_small", [P, 4])
                    member, spread = self.sb(c3, "member", [P, MT, NH]), self.sb(c3, "spread", [NH, MT, P])
                    gq, gk, gkv = small[:, 0:1], small[:, 1:2], small[:, 2:4]
                    one = lambda ap: ap.rearrange("(p a) -> p a", a=1)
                    self.load([(small[64 * s:64 * s + 64, k:k + 1], one(d[nm][0])) for s in range(2)
                               for k, nm in enumerate(("o_g_q", "o_g_k"))]
                              + [(gkv, d["o_g_kv"][0].rearrange("(m p) -> p m", p=P)), (member[:, :, :], d["c_member"]),
                                 (spread[:, :, :], d["c_spread"])])
                    self.dense("o_q", xh, xl,
                               self.keep(lambda i, j: flat(qT[:, rows(i * 2 + j), :])))
                    dsts = [ckv[:, 0, :], ckv[:, 1, :], qi[:, 0, :], qi[:, 1, :]]
                    self.dense("o_ckv_qi", xh, xl,
                               self.keep(lambda i, j: dsts[2 * i + j]))
                    tiles = [[(1536, 64), (1536, 64)], [(1600, 64), (1664, 64)]]
                    self.dense("o_ki_wi", xh, xl,
                               self.keep(lambda i, j: (ki, wi)[j][:, :]))
                    self.norm_heads(qT, NH, HD, member, spread, lambda m: gq)
                    ch = self.sb(c3, "ckv_hi", [P, 2, 512], F32R)
                    cl = self.sb(c3, "ckv_lo", [P, 2, 512], F32R)
                    self.norm(1, 2, lambda m: ckv[:, m, :], lambda m: gkv[:, m:m + 1], lambda m: self.xtmp[:, m % 2, :],
                              lambda m: ch[:, m, :], lambda m: cl[:, m, :])
                    self.dense("o_uk", lambda k: ch[:, k, :],
                               lambda k: cl[:, k, :], self.keep(lambda i, j: flat(kT[:, rows(i * 2 + j), :])))
                    self.norm_heads(kT, NH, HD, member, spread, lambda m: gk)
                    vF = oT
                    self.dense("o_uv", lambda k: ch[:, k, :],
                               lambda k: cl[:, k, :], self.keep(lambda i, j: flat(vF[:, rows(i * 2 + j), :])))
                    self.turn(MT, lambda m, t: vF[:, m, t * P:(t + 1) * P], lambda m: vt[:, :, m * P:(m + 1) * P])
                    self.turn(1, lambda m, t: wi[:, t * P:(t + 1) * P], lambda m: wit[:, :, :])
                    self.choose(c3, qi, ki, wit, mask)
                zT = self.sb(c2, "zT", [P, MT, 512])
                silu = lambda j: [("act", lambda i, ps: nc.scalar.activation(flat(zT[:, rows(i * 2 + j), :]), ps, ACT.Silu))]
                self.dense("o_z", xh, xl, [silu(0), silu(1)])
                self.attention(lambda i: qT[:, rows(i * 2, 2), :], lambda i: kT[:, rows(i * 2, 2), :], (2, 512),
                               lambda i: vt[:, :, rows(i * 256, 256)], [P, QT, 256], 4, self.causal, 512, 0, oT,
                               mask=lambda t, nk: mask[:, t:t + 1, 0:nk].broadcast_to([P, 2, nk]))
                self.multiply(oT, zT)
            self.project_out(c, oT, "o_out")

    def multiply(self, x, y):
        nc, done = self.nc, self.sig("multiplied")
        with self.block() as block:
            @block.vector
            def _(dve):
                nc.vector.tensor_tensor(x[:, :, :], x[:, :, :], y[:, :, :], ALU.mult).then_inc(done.sem, 1)

    def choose(self, c, qi, ki, wit, mask):
        nc, d = self.nc, self.d
        dots, acts, acc = self.sig("idx_dots"), self.sig("idx_relu"), self.sig("idx_step")
        sc = self.sb(c, "idx_score", [P, 512])
        rl = self.sb(c, "idx_relu_buf", [P, 2, 512])
        top = self.sb(c, "idx_top", [P, 8])
        later = self.sb(c, "idx_later", [P, P])
        self.load([(later[:, :], d["c_later"])])
        nrel = 12
        with self.block() as block:
            @block.tensor
            def _(pe):
                for n in range(nrel):
                    t, h = 1 + n // 4, n % 4
                    nk = (t + 1) * P
                    if n >= 2:
                        pe.wait_ge(acts.sem, n - 1)
                    s = 64 * (h % 2)
                    nc.tensor.matmul(self.ps[n % 2][:, 0:nk], qi[s:s + 64, h // 2, t * P:(t + 1) * P],
                                     ki[s:s + 64, 0:nk], start=True, stop=True).then_inc(dots.sem, 1)

            per_tile = 4 + 1 + 2 * (TOPK // 8) + 2

            def head_done(n):
                return (n // 4) * per_tile + n % 4 + 1 + 1

            @block.scalar
            def _(act):
                for n in range(nrel):
                    t = 1 + n // 4
                    nk = (t + 1) * P
                    act.wait_ge(dots.sem, n + 1)
                    if n >= 2:
                        act.wait_ge(acc.sem, head_done(n - 2))
                    nc.scalar.activation(rl[:, n % 2, 0:nk], self.ps[n % 2][:, 0:nk], ACT.Relu,
                                         scale=(64 ** -0.5) * (4 ** -0.5)).then_inc(acts.sem, 1)

            @block.vector
            def _(dve):
                n = 0

                def link(ins):
                    nonlocal n
                    n += 1
                    ins.then_inc(acc.sem, 1)
                    dve.wait_ge(acc.sem, n)

                link(nc.vector.memset(mask[:, 0, :], 0.0))
                for t in range(1, QT):
                    nk = (t + 1) * P
                    s = sc[:, 0:nk]
                    for h in range(4):
                        k = (t - 1) * 4 + h
                        dve.wait_ge(acts.sem, k + 1)
                        wt = wit[:, t, h:h + 1]
                        if h == 0:
                            link(nc.vector.tensor_scalar(s, rl[:, k % 2, 0:nk], wt, None, ALU.mult))
                        else:
                            link(nc.vector.scalar_tensor_tensor(s, rl[:, k % 2, 0:nk], wt, s, ALU.mult, ALU.add))
                    link(nc.vector.tensor_tensor(sc[:, t * P:nk], sc[:, t * P:nk], later[:, :], ALU.add))
                    for _ in range(TOPK // 8):
                        link(nc.vector.max(top[:, :], s))
                        link(nc.vector.match_replace(s, top[:, :], s, CUT))
                    link(nc.vector.tensor_scalar(s, s, CUT, 1.0, ALU.is_equal, ALU.subtract))
                    link(nc.vector.tensor_scalar(mask[:, t, 0:nk], s, -NEG, None, ALU.mult))

    def project_out(self, c, oT, name, bias=None):
        o_hi = self.sb(c, f"o_hi{self.stage_n}", [P, MT, 512], F32R)
        o_lo = self.sb(c, f"o_lo{self.stage_n}", [P, MT, 512], F32R)
        self.stage_n += 1
        self.split_tiles(MT, lambda m: oT[:, m, :], lambda m: o_hi[:, m, :], lambda m: o_lo[:, m, :])
        self.dense(name, lambda k: o_hi[:, k, :], lambda k: o_lo[:, k, :], self.add_residual(bias))

    def windowed(self):
        nc, d = self.nc, self.d
        w = d["a_w_qkv_2"][0]
        hi, lo = self.xs_hi, self.xs_lo
        xh, xl = (lambda k: hi[:, k, :]), (lambda k: lo[:, k, :])
        self.norm_stream(self.gains[:, 2, :], hi, lo, self.xtmp)
        with ExitStack() as c:
            oT = self.sb(c, "oT_w", [P, MT, 512])
            small = self.sb(c, "win_small", [P, 40])
            bq, bk, bv, bo, sink = small[:, 0:8], small[:, 8:10], small[:, 10:11], small[:, 11:19], small[:, 20:36]
            b = d["a_b_qkv_2"][0]
            col = lambda ap: ap.rearrange("(m p) -> p m", p=ap.shape[0] if ap.shape[0] < P else P)
            self.load([(bq, col(b[0:1024])), (bv, col(b[1152:1280])), (bo, col(d["a_b_o_2"][0])),
                       (sink, d["a_sinks_2"].broadcast_to([P, NH]))]
                      + [(small[64 * s:64 * s + 64, 8 + g:9 + g], col(b[1024 + 64 * g:1088 + 64 * g]))
                         for s in range(2) for g in range(2)])
            with ExitStack() as c2:
                qT = self.sb(c2, "qT_w", [P, MT, 512])
                kT = self.sb(c2, "kT_w", [P, 2, 512])
                vF = self.sb(c2, "vF_w", [P, 512])
                vt = self.sb(c2, "vt_w", [P, QT, P])
                step = lambda j: [("act", lambda i, ps: nc.scalar.activation(
                    flat(qT[:, rows(i * 2 + j), :]), ps, ACT.Identity, bias=bq[:, rows(i * 2 + j)]))]
                self.dense("a_q", xh, xl, [step(0), step(1)])
                dst = [(kT[:, 0, :], bk[:, 0:1]), (kT[:, 1, :], bk[:, 1:2]), (vF[:, :], bv), (vF[:, :], bv)]
                step2 = lambda j: [("act", lambda i, ps: nc.scalar.activation(dst[2 * i + j][0], ps, ACT.Identity,
                                                                              bias=dst[2 * i + j][1]))]
                self.dense("a_kv", xh, xl, [step2(0), step2(1)])
                self.turn(1, lambda m, t: vF[:, t * P:(t + 1) * P], lambda m: vt[:, :, :])

                def keys(t):
                    return (0, P, [(0, P)]) if t == 0 else ((t - 1) * P, 2 * P, [(t - 1, P), (t, P)])
                self.attention(lambda i: qT[:, rows(i * 4, 4), :], lambda i: kT[:, rows(i), :], (1, 512),
                               lambda i: vt[:, :, rows(i * HD, HD)], [P, QT, HD], 8, keys, 256, 1, oT,
                               sink=sink.rearrange("p (a e) -> p a e", e=2))
            self.project_out(c, oT, "a_out", bias=bo)

    def feed_forward(self, layer):
        nc, d = self.nc, self.d
        w, wd = d["ffn_w_gu_2"][layer], d["ffn_w_down_2"][layer]
        hi, lo = self.xs_hi, self.xs_lo
        self.norm_stream(self.gains[:, 4 + layer, :], hi, lo, self.xtmp)
        T = DFF // P
        with ExitStack() as c:
            a_hi = self.sb(c, f"a_hi{layer}", [P, T, 512], F32R)
            a_lo = self.sb(c, f"a_lo{layer}", [P, T, 512], F32R)
            tmp = self.sb(c, f"ff_tmp{layer}", [P, 2, 512])
            gate = [("act", lambda i, ps: nc.scalar.activation(tmp[:, 0, :], ps, ACT.Silu))]
            up = [("dve", lambda i, ps: nc.vector.tensor_tensor(tmp[:, 1, :], ps, tmp[:, 0, :], ALU.mult)),
                  ("act", lambda i, ps: nc.scalar.activation(flat(a_hi[:, rows(i), :]), tmp[:, 1, :], ACT.Copy)),
                  ("dve", lambda i, ps: nc.vector.tensor_tensor(flat(a_lo[:, rows(i), :]), tmp[:, 1, :],
                                                                flat(a_hi[:, rows(i), :]).bitcast(F32), ALU.subtract))]
            self.dense(f"ff_gu{layer}", lambda k: hi[:, k, :], lambda k: lo[:, k, :], [gate, up])
            self.dense(f"ff_down{layer}", lambda k: a_hi[:, k, :], lambda k: a_lo[:, k, :],
                       self.add_residual())

    def sparse(self):
        nc, d = self.nc, self.d
        w = d["b_w_in_2"][0]
        hi, lo = self.xs_hi, self.xs_lo
        xh, xl = (lambda k: hi[:, k, :]), (lambda k: lo[:, k, :])
        self.norm_stream(self.gains[:, 3, :], hi, lo, self.xtmp)
        with ExitStack() as c:
            oT = self.sb(c, "oT_s", [P, MT, 512])
            with ExitStack() as c2:
                qT = self.sb(c2, "qT_s", [P, MT, 512])
                kT = self.sb(c2, "kT_s", [P, 2, 2, 512])
                vt = self.sb(c2, "vt_s", [P, 2, QT, P])
                gt = self.sb(c2, "gt_s", [P, QT, P])
                kcT = self.sb(c2, "kcT", [P, 2, 32])
                vc = self.sb(c2, "vc", [32, 2, HD])
                seen = self.sb(c2, "seen", [P, 1])
                self.dense("b_q", xh, xl,
                           self.keep(lambda i, j: flat(qT[:, rows(i * 2 + j), :])))
                with ExitStack() as c3:
                    cT = self.sb(c3, "cmpT", [P, 2, 2, 512])
                    vF = self.sb(c3, "vF_s", [P, 3, 512])
                    dsts = [dst[:, h, :] for dst in (cT[:, 0], cT[:, 1], kT[:, 0], kT[:, 1]) for h in range(2)]
                    dsts += [vF[:, 0, :], vF[:, 1, :], vF[:, 2, :], vF[:, 2, :]]

                    def step(j):
                        def f(i, ps):
                            return nc.scalar.activation(dsts[2 * i + j], ps, ACT.Sigmoid if 2 * i + j >= 10 else ACT.Copy)
                        return [("act", f)]
                    self.dense("b_rest", xh, xl, [step(0), step(1)])
                    outs = [vt[:, 0], vt[:, 1], gt[:, :, :]]
                    self.turn(3, lambda m, t: vF[:, m, t * P:(t + 1) * P], lambda m: outs[m])
                    self.compress(c3, cT, kcT, vc)
                self.load([(seen[:, :], d["c_seen"])])
                self.scale_rows(gt[:, 0, :], seen)
                gates = gt[:, :, 80:128].rearrange("p t (a e g) -> p t a e g", e=2, g=3)
                gate = lambda g: lambda p, half, t: gates[:, t, rows(p, 2), half, g]
                qs = lambda i: qT[:, rows(i * 4, 4), :]

                def cmp_keys(t):
                    n = 8 * t + 7
                    return 0, n, [(0, n)]
                self.attention(qs, lambda i: kcT[:, rows(i), 0:NCMP], (1, NCMP), lambda i: vc[0:NCMP, rows(i), :],
                               [32, 1, HD], 8, cmp_keys, 512, 2, oT, gate=gate(0),
                               bias_at=lambda t, nk: slice(415 - P * t, 416 - P * t + 16 * (nk - 1), 16))
                for s in range(2):
                    self.attention(qs, lambda i: kT[:, s, rows(i), :], (1, 512), lambda i: vt[:, s, :, rows(i * HD, HD)],
                                   [P, QT, HD], 8, self.causal, 512, None, oT, add=True, gate=gate(1 + s))
            self.project_out(c, oT, "b_out")

    def scale_rows(self, gt, seen):
        nc, done = self.nc, self.sig("rows_scaled")
        with self.block() as block:
            @block.vector
            def _(dve):
                g = gt[:, 80:128].rearrange("p (h g) -> p h g", g=3)[:, :, 0]
                nc.vector.tensor_scalar(g, g, seen[:, 0:1], None, ALU.mult).then_inc(done.sem, 1)

    def compress(self, c, cT, kcT, vc):
        nc, d = self.nc, self.d
        N = 2 * NCMP
        blk = self.sb(c, "cmp_blk", [P, 16, N])
        w1 = self.sb(c, "cmp_w1", [P, 16, 256])
        w2 = self.sb(c, "cmp_w2", [P, 2, P])
        pos = self.sb(c, "cmp_pos", [P, 16])
        hid = self.sb(c, "cmp_hid", [P, 2, N])
        arg = self.sb(c, "cmp_arg", [P, 2, N])
        built, made, step = self.sig("cmp_built"), self.sig("cmp_made"), self.sig("cmp_step")
        second, kept = self.sig("cmp_second"), self.sig("cmp_kept")
        for s in range(2):
            w2d = d["b_cmp_w2_2"][0, s].rearrange("(m p) c -> p m c", p=P)
            self.load([(w1[:, :, :], d["b_cmp_w1_2"][0, s].rearrange("(j p) c -> p j c", p=P)),
                       (w2[:, :, 0:HD], w2d), (w2[:, :, HD:P], w2d),
                       (pos[:, :], d["b_cmp_pos_2"][0, s].rearrange("(j e) c -> (e c) j", e=2))])
            with self.block() as block:
                @block.vector
                def _(dve):
                    for half in range(2):
                        r = slice(64 * half, 64 * half + 64)
                        for h in range(2):
                            x = cT[r, s, h, :].rearrange("p (b j e) -> p e j b", j=8, e=2)
                            for b in range(2):
                                ins = nc.vector.tensor_tensor(
                                    blk[r, 8 * b:8 * b + 8, NCMP * h:NCMP * (h + 1)], x[:, half, :, b:b + NCMP],
                                    pos[r, 8 * b:8 * b + 8].rearrange("p (j a) -> p j a", a=1).broadcast_to([64, 8, NCMP]),
                                    ALU.add)
                    ins.then_inc(built.sem, 1)
                    dve.wait_ge(made.sem, s + 1)
                    h0 = hid[:, :, :].rearrange("p m n -> p (m n)")
                    a0 = arg[:, :, :].rearrange("p m n -> p (m n)")
                    ps = self.ps[0][:, 0:2 * N]
                    b0 = 6 * s
                    nc.vector.tensor_copy(h0, ps).then_inc(step.sem, 1)
                    dve.wait_ge(step.sem, b0 + 1)
                    nc.vector.tensor_tensor(a0, h0, h0, ALU.mult).then_inc(step.sem, 1)
                    dve.wait_ge(step.sem, b0 + 2)
                    nc.vector.tensor_scalar(a0, a0, 0.044715, 1.0, ALU.mult, ALU.add).then_inc(step.sem, 1)
                    dve.wait_ge(step.sem, b0 + 3)
                    nc.vector.tensor_tensor(a0, a0, h0, ALU.mult).then_inc(step.sem, 1)
                    dve.wait_ge(step.sem, b0 + 5)
                    nc.vector.tensor_tensor(h0, a0, h0, ALU.mult).then_inc(step.sem, 1)
                    dve.wait_ge(second.sem, s + 1)
                    if s == 0:
                        nc.vector.tensor_copy(kcT[:, :, 0:NCMP], self.ps[1][:, 0:N].rearrange("p (h n) -> p h n", h=2))
                    else:
                        nc.vector.tensor_copy(vc[0:NCMP, :, :], self.ps[1][0:NCMP, 0:2 * HD].rearrange("p (h n) -> p h n", h=2))

                @block.scalar
                def _(act):
                    a0 = arg[:, :, :].rearrange("p m n -> p (m n)")
                    act.wait_ge(step.sem, 6 * s + 4)
                    nc.scalar.activation(a0, a0, ACT.Sigmoid, scale=2 * math.sqrt(2 / math.pi)).then_inc(step.sem, 1)

                @block.tensor
                def _(pe):
                    pe.wait_ge(built.sem, s + 1)
                    for m in range(2):
                        for j in range(16):
                            ins = nc.tensor.matmul(self.ps[0][:, m * N:(m + 1) * N], w1[:, j, m * P:(m + 1) * P], blk[:, j, :],
                                                   start=(j == 0), stop=(j == 15))
                    ins.then_inc(made.sem, 1)
                    pe.wait_ge(step.sem, 6 * s + 6)
                    if s == 0:
                        for m in range(2):
                            ins = nc.tensor.matmul(self.ps[1][:, 0:N], w2[:, m, :], hid[:, m, :], start=(m == 0), stop=(m == 1))
                    else:
                        for h in range(2):
                            for m in range(2):
                                ins = nc.tensor.matmul(self.ps[1][0:NCMP, HD * h:HD * (h + 1)],
                                                       hid[:, m, NCMP * h:NCMP * (h + 1)], w2[:, m, 0:HD],
                                                       start=(m == 0), stop=(m == 1))
                    ins.then_inc(second.sem, 1)

    def finish(self, out, final=True):
        nc, d = self.nc, self.d
        stored = self.sig("stored")
        with ExitStack() as c:
            y = self.sb(c, "y", [P, MT, 512])
            tok = self.sb(c, "tok", [P, QT, DM])
            g = self.sb(c, "final_gain", [P, MT])
            self.load([(g[:, :], d["final_norm_2"].rearrange("(m p) -> p m", p=P))])
            if final:
                self.norm(1, MT, lambda m: self.hT[:, m, :], lambda m: g[:, m:m + 1], lambda m: y[:, m, :])
            src = y if final else self.hT
            self.turn(MT, lambda m, t: src[:, m, t * P:(t + 1) * P], lambda m: tok[:, :, m * P:(m + 1) * P])
            with self.block() as block:
                @block.sync
                def _(sp):
                    sp.dma_start(out[0].rearrange("(t p) c -> p t c", p=P), tok[:, :, :]).then_inc(stored.sem, 16)
                    sp.wait_ge(stored.sem, 16)


def build(nc, dram, out, layers=6):
    with ExitStack() as ctx:
        k = Kernel(nc, dram, ctx)
        k.setup()
        for stage in (k.even, k.odd, k.windowed, lambda: k.feed_forward(0), k.sparse, lambda: k.feed_forward(1))[:layers]:
            stage()
        k.finish(out, layers == 6)


def _buckets(dist, max_dist):
    rel = np.maximum(dist, 0)
    f = np.maximum(rel, 1).astype(np.float32)
    large = 16 + (np.log(f / np.float32(16)) / np.float32(math.log(max_dist / 16)) * np.float32(16)).astype(np.int32)
    return np.where(rel < 16, rel, np.minimum(large, 31))


def _one_hot(max_dist, valid):
    dist = 511 - np.arange(BIAS_L)
    hot = np.zeros((33, BIAS_L), np.float32)
    ok = valid(dist)
    hot[_buckets(dist, max_dist)[ok], np.nonzero(ok)[0]] = 1.0
    hot[32, ~ok] = NEG
    return hot


def _constants():
    pos = np.arange(SEQ)
    cnt = np.stack([1.0 / np.minimum(pos + 1, w).astype(np.float32) for w in (2, 4, 8, 16)]).astype(np.float32)
    feature = np.arange(P)[:, None] + P * np.arange(MT)[None, :]
    member = (feature[:, :, None] // HD == np.arange(NH)).astype(np.float32)
    member4 = (feature[:, :, None] // 256 == np.arange(4)).astype(np.float32)
    return {
        "c_ident": np.eye(P, dtype=np.float32),
        "c_one": np.ones((1, NH), np.float32),
        "c_member": member, "c_spread": member.transpose(2, 1, 0).copy(),
        "c_member4": member4, "c_spread4": member4.transpose(2, 1, 0).copy(),
        "c_pool": np.broadcast_to(cnt, (P, 4, SEQ)).copy(),
        "c_tri": np.triu(np.ones((P, P), np.float32)),
        "c_later": np.where(np.arange(P)[None, :] > np.arange(P)[:, None], BEYOND, 0).astype(np.float32),
        "c_seen": (np.arange(P) >= 31).astype(np.float32).reshape(P, 1),
        "c_hot": np.stack([_one_hot(128, lambda x: x >= 0), _one_hot(1024, lambda x: (x >= 0) & (x < 128)),
                           _one_hot(1024, lambda x: x >= 0)]),
    }


def kernel(**inputs):
    import concourse.bacc as bacc
    from concourse.bass_utils import run_bass_kernel_spmd as run

    nc = bacc.Bacc("TRN2", target_bir_lowering=False, num_devices=1)
    arrays = {n: np.ascontiguousarray(a) for n, a in inputs.items()}
    arrays.update(_constants())
    dram = {n: nc.dram_tensor(f"in_{n}", a.shape, F32, kind="ExternalInput").ap() for n, a in arrays.items()}
    dram["s_rows"] = nc.dram_tensor("s_rows", (2, 4, 512), F32, kind="Internal").ap()
    dram["s_bias"] = nc.dram_tensor("s_bias", (3, NH, BIAS_L), F32, kind="Internal").ap()
    dram["s_skew"] = nc.dram_tensor("s_skew", (3, NH, P, BIAS_L), F32, kind="Internal").ap()
    out = nc.dram_tensor("out", (1, SEQ, DM), F32, kind="ExternalOutput").ap()
    build(nc, dram, out, LAYERS)
    r = run(nc, [{f"in_{n}": a for n, a in arrays.items()}], core_ids=[0])
    return r.results[0]["out"]


LAYERS = 6
```

```python
import math
from contextlib import ExitStack

import numpy as np

import concourse.bass as bass
from concourse import mybir

F32 = mybir.dt.float32
F32R = mybir.dt.float32r
ALU = mybir.AluOpType
ACT = mybir.ActivationFunctionType
AX_X = mybir.AxisListType.X

P = 128
SEQ = 512
DM = 1024
MT = DM // P
QT = SEQ // P
EPS = 1e-6
NEG = -1e30
CUT = -3e38
BEYOND = -1e38
CREDIT = 64
HD = 64
NH = 16
TOPK = 128
DFF = 2816
NCMP = 31
CREDITED = ["small_loads", "tile_turned", "tile_kept", "norm_squared", "norm_summed", "norm_var", "norm_std",
            "norm_inv", "norm_scaled", "norm_high", "norm_low", "weights_landed0", "weights_landed1",
            "weights_high", "weights_low", "tile_summed", "tile_steps",
            "gate_rows_spread", "gate_floors_spread", "mem_k_staged", "mem_v_staged", "mem_scores", "mem_gaps", "mem_decays", "mem_weighed",
            "mem_masked", "mem_read", "mem_tail", "idx_found", "idx_marked", "att_bias0", "att_bias1", "att_staged", "att_values_staged", "att_scores", "att_logits", "att_peaks", "att_shifts", "att_probs", "att_dens",
            "att_ready", "att_turned", "att_kept", "att_mixed", "att_outs", "heads_squared", "heads_summed",
            "heads_root", "heads_spread", "heads_scaled"]
BIAS_L = 640


class Signal:

    def __init__(self, sem, base):
        self.sem = sem
        self.base = base

    def at(self, n):
        return n + self.base

    def advance(self, n):
        self.base += n


class Stage:

    def __init__(self, on_sp, on_act, on_pe, on_dve, wait, done):
        self.on_sp, self.on_act, self.on_pe, self.on_dve = on_sp, on_act, on_pe, on_dve
        self.wait, self.done = wait, done


def rows(i, n=1):
    return bass.ds(i, n)


def flat(ap):
    return ap.rearrange("p a b -> p (a b)")


class Kernel:
    def __init__(self, nc, dram, ctx):
        self.nc, self.d, self.ctx = nc, dram, ctx
        self.signals = {}
        self.stage_n = 0
        self.banks = ctx.enter_context(nc.psum_tensor("banks", [P, 8, 512], F32))
        self.ps = [self.banks[:, i, :] for i in range(8)]
        self.plan = self.weight_plan()
        self.planned = 0

    def sb(self, ctx, name, shape, dt=F32):
        return ctx.enter_context(self.nc.sbuf_tensor(name, shape, dt))

    def sig(self, name):
        if name not in self.signals:
            credit = CREDIT if name in CREDITED else 0
            self.signals[name] = Signal(self.ctx.enter_context(self.nc.semaphore(name)), credit)
        return self.signals[name]

    def block(self):
        return self.nc.Block(no_gpsimd_drain=True)

    def load(self, pairs):
        nc, arrived = self.nc, self.sig("small_loads")
        with self.block() as block:
            @block.sync
            def _(sp):
                for dst, src in pairs:
                    sp.dma_start(dst, src, allow_slow_non_contiguous=True).then_inc(arrived.sem, 16)
                sp.wait_ge(arrived.sem, arrived.at(16 * len(pairs)))
        arrived.advance(16 * len(pairs))

    def start_load(self, name, pairs):
        nc, arrived = self.nc, self.sig(name)
        with self.block() as block:
            @block.sync
            def _(sp):
                for dst, src in pairs:
                    sp.dma_start(dst, src, allow_slow_non_contiguous=True).then_inc(arrived.sem, 16)
        arrived.advance(16 * len(pairs))

    def arrived(self, name):
        with self.block() as block:
            @block.sync
            def _(sp):
                sp.wait_ge(self.sig(name).sem, self.sig(name).at(0))

    def turn(self, tiles, src, dst):
        nc, turned, kept = self.nc, self.sig("tile_turned"), self.sig("tile_kept")
        with self.block() as block:
            @block.tensor
            def _(pe):
                for m in range(tiles):
                    pe.wait_ge(kept.sem, kept.at(m - 1))
                    for t in range(4):
                        ins = nc.tensor.transpose(self.banks[:, m % 2, t * P:(t + 1) * P], src(m, t), self.ident[:, :])
                    ins.then_inc(turned.sem, 1)

            @block.vector
            def _(dve):
                for m in range(tiles):
                    dve.wait_ge(turned.sem, turned.at(m + 1))
                    nc.vector.tensor_copy(dst(m), self.ps[m % 2][:, :].rearrange("p (t c) -> p t c", t=4)).then_inc(kept.sem, 1)
        turned.advance(tiles)
        kept.advance(tiles)

    def norm(self, c, tiles, src, gain, out, hi=None, lo=None, squares=None, loads=None, wait_loads=False):
        nc = self.nc
        squared, summed = self.sig("norm_squared"), self.sig("norm_summed")
        var, std, inv = self.sig("norm_var"), self.sig("norm_std"), self.sig("norm_inv")
        scaled, high, low = self.sig("norm_scaled"), self.sig("norm_high"), self.sig("norm_low")
        parts = tiles if squares is None else 1
        if squares is None:
            sq = self.sb(c, f"sq{self.stage_n}", [P, 2, 512])
        rs = self.sb(c, f"rs{self.stage_n}", [P, 2, 512])
        self.stage_n += 1
        arrived = self.sig(loads[0]) if loads is not None else None

        def on_sp(sp):
            if loads is not None:
                for dst, load in loads[1]:
                    sp.dma_start(dst, load, allow_slow_non_contiguous=True).then_inc(arrived.sem, 16)

        def on_act(act):
            if squares is None:
                for m in range(tiles):
                    act.wait_ge(summed.sem, summed.at(m - 1))
                    nc.scalar.activation(sq[:, m % 2, :], src(m), ACT.Square).then_inc(squared.sem, 1)
            act.wait_ge(var.sem, var.at(1))
            nc.scalar.activation(rs[:, 0, :], rs[:, 0, :], ACT.Sqrt).then_inc(std.sem, 1)
            if hi is not None:
                for m in range(tiles):
                    act.wait_ge(scaled.sem, scaled.at(m + 1))
                    nc.scalar.activation(hi(m), out(m), ACT.Copy).then_inc(high.sem, 1)
            if wait_loads:
                act.wait_ge(arrived.sem, arrived.at(16 * len(loads[1])))

        def on_pe(pe):
            for m in range(parts):
                if squares is None:
                    pe.wait_ge(squared.sem, squared.at(m + 1))
                part = sq[:, m % 2, :] if squares is None else squares[:, :]
                nc.tensor.matmul(self.ps[2][:, :], self.ones[:, :], part, start=(m == 0),
                                 stop=(m == parts - 1)).then_inc(summed.sem, 1)

        def on_dve(dve):
            dve.wait_ge(summed.sem, summed.at(parts))
            nc.vector.tensor_scalar(rs[:, 0, :], self.ps[2][:, :], 1.0 / (tiles * P), EPS, ALU.mult,
                                    ALU.add).then_inc(var.sem, 1)
            dve.wait_ge(std.sem, std.at(1))
            nc.vector.reciprocal(rs[:, 1, :], rs[:, 0, :]).then_inc(inv.sem, 1)
            dve.wait_ge(inv.sem, inv.at(1))
            for m in range(tiles):
                if hi is not None:
                    dve.wait_ge(high.sem, high.at(m - 1))
                    dve.wait_ge(low.sem, low.at(m - 1))
                nc.vector.scalar_tensor_tensor(out(m), src(m), gain(m), rs[:, 1, :], ALU.mult,
                                               ALU.mult).then_inc(scaled.sem, 1)
                if hi is not None and m >= 1:
                    dve.wait_ge(high.sem, high.at(m))
                    nc.vector.tensor_tensor(lo(m - 1), out(m - 1), hi(m - 1).bitcast(F32), ALU.subtract).then_inc(low.sem, 1)
            if hi is not None:
                dve.wait_ge(high.sem, high.at(tiles))
                nc.vector.tensor_tensor(lo(tiles - 1), out(tiles - 1), hi(tiles - 1).bitcast(F32),
                                        ALU.subtract).then_inc(low.sem, 1)
        def wait(pe, m):
            pe.wait_ge(low.sem, low.at(m + 1))

        def done():
            if squares is None:
                squared.advance(tiles)
            summed.advance(parts)
            for sgn in (var, std, inv):
                sgn.advance(1)
            scaled.advance(tiles)
            if hi is not None:
                high.advance(tiles)
                low.advance(tiles)
            if loads is not None:
                arrived.advance(16 * len(loads[1]))
        return Stage(on_sp, on_act, on_pe, on_dve, wait, done)

    def run(self, make):
        with ExitStack() as c:
            stage = make(c)
            with self.block() as block:
                block.sync(stage.on_sp)
                block.scalar(stage.on_act)
                block.tensor(stage.on_pe)
                block.vector(stage.on_dve)
            stage.done()

    def norm_heads(self, x, heads, width, member, spread, gain):
        nc = self.nc
        squared, summed, root = self.sig("heads_squared"), self.sig("heads_summed"), self.sig("heads_root")
        out, scaled = self.sig("heads_spread"), self.sig("heads_scaled")
        with ExitStack() as ctx:
            sq = self.xtmp
            rs = self.sb(ctx, f"hrs{self.stage_n}", [heads, 2, 512])
            self.stage_n += 1
            block = ctx.enter_context(self.block())

            @block.scalar
            def _(act):
                for m in range(MT):
                    act.wait_ge(summed.sem, summed.at(m - 1))
                    nc.scalar.activation(sq[:, m % 2, :], x[:, m, :], ACT.Square).then_inc(squared.sem, 1)
                act.wait_ge(root.sem, root.at(1))
                nc.scalar.activation(rs[:, 0, :], rs[:, 0, :], ACT.Sqrt).then_inc(root.sem, 1)

            @block.tensor
            def _(pe):
                for m in range(MT):
                    pe.wait_ge(squared.sem, squared.at(m + 1))
                    nc.tensor.matmul(self.ps[0][0:heads, :], member[:, m, :], sq[:, m % 2, :], start=(m == 0),
                                     stop=(m == MT - 1)).then_inc(summed.sem, 1)
                pe.wait_ge(root.sem, root.at(3))
                for m in range(MT):
                    pe.wait_ge(scaled.sem, scaled.at(m - 1))
                    nc.tensor.matmul(self.ps[1 + m % 2][:, :], spread[:, m, :], rs[:, 1, :], start=True,
                                     stop=True).then_inc(out.sem, 1)

            @block.vector
            def _(dve):
                dve.wait_ge(summed.sem, summed.at(MT))
                nc.vector.tensor_scalar(rs[:, 0, :], self.ps[0][0:heads, :], 1.0 / width, EPS, ALU.mult,
                                        ALU.add).then_inc(root.sem, 1)
                dve.wait_ge(root.sem, root.at(2))
                nc.vector.reciprocal(rs[:, 1, :], rs[:, 0, :]).then_inc(root.sem, 1)
                for m in range(MT):
                    dve.wait_ge(out.sem, out.at(m + 1))
                    nc.vector.scalar_tensor_tensor(x[:, m, :], x[:, m, :], gain(m), self.ps[1 + m % 2][:, :], ALU.mult,
                                                   ALU.mult).then_inc(scaled.sem, 1)
        for s in (squared, summed, out, scaled):
            s.advance(MT)
        root.advance(3)

    def dense(self, name, x_hi, x_lo, steps, prepare=None, spread=None, on_pool=None, side=None):
        nc = self.nc
        spec = self.plan[self.planned]
        assert spec[0] == name, (spec[0], name)
        self.planned += 1
        after_this = self.plan[self.planned] if self.planned < len(self.plan) else None
        _, kc, cpt, pairs, weights, rolled = spec
        U = 2 * cpt
        L = [len(steps[0]), len(steps[1])]
        LB = L[0] + L[1]
        raw, whi, wlo = self.raw, self.whi, self.wlo
        landed = [self.sig("weights_landed0"), self.sig("weights_landed1")]
        high, low = self.sig("weights_high"), self.sig("weights_low")
        summed, evac = self.sig("tile_summed"), self.sig("tile_steps")
        pieces = len(weights(0, 0, 0))

        def done_steps(i, j, k):
            return evac.at(i * LB + (L[0] if j else 0) + k)

        def wait_chunk(i, j, half):
            return i * U + j * cpt + half

        def loop(eng, n, body, first=0):
            if rolled and n > first + 1:
                with eng.Fori(first, n) as i:
                    body(i)
            else:
                for i in range(first, n):
                    body(i)

        with ExitStack() as ctx:
            stage = prepare(ctx) if prepare is not None else None
            block = ctx.enter_context(self.block())

            @block.sync
            def _(sp):
                if stage is not None:
                    stage.on_sp(sp)

                def load(i, q):
                    sp.wait_ge(low.sem, low.at(i * U + (q - 1)))
                    self.load_chunk(sp, spec, landed, i, q // cpt, q % cpt)

                def body(i):
                    for q in range(2, U + 2):
                        load(i + q // U, q % U)

                if pairs > 1:
                    loop(sp, pairs - 1, body)
                for q in range(2, U):
                    load(pairs - 1, q)
                if after_this is not None:
                    for q in range(2):
                        sp.wait_ge(low.sem, low.at(pairs * U - 1 + q))
                        self.load_chunk(sp, after_this, landed, 0, q // after_this[2], q % after_this[2])

            def split_chunk(eng, who, slot, k_tiles, weights_here, slot_free, nth):
                a = raw[:, slot, 0:k_tiles, :]
                h, lw = whi[:, slot, 0:k_tiles, :], wlo[:, slot, 0:k_tiles, :]
                if who == "act":
                    eng.wait_ge(landed[slot].sem, weights_here)
                    eng.wait_ge(summed.sem, slot_free)
                    nc.scalar.activation(h, a, ACT.Copy).then_inc(high.sem, 1)
                else:
                    eng.wait_ge(high.sem, nth)
                    nc.vector.tensor_tensor(lw, a, h.bitcast(F32), ALU.subtract).then_inc(low.sem, 1)

            def split(eng, who, i, j, first=0):
                for half in range(first, cpt):
                    c = wait_chunk(i, j, half)
                    slot = (j * cpt + half) % 2
                    nth = i * cpt + ((j * cpt + half) // 2 + 1)
                    split_chunk(eng, who, slot, kc, landed[slot].at(nth * 16 * pieces), summed.at(c - 1), high.at(c + 1))

            def split_next(eng, who):
                if after_this is not None:
                    its_pieces = len(after_this[4](0, 0, 0))
                    split_chunk(eng, who, 0, after_this[1], landed[0].at((pairs * cpt * pieces + its_pieces) * 16),
                                summed.at(pairs * U - 1), high.at(pairs * U + 1))

            def after(eng, who, i, j):
                for k, (engine, step) in enumerate(steps[j]):
                    if engine != who:
                        continue
                    if k == 0:
                        eng.wait_ge(summed.sem, summed.at(i * U + (j + 1) * cpt))
                    eng.wait_ge(evac.sem, done_steps(i, j, k))
                    step(i, self.ps[j][:, :]).then_inc(evac.sem, 1)

            def splitter(eng, who):
                if stage is not None:
                    (stage.on_act if who == "act" else stage.on_dve)(eng)
                beside = side if who == "dve" and side is not None else (lambda eng, n: None)
                ready = 1 if self.planned > 1 else 0

                def body(i):
                    split(eng, who, i + 1, 0)
                    after(eng, who, i, 0)
                    beside(eng, i * 2)
                    split(eng, who, i + 1, 1)
                    after(eng, who, i, 1)
                    beside(eng, i * 2 + 1)

                def halves_body(i):
                    split(eng, who, i, 1)
                    after(eng, who, i, 0)
                    split(eng, who, i + 1, 0)
                    after(eng, who, i, 1)

                split(eng, who, 0, 0, ready)
                if cpt == 1:
                    split(eng, who, 0, 1)
                if pairs > 1:
                    loop(eng, pairs - 1, body if cpt == 1 else halves_body)
                if cpt == 2:
                    split(eng, who, pairs - 1, 1)
                after(eng, who, pairs - 1, 0)
                beside(eng, 2 * pairs - 2)
                split_next(eng, who)
                after(eng, who, pairs - 1, 1)
                beside(eng, 2 * pairs - 1)

            if any(who == "pool" for step in steps for who, _ in step):
                @block.gpsimd
                def _(pool):
                    def body(i):
                        for j in range(2):
                            after(pool, "pool", i, j)
                    if on_pool is not None:
                        on_pool(pool)
                    loop(pool, pairs, body)
                    pool.wait_ge(evac.sem, evac.at(pairs * LB))
            elif on_pool is not None:
                @block.gpsimd
                def _(pool):
                    on_pool(pool)

            @block.scalar
            def _(act):
                if spread is not None:
                    self.spread_bias(act, *spread)
                splitter(act, "act")

            @block.vector
            def _(dve):
                splitter(dve, "dve")

            @block.tensor
            def _(pe):
                def body(i, first_pair=False):
                    for j in range(2):
                        pe.wait_ge(evac.sem, done_steps(i, j, 1 - LB))
                        for half in range(cpt):
                            slot = (j * cpt + half) % 2
                            pe.wait_ge(low.sem, low.at(wait_chunk(i, j, half) + 1))
                            for k in range(kc):
                                kt = half * kc + k
                                if first_pair and j == 0:
                                    stage.wait(pe, kt)
                                first, last = kt == 0, kt == cpt * kc - 1
                                out = self.ps[j][:, :]
                                nc.tensor.matmul(out, wlo[:, slot, k, :], x_hi(kt), start=first, stop=False)
                                nc.tensor.matmul(out, whi[:, slot, k, :], x_lo(kt), start=False, stop=False)
                                ins = nc.tensor.matmul(out, whi[:, slot, k, :], x_hi(kt), start=False, stop=last)
                            ins.then_inc(summed.sem, 1)

                if stage is not None:
                    stage.on_pe(pe)
                    body(0, True)
                loop(pe, pairs, body, 0 if stage is None else 1)
        if stage is not None:
            stage.done()
        for s in landed:
            s.advance(pairs * cpt * 16 * pieces)
        for s in (high, low, summed):
            s.advance(pairs * U)
        evac.advance(pairs * LB)

    def weight_plan(self):
        d = self.d
        ew, ow, aw, bw = d["e_w_in"][0], d["o_w_in"][0], d["a_w_qkv_2"][0], d["b_w_in_2"][0]
        plain = lambda name, w, first, rolled=True: (name, 8, 1, 4, self.columns(w, 8, first, P, 256), rolled)
        key = lambda c: [(c, 64), (c, 64)]
        plan = [
            plain("e_u", ew, 5128), plain("e_v", ew, 2048), plain("e_zb", ew, 6152),
            ("e_qk", 8, 1, 8, self.columns(ew, 8, 0, P, 256), True),
            ("e_gates", 8, 1, 1, self.columns(ew, 8, 5120, 4, 8), False),
            plain("e_o", ew, 3072), plain("e_za", ew, 4096),
            ("e_out", 8, 2, 4, self.columns(d["e_w_out"][0], 8, 0, P, 256), True),
            ("o_ckv_qi", 8, 1, 2, self.columns(ow, 8, 1024, P, 256), False),
            ("o_ki_wi", 8, 1, 1, self.listed(ow, 8, [key(1536), [(1600, 64), (1664, 64)]]), False),
            plain("o_q", ow, 0, False),
            ("o_uk", 2, 1, 4, self.columns(d["o_w_uk"][0], 2, 0, P, 256), True),
            ("o_uv", 2, 1, 4, self.columns(d["o_w_uv"][0], 2, 0, P, 256), True),
            plain("o_z", ow, 1604, False), plain("o_out", d["o_w_out"][0], 0),
            plain("a_q", aw, 0),
            ("a_kv", 8, 1, 2, self.listed(aw, 8, [key(1024), key(1088), [(1152, 64), (1216, 64)],
                                                  [(1152, 64), (1216, 64)]]), False),
            plain("a_out", d["a_w_o_2"][0], 0)]
        ffn = lambda n: [
            (f"ff_gu{n}", 8, 1, DFF // P, self.columns(d["ffn_w_gu_2"][n], 8, 0, DFF, P), True),
            (f"ff_down{n}", 11, 2, 4, self.columns(d["ffn_w_down_2"][n], 11, 0, P, 256), True)]
        kv = lambda n: 1024 + P * n
        tiles = [key(kv(n) + 64 * h) for n in (0, 1, 2, 4) for h in range(2)]
        tiles += [[(kv(n), 64), (kv(n) + 64, 64)] for n in (3, 5)] + [[(1712, 64), (1776, 64)]] * 2
        return (plan + ffn(0) + [plain("b_q", bw, 0), ("b_rest", 8, 1, 6, self.listed(bw, 8, tiles), False),
                                 plain("b_out", d["b_w_o_2"][0], 0)] + ffn(1))

    def load_chunk(self, sp, spec, landed, i, j, half):
        _, kc, cpt, _, weights, _ = spec
        slot = (j * cpt + half) % 2
        for c0, n, ap in weights(i, j, half):
            sp.dma_start(self.raw[:, slot, 0:kc, c0:c0 + n], ap).then_inc(landed[slot].sem, 16)

    def load_first(self, sp, spec, landed):
        for q in range(2):
            self.load_chunk(sp, spec, landed, 0, q // spec[2], q % spec[2])

    def columns(self, w, kc, first, stride, pair_stride):
        def of(i, j, half):
            src = w[half * kc * P:(half + 1) * kc * P, :]
            return [(0, P, src[:, rows(i * pair_stride + (first + j * stride), P)].rearrange("(k p) c -> p k c", p=P))]
        return of

    def listed(self, w, kc, tiles):
        def of(i, j, half):
            out, at = [], 0
            for c, n in tiles[2 * i + j]:
                out.append((at, n, w[half * kc * P:(half + 1) * kc * P, c:c + n].rearrange("(k p) c -> p k c", p=P)))
                at += n
            return out
        return of

    def keep(self, dst, engine="act"):
        nc = self.nc

        def step(j):
            if engine == "act":
                return [("act", lambda i, ps: nc.scalar.activation(dst(i, j), ps, ACT.Copy))]
            return [("dve", lambda i, ps: nc.vector.tensor_copy(dst(i, j), ps))]
        return [step(0), step(1)]

    def add_to_residual(self, name, x_hi, x_lo, bias=None, prepare=None, spread=None):
        nc, hT, sq = self.nc, self.hT, self.xtmp
        cleared = self.sig("squares_cleared")

        def step(j):
            tile = lambda i: flat(hT[:, rows(i * 2 + j), :])
            if bias is None:
                add = lambda i, ps: nc.vector.tensor_tensor(tile(i), ps, tile(i), ALU.add)
            else:
                add = lambda i, ps: nc.vector.scalar_tensor_tensor(tile(i), ps, bias[:, rows(i * 2 + j)], tile(i),
                                                                   ALU.add, ALU.add)
            return [("dve", add),
                    ("act", lambda i, ps: nc.scalar.activation(sq[:, j, :], tile(i), ACT.Square)),
                    ("pool", lambda i, ps: nc.gpsimd.tensor_tensor(self.squares[:, :], self.squares[:, :], sq[:, j, :],
                                                                   ALU.add))]

        def clear(pool):
            nc.gpsimd.memset(self.squares[:, :], 0.0).then_inc(cleared.sem, 1)
            pool.wait_ge(cleared.sem, cleared.at(1))
            cleared.advance(1)
        self.dense(name, x_hi, x_lo, [step(0), step(1)], prepare, spread, clear)

    def norm_stream(self, layer, loads=None, wait_loads=False):
        gain, tmp = self.gains[:, layer, :], self.xtmp
        return lambda c: self.norm(c, MT, lambda m: self.hT[:, m, :], lambda m: gain[:, m:m + 1],
                                   lambda m: tmp[:, m % 2, :], lambda m: self.xs_hi[:, m, :],
                                   lambda m: self.xs_lo[:, m, :], None if layer == 0 else self.squares, loads, wait_loads)

    def setup(self):
        nc, d, ctx = self.nc, self.d, self.ctx
        self.hT = self.sb(ctx, "hT", [P, MT, 512])
        self.ident = self.sb(ctx, "ident", [P, P])
        self.ones = self.sb(ctx, "ones", [P, P])
        self.raw = self.sb(ctx, "raw", [P, 2, 11, P])
        self.whi = self.sb(ctx, "whi", [P, 2, 11, P], F32R)
        self.wlo = self.sb(ctx, "wlo", [P, 2, 11, P], F32R)
        self.gains = self.sb(ctx, "gains", [P, 7, MT])
        self.xs = self.sb(ctx, "xs", [P, 2, MT, 512], F32R)
        self.xs_hi, self.xs_lo = self.xs[:, 0], self.xs[:, 1]
        self.xtmp = self.sb(ctx, "x_tmp", [P, 2, 512])
        self.squares = self.sb(ctx, "squares", [P, 512])

        for n in CREDITED:
            self.sig(n)
        started = self.ctx.enter_context(nc.semaphore("started"))
        with self.block() as block:
            @block.sync
            def _(sp):
                self.load_first(sp, self.plan[0], [self.sig("weights_landed0"), self.sig("weights_landed1")])

            @block.gpsimd
            def _(pool):
                for n in CREDITED:
                    pool.sem_inc(self.signals[n].sem, CREDIT)
                nc.gpsimd.memset(self.ones[:, :], 1.0).then_inc(started, 1)
                pool.wait_ge(started, 1)

        gain = lambda ap: ap.rearrange("(m p) -> p m", p=P)
        with ExitStack() as c:
            xin = self.sb(c, "xin", [P, QT, DM])
            tab = self.sb(c, "tab", [33, 2, NH])
            hot = self.sb(c, "hot", [33, 3, BIAS_L])
            tables = [d["rel_bias"], d["rel_table_2"]]
            self.start_load("bias_inputs", [(tab[0:32, i, :], tables[i]) for i in range(2)]
                            + [(tab[32:33, i, :], d["c_one"]) for i in range(2)]
                            + [(hot[:, :, :], d["c_hot"].rearrange("a b e -> b a e"))])
            norms = [d["e_norm"][0], d["o_norm"][0], *(d[n][i] for n in ("attn_norm_2", "ffn_norm_2") for i in range(2)), d["final_norm_2"]]
            self.load([(self.ident[:, :], d["c_ident"]), (xin[:, :, :], d["x"][0].rearrange("(t p) c -> p t c", p=P))])
            self.start_load("norm_gains", [(self.gains[:, i, :], gain(norms[i])) for i in range(7)])
            self.turn(MT, lambda m, t: xin[:, t, m * P:(m + 1) * P],
                      lambda m: self.hT[:, m, :].rearrange("p (t c) -> p t c", t=4))
            self.bias_tables(c, tab, hot)
            self.arrived("norm_gains")

    def even(self):
        nc, d = self.nc, self.d
        hi, lo = self.xs_hi, self.xs_lo
        xh, xl = (lambda k: hi[:, k, :]), (lambda k: lo[:, k, :])
        with ExitStack() as c:
            yb = self.sb(c, "yb", [P, MT, 512])
            ha = self.sb(c, "ha", [P, MT, 512])
            tmp = self.sb(c, "even_tmp", [P, 3, 512])
            small = self.sb(c, "even_small", [P, 96])
            conv, ghead, spool = small[:, 0:64], small[:, 64:72], small[:, 72:80]
            bif = small[0:4, 80:82]
            gain = lambda ap: ap.rearrange("(m p) -> p m", p=P)
            with ExitStack() as c2:
                u = self.sb(c2, "u", [P, MT, 512])
                pooled = self.sb(c2, "pooled", [P, MT, 512])
                wp = self.sb(c2, "wp", [P, 4, 2, 256])
                cnt = self.sb(c2, "cnt", [P, 4, 512])
                win = self.sb(c2, "win", [P, 2, 2, 512])
                first_norm = self.norm_stream(0, ("even_loads", [
                    (cnt[:, :, :], d["c_pool"]), (spool, gain(d["e_s_pool"][0])),
                    *((wp[:, g], d["e_w_pool"][0, g].rearrange("(k p) c -> p k c", p=P)) for g in range(4)),
                    *((conv.rearrange("p (m j) -> p m j", j=4)[:, :, j], gain(d["e_conv"][0, j])) for j in range(4)),
                    (ghead, gain(d["e_g_head"][0].rearrange("a b -> (a b)"))),
                    (bif, d["e_b_if"][0].rearrange("(k h) -> h k", h=4))]))

                self.dense("e_u", xh, xl, self.keep(lambda i, j: flat(u[:, rows(i * 2 + j), :])), first_norm)
                self.arrived("even_loads")
                self.dense("e_v", xh, xl, self.keep(lambda i, j: flat(ha[:, rows(i * 2 + j), :])), spread=(0, (0, 8)),
                           on_pool=lambda pool: self.pool(pool, u, win, cnt, pooled))
                self.mix_pooled(wp, pooled, yb)
            gate = lambda j: [
                ("act", lambda i, ps: nc.scalar.activation(tmp[:, j, :], ps, ACT.Silu)),
                ("dve", lambda i, ps: nc.vector.scalar_tensor_tensor(
                    flat(yb[:, rows(i * 2 + j), :]), flat(yb[:, rows(i * 2 + j), :]), spool[:, rows(i * 2 + j)],
                    tmp[:, j, :], ALU.mult, ALU.mult))]
            self.dense("e_zb", xh, xl, [gate(0), gate(1)], spread=(0, (8, 8)))

            with ExitStack() as c2:
                vt = self.sb(c2, "vt", [P, QT, DM])
                self.turn(MT, lambda m, t: ha[:, m, t * P:(t + 1) * P], lambda m: vt[:, :, m * P:(m + 1) * P])

                qk = self.sb(c2, "qk", [P, 16, 512])
                acol = self.sb(c2, "acol", [P, QT, 4])
                with ExitStack() as c3:
                    pad = self.sb(c3, "pad", [P, 2, 516])
                    self.clear(pad[:, :, 0:4])

                    def conv_steps(j):
                        wt = lambda i, t: conv[:, rows(i * 8 + (4 * j + t))]

                        def tap(t):
                            return ("dve", lambda i, ps: nc.vector.scalar_tensor_tensor(
                                tmp[:, j, :], pad[:, j, 1 + t:513 + t], wt(i, t), tmp[:, j, :], ALU.mult, ALU.add))
                        return [("act", lambda i, ps: nc.scalar.activation(pad[:, j, 4:516], ps, ACT.Copy)),
                                ("act", lambda i, ps: nc.scalar.activation(tmp[:, j, :], pad[:, j, 4:516], ACT.Copy,
                                                                           scale=wt(i, 3))),
                                tap(0), tap(1), tap(2),
                                ("act", lambda i, ps: nc.scalar.activation(flat(qk[:, rows(i * 2 + j), :]),
                                                                           tmp[:, j, :], ACT.Silu))]
                    self.dense("e_qk", xh, xl, [conv_steps(0), conv_steps(1)], spread=(1, (0, 8)))

                with ExitStack() as c3:
                    gi = self.sb(c3, "gates", [4, 2, 512])
                    gk = [[("act", lambda i, ps, j=j: nc.scalar.activation(gi[:, j, :], ps[0:4, :], ACT.Identity,
                                                                           bias=bif[:, j:j + 1]))] for j in range(2)]
                    self.dense("e_gates", xh, xl, gk)
                    self.stabilize(c3, gi, acol)
                self.recall(c2, qk, vt, acol, ha)

            gate_o = lambda j: [
                ("act", lambda i, ps: nc.scalar.activation(tmp[:, j, :], ps, ACT.Sigmoid)),
                ("dve", lambda i, ps: nc.vector.tensor_tensor(flat(ha[:, rows(i * 2 + j), :]), tmp[:, j, :],
                                                              flat(ha[:, rows(i * 2 + j), :]), ALU.mult))]
            self.dense("e_o", xh, xl, [gate_o(0), gate_o(1)], spread=(1, (8, 8)))
            with ExitStack() as c2:
                member, spread = self.sb(c2, "member4", [P, MT, 4]), self.sb(c2, "spread4", [4, MT, P])
                self.load([(member[:, :, :], d["c_member4"]), (spread[:, :, :], d["c_spread4"])])
                self.norm_heads(ha, 4, 256, member, spread, lambda m: ghead[:, m:m + 1])
            gate_z = lambda j: [
                ("act", lambda i, ps: nc.scalar.activation(tmp[:, j, :], ps, ACT.Silu)),
                ("dve", lambda i, ps: nc.vector.tensor_tensor(flat(ha[:, rows(i * 2 + j), :]), tmp[:, j, :],
                                                              flat(ha[:, rows(i * 2 + j), :]), ALU.mult))]
            self.dense("e_za", xh, xl, [gate_z(0), gate_z(1)], spread=(2, (0, 8)))

            y_hi, y_lo = self.sb(c, "y_hi", [P, 16, 512], F32R), self.sb(c, "y_lo", [P, 16, 512], F32R)
            split = self.split_tiles(16, lambda m: (ha if m < 8 else yb)[:, m % 8, :], lambda m: y_hi[:, m, :],
                             lambda m: y_lo[:, m, :])
            self.add_to_residual("e_out", lambda k: y_hi[:, k, :], lambda k: y_lo[:, k, :], prepare=split, spread=(2, (8, 8)))

    def clear(self, ap):
        nc, cleared = self.nc, self.sig("cleared")
        with self.block() as block:
            @block.vector
            def _(dve):
                nc.vector.memset(ap, 0.0).then_inc(cleared.sem, 1)

    def split_tiles(self, n, src, hi, lo):
        nc, high, low = self.nc, self.sig("norm_high"), self.sig("norm_low")

        def on_act(act):
            for m in range(n):
                nc.scalar.activation(hi(m), src(m), ACT.Copy).then_inc(high.sem, 1)

        def on_dve(dve):
            for m in range(n):
                dve.wait_ge(high.sem, high.at(m + 1))
                nc.vector.tensor_tensor(lo(m), src(m), hi(m).bitcast(F32), ALU.subtract).then_inc(low.sem, 1)

        def wait(pe, m):
            pe.wait_ge(low.sem, low.at(m + 1))

        def done():
            high.advance(n)
            low.advance(n)
        nothing = lambda eng: None
        return lambda c: Stage(nothing, on_act, nothing, on_dve, wait, done)

    def pool(self, pool, u, win, cnt, pooled):
        nc, step = self.nc, self.sig("pool_step")
        n = 0

        def link(ins):
            nonlocal n
            n += 1
            ins.then_inc(step.sem, 1)
            pool.wait_ge(step.sem, n)

        for g in range(4):
            src = u[:, 2 * g:2 * g + 2, :]
            cur = src
            for b in range(g + 1):
                w = 1 << b
                nxt = win[:, b % 2]
                link(nc.gpsimd.tensor_copy(nxt[:, :, 0:w], cur[:, :, 0:w]))
                link(nc.gpsimd.tensor_tensor(nxt[:, :, w:512], cur[:, :, w:512], cur[:, :, 0:512 - w], ALU.add))
                cur = nxt
            for t in range(2):
                link(nc.gpsimd.tensor_tensor(pooled[:, 2 * g + t, :], cur[:, t, :], cnt[:, g, :], ALU.mult))
            link(nc.gpsimd.tensor_tensor(pooled[:, 2 * g:2 * g + 2, :], pooled[:, 2 * g:2 * g + 2, :], src, ALU.subtract))

    def mix_pooled(self, wp, pooled, yb):
        nc, mixed, kept = self.nc, self.sig("pool_mixed"), self.sig("pool_kept")
        with self.block() as block:
            @block.tensor
            def _(pe):
                for m in range(MT):
                    g, t = m // 2, m % 2
                    if m >= 2:
                        pe.wait_ge(kept.sem, m - 1)
                    for k in range(2):
                        ins = nc.tensor.matmul(self.ps[m % 2][:, :], wp[:, g, k, t * P:(t + 1) * P],
                                               pooled[:, 2 * g + k, :], start=(k == 0), stop=(k == 1))
                    ins.then_inc(mixed.sem, 1)

            @block.scalar
            def _(act):
                for m in range(MT):
                    act.wait_ge(mixed.sem, m + 1)
                    nc.scalar.activation(yb[:, m, :], self.ps[m % 2][:, :], ACT.Copy).then_inc(kept.sem, 1)

    def stabilize(self, c, gi, acol):
        nc, d = self.nc, self.d
        row, colsum = self.sig("gate_step"), self.sig("gate_turned")
        stored = self.sig("gate_rows_stored")
        rowsT = self.sb(c, "gate_rows", [4, 8, 512])
        scratch = d["s_rows"]
        i_pre, f_pre = gi[:, 0, :], gi[:, 1, :]
        t0, t1, F, a, M, m, one, em = [rowsT[:, k, :] for k in range(8)]
        with self.block() as block:
            @block.scalar
            def _(act):
                nc.scalar.activation(t0, f_pre, ACT.Abs).then_inc(row.sem, 1)
                act.wait_ge(row.sem, 1)
                nc.scalar.activation(t0, t0, ACT.Exp, scale=-1.0).then_inc(row.sem, 1)
                act.wait_ge(row.sem, 2)
                nc.scalar.activation(t0, t0, ACT.Ln, bias=1.0).then_inc(row.sem, 1)
                act.wait_ge(row.sem, 11)
                nc.scalar.activation(em, m, ACT.Exp, scale=-1.0).then_inc(row.sem, 1)

            @block.vector
            def _(dve):
                dve.wait_ge(row.sem, 3)
                nc.vector.memset(one, 1.0).then_inc(row.sem, 1)
                dve.wait_ge(row.sem, 4)
                nc.vector.tensor_scalar(t1, f_pre, 0.0, None, ALU.min).then_inc(row.sem, 1)
                dve.wait_ge(row.sem, 5)
                nc.vector.tensor_tensor(t1, t1, t0, ALU.subtract).then_inc(row.sem, 1)
                dve.wait_ge(row.sem, 6)
                nc.vector.tensor_tensor_scan(F, one, t1, 0.0, ALU.mult, ALU.add).then_inc(row.sem, 1)
                dve.wait_ge(row.sem, 7)
                nc.vector.tensor_tensor(a, i_pre, F, ALU.subtract).then_inc(row.sem, 1)
                dve.wait_ge(row.sem, 8)
                nc.vector.memset(t0, 0.0).then_inc(row.sem, 1)
                dve.wait_ge(row.sem, 9)
                nc.vector.tensor_tensor_scan(M, a, t0, 0.0, ALU.max, ALU.add).then_inc(row.sem, 1)
                dve.wait_ge(row.sem, 10)
                nc.vector.tensor_tensor(m, F, M, ALU.add).then_inc(row.sem, 1)
                dve.wait_ge(colsum.sem, 1)
                nc.vector.tensor_copy(acol[:, :, :], self.ps[0][:, 0:16].rearrange("p (t h) -> p t h", t=4))

            @block.tensor
            def _(pe):
                pe.wait_ge(row.sem, 8)
                for t in range(4):
                    ins = nc.tensor.transpose(self.ps[0][:, 4 * t:4 * t + 4], a[:, t * P:(t + 1) * P], self.ident[0:4, 0:4])
                ins.then_inc(colsum.sem, 1)

            @block.sync
            def _(sp):
                sp.wait_ge(row.sem, 12)
                sp.dma_start(scratch[0], M).then_inc(stored.sem, 16)
                sp.dma_start(scratch[1], em).then_inc(stored.sem, 16)
                sp.wait_ge(stored.sem, 32)

    def recall(self, c, qk, vt, acol, ha):
        nc, scratch = self.nc, self.d["s_rows"]
        spread, floors = self.sig("gate_rows_spread"), self.sig("gate_floors_spread")
        kh = self.sb(c, "kh", [P, 2, 512])
        vh = self.sb(c, "vh", [P, QT, 256])
        W = self.sb(c, "Wst", [P, QT, 512])
        Mb = self.sb(c, "Mb", [P, 2, 512])
        D = self.sb(c, "Dst", [P, 2, 512])
        den = self.sb(c, "den", [P, 2, 512])
        tri = self.sb(c, "tri", [P, P])
        self.load([(tri[:, :], self.d["c_tri"])])
        k_staged, v_staged = self.sig("mem_k_staged"), self.sig("mem_v_staged")
        scores, gaps, decays = self.sig("mem_scores"), self.sig("mem_gaps"), self.sig("mem_decays")
        weighed, masked = self.sig("mem_weighed"), self.sig("mem_masked")
        read, tail = self.sig("mem_read"), self.sig("mem_tail")
        with self.block() as block:
            @block.sync
            def _(sp):
                with sp.Fori(0, 4) as h:
                    sp.wait_ge(gaps.sem, h * 4 + CREDIT)
                    sp.dma_start(Mb[:, 0, :], scratch[0, rows(h), :].broadcast_to([P, 512])).then_inc(spread.sem, 16)
                    sp.wait_ge(tail.sem, h * 5 + CREDIT)
                    sp.dma_start(Mb[:, 1, :], scratch[1, rows(h), :].broadcast_to([P, 512])).then_inc(floors.sem, 16)

            @block.scalar
            def _(act):
                with act.Fori(0, 4) as h:
                    act.wait_ge(scores.sem, h * 4 + CREDIT)
                    nc.scalar.activation(kh[:, :, :], qk[:, rows(h * 2 + 8, 2), :], ACT.Copy,
                                         scale=256 ** -0.5).then_inc(k_staged.sem, 1)
                    act.wait_ge(read.sem, h * 3 + CREDIT)
                    nc.scalar.activation(vh[:, :, :], vt[:, :, rows(h * 256, 256)], ACT.Copy).then_inc(v_staged.sem, 1)
                    for s in range(QT):
                        n = 512 - s * P
                        act.wait_ge(gaps.sem, h * 4 + (s + 1 + CREDIT))
                        nc.scalar.activation(D[:, s % 2, 0:n], D[:, s % 2, 0:n], ACT.Exp, scale=-1.0).then_inc(decays.sem, 1)

            @block.vector
            def _(dve):
                with dve.Fori(0, 4) as h:
                    dve.wait_ge(spread.sem, h * 16 + (16 + CREDIT))
                    for s in range(QT):
                        n, t = 512 - s * P, s * P
                        dve.wait_ge(weighed.sem, h * 4 + (s - 1 + CREDIT))
                        nc.vector.tensor_scalar(D[:, s % 2, 0:n], Mb[:, 0, t:512], acol[:, s, rows(h)], 0.0, ALU.subtract,
                                                ALU.max).then_inc(gaps.sem, 1)
                        dve.wait_ge(decays.sem, h * 4 + (s + 1 + CREDIT))
                        dve.wait_ge(scores.sem, h * 4 + (s + 1 + CREDIT))
                        nc.vector.tensor_tensor(W[:, s, 0:n], D[:, s % 2, 0:n], self.ps[s % 2][:, 0:n],
                                                ALU.mult).then_inc(weighed.sem, 1)
                    dve.wait_ge(floors.sem, h * 16 + (16 + CREDIT))
                    dve.wait_ge(read.sem, h * 3 + (1 + CREDIT))
                    nc.vector.scalar_tensor_tensor(den[:, 0, :], self.ps[4][:, :], -1.0, Mb[:, 1, :], ALU.mult,
                                                   ALU.max).then_inc(tail.sem, 1)
                    dve.wait_ge(tail.sem, h * 5 + (1 + CREDIT))
                    nc.vector.tensor_tensor(den[:, 0, :], self.ps[4][:, :], den[:, 0, :], ALU.max).then_inc(tail.sem, 1)
                    dve.wait_ge(tail.sem, h * 5 + (2 + CREDIT))
                    nc.vector.reciprocal(den[:, 1, :], den[:, 0, :]).then_inc(tail.sem, 1)
                    dve.wait_ge(tail.sem, h * 5 + (3 + CREDIT))
                    for v in range(2):
                        dve.wait_ge(read.sem, h * 3 + (2 + v + CREDIT))
                        nc.vector.tensor_tensor(flat(ha[:, rows(h * 2 + v), :]), self.ps[2 + v][:, :], den[:, 1, :],
                                                ALU.mult).then_inc(tail.sem, 1)

            @block.gpsimd
            def _(pool):
                with pool.Fori(0, 4) as h:
                    for s in range(QT):
                        pool.wait_ge(weighed.sem, h * 4 + (s + 1 + CREDIT))
                        nc.gpsimd.tensor_tensor(W[:, s, 0:P], W[:, s, 0:P], tri[:, :], ALU.mult).then_inc(masked.sem, 1)

            @block.tensor
            def _(pe):
                with pe.Fori(0, 4) as h:
                    pe.wait_ge(k_staged.sem, h + (1 + CREDIT))
                    for s in range(QT):
                        n, t = 512 - s * P, s * P
                        pe.wait_ge(weighed.sem, h * 4 + (s - 1 + CREDIT))
                        for k in range(2):
                            ins = nc.tensor.matmul(self.ps[s % 2][:, 0:n], kh[:, k, s * P:(s + 1) * P],
                                                   flat(qk[:, rows(h * 2 + k), t:512]), start=(k == 0), stop=(k == 1))
                        ins.then_inc(scores.sem, 1)
                    pe.wait_ge(masked.sem, h * 4 + (4 + CREDIT))
                    pe.wait_ge(v_staged.sem, h + (1 + CREDIT))
                    pe.wait_ge(tail.sem, h * 5 + CREDIT)
                    for o, lhs in ((4, None), (2, 0), (3, 1)):
                        for s in range(QT):
                            n, t = 512 - s * P, s * P
                            st = self.ones[:, :] if lhs is None else vh[:, s, lhs * P:(lhs + 1) * P]
                            ins = nc.tensor.matmul(self.ps[o][:, t:512], st, W[:, s, 0:n], start=(s == 0),
                                                   stop=(s == QT - 1))
                        ins.then_inc(read.sem, 1)

    def bias_tables(self, c, tab, hot):
        nc, d = self.nc, self.d
        made, kept, stored = self.sig("bias_made"), self.sig("bias_kept"), self.sig("bias_spread")
        vec = self.sb(c, "vec", [NH, 3, BIAS_L])
        with self.block() as block:
            @block.tensor
            def _(pe):
                pe.wait_ge(self.sig("bias_inputs").sem, self.sig("bias_inputs").at(0))
                for a in range(3):
                    w = tab[:, min(a, 1), :]
                    nc.tensor.matmul(self.banks[0:NH, 2 * a, :], w, hot[:, a, 0:512], start=True, stop=True)
                    ins = nc.tensor.matmul(self.banks[0:NH, 2 * a + 1, 0:P], w, hot[:, a, 512:BIAS_L], start=True, stop=True)
                ins.then_inc(made.sem, 1)

            @block.scalar
            def _(act):
                act.wait_ge(made.sem, 1)
                for a in range(3):
                    nc.scalar.activation(vec[:, a, 0:512], self.banks[0:NH, 2 * a, :], ACT.Copy).then_inc(kept.sem, 1)
                    nc.scalar.activation(vec[:, a, 512:BIAS_L], self.banks[0:NH, 2 * a + 1, 0:P], ACT.Copy).then_inc(kept.sem, 1)
                act.wait_ge(kept.sem, 6)
                act.dma_start(d["s_bias"].rearrange("a h e -> h a e"), vec[:, :, :]).then_inc(stored.sem, 16)
                act.wait_ge(stored.sem, 16)

    def spread_bias(self, act, a, heads):
        first, n = heads
        src = bass.AP(tensor=self.d["s_bias"].tensor, offset=(a * NH + first) * BIAS_L, ap=[[BIAS_L, n], [0, P], [1, BIAS_L]])
        act.dma_start(self.d["s_skew"][a, first:first + n], src).then_inc(self.sig("bias_spread").sem, 16)

    def attention(self, q, k, v, keys, n_bias, table, out, grouped, add=False, times=None, mask=None, sink=None,
                  gate=None, bias_at=None):
        nc = self.nc
        LOOPS = NH // 4
        steps = [(half, t) for half in range(2) for t in (3, 1, 2, 0)]
        NS = len(steps)
        TURN, MIX, FINISH = 3, 4, 5
        sg = self.sig
        landed, staged = [sg("att_bias0"), sg("att_bias1")], sg("att_staged")
        scores, logits = sg("att_scores"), sg("att_logits")
        v_staged = sg("att_values_staged")
        peaks, shifts, probs, dens = sg("att_peaks"), sg("att_shifts"), sg("att_probs"), sg("att_dens")
        ready, turned, kept, mixed = sg("att_ready"), sg("att_turned"), sg("att_kept"), sg("att_mixed")
        outs = sg("att_outs")
        n_staged = 1 if grouped else 2
        n_logits = 3 if mask is not None else 2
        n_shifts = 2 if sink is not None else 1
        n_probs = 3 if sink is not None else 2
        n_dens = 1 + (sink is not None) + (gate is not None)
        bias = self.xs[:, :, :, :].bitcast(F32).rearrange("p a b c -> p (a b c)")[:, 0:4 * n_bias]
        bias = bias.rearrange("p (e x n) -> p e x n", e=2, x=2)
        with ExitStack() as c:
            n = self.stage_n
            self.stage_n += 1
            qs = self.sb(c, f"qs{n}", [P, 2, 512])
            if not grouped:
                ks = self.sb(c, f"ks{n}", [P, 2, 512])
                vs = self.sb(c, f"vs{n}", [P, QT, 2, 2, HD])
            prob = self.sb(c, f"prob{n}", [P, 2, 2 * 512 + 2 * 256])
            probs_of = [prob[:, 0, 0:1024], prob[:, 0, 1024:1536], prob[:, 1, 0:1024], prob[:, 1, 1024:1536]]
            probs_of = [ap.rearrange("p (x n) -> p x n", x=2) for ap in probs_of]
            pT = self.sb(c, f"pT{n}", [P, 1024 + 512])
            turned_of = [pT[:, 0:1024], pT[:, 1024:1536]]
            st = self.sb(c, f"stat{n}", [P, 4, 6, 2])
            S = [self.banks[:, 0:2, :], self.banks[:, 2, :].rearrange("p (x n) -> p x n", x=2)]
            T = [self.banks[:, 4:6, :].rearrange("p a b -> p (a b)"), self.banks[:, 6, :]]
            O = [self.banks[:, b, 0:2 * P] for b in (3, 7)]
            block = c.enter_context(self.block())

            def stat(s, k):
                return st[:, s % 4, k, :]

            def step(s):
                return steps[s % NS]

            def sel(i, s=0):
                i = i + (-1) if s < 0 else i
                return bass.ds(i, 2, step=4) if grouped else bass.ds(i * 2, 2)

            def pipeline(eng, body):
                for j in range(NS):
                    body(0, j, True, False)
                with eng.Fori(1, LOOPS) as i:
                    for j in range(NS):
                        body(i, j, False, False)
                for j in range(NS, NS + FINISH):
                    body(LOOPS - 1, j, False, True)

            @block.sync
            def _(sp):
                sp.wait_ge(sg("bias_spread").sem, 16 * (1 + 2 * 3))
                for i in range(LOOPS):
                    for half in range(2):
                        if i >= 1:
                            sp.wait_ge(logits.sem, logits.at((i * NS - NS + 4 * half + 4) * n_logits))
                        h = 2 * i + half if grouped else 4 * i + half
                        src = bass.AP(tensor=self.d["s_skew"].tensor, offset=(table * NH + h) * P * BIAS_L + 127 + 512 - n_bias,
                                      ap=[[BIAS_L - 1, P], [(8 if grouped else 2) * P * BIAS_L, 2], [1, n_bias]])
                        sp.dma_start(bias[:, half], src).then_inc(landed[half].sem, 16)

            @block.tensor
            def _(pe):
                def score(i, s):
                    half, t = step(s)
                    k0, nk, _ = keys(t)
                    if s == 0:
                        pe.wait_ge(staged.sem, staged.at(i * n_staged + n_staged))
                    pe.wait_ge(logits.sem, logits.at((i * NS + (s - 1)) * n_logits))
                    r = slice(64 * half, 64 * half + 64)
                    for x in range(2):
                        kx = k[r, x, k0:k0 + nk] if grouped else ks[r, x, k0:k0 + nk]
                        ins = nc.tensor.matmul(S[s % 2][:, x, 0:nk], qs[r, x, t * P:(t + 1) * P], kx, start=True, stop=True)
                    ins.then_inc(scores.sem, 1)

                def turn(i, s):
                    _, _, blocks = keys(step(s)[1])
                    pe.wait_ge(kept.sem, kept.at(i * NS + (s - 1)))
                    pe.wait_ge(ready.sem, ready.at((i * NS + (s + 1)) * 2))
                    for b, (_, r) in enumerate(blocks):
                        for x in range(2):
                            ins = nc.tensor.transpose(T[s % 2][0:r, (2 * b + x) * P:(2 * b + x + 1) * P],
                                                      probs_of[s % 4][:, x, b * P:b * P + r], self.ident[:, :])
                    ins.then_inc(turned.sem, 1)

                def mix(i, s):
                    half, t = step(s)
                    _, _, blocks = keys(t)
                    o = O[s % 2][64 * half:64 * half + 64, :]
                    if not grouped:
                        pe.wait_ge(v_staged.sem, v_staged.at((i if s >= 0 else i + (-1)) * 2 + (1 + half)))
                    pe.wait_ge(outs.sem, outs.at(i * NS + (s - 1)))
                    pe.wait_ge(kept.sem, kept.at(i * NS + (s + 1)))
                    last = len(blocks) - 1
                    for x in range(2):
                        for b, (kb, r) in enumerate(blocks):
                            vx = v(kb, r, x) if grouped else vs[0:r, kb, x, half, :]
                            ins = nc.tensor.matmul(o[:, x * P:(x + 1) * P], vx, turned_of[s % 2][0:r, (2 * b + x) * P:(2 * b + x + 1) * P],
                                                   start=(b == 0), stop=(b == last))
                    ins.then_inc(mixed.sem, 1)

                def body(i, j, first, last):
                    if not last:
                        score(i, j)
                    if (not first or j >= TURN) and j - TURN < NS:
                        turn(i, j - TURN)
                    if (not first or j >= MIX) and j - MIX < NS:
                        mix(i, j - MIX)

                pipeline(pe, body)

            @block.vector
            def _(dve):
                def logit(i, s):
                    half, t = step(s)
                    _, nk, _ = keys(t)
                    at = i * NS + s
                    pr = probs_of[s % 4][:, :, 0:nk]
                    b = bias[:, half, :, n_bias - nk:n_bias] if bias_at is None else bias[:, half, :, bias_at(t, nk)]
                    if t == steps[0][1]:
                        dve.wait_ge(landed[half].sem, landed[half].at(i * 16 + 16))
                    dve.wait_ge(turned.sem, turned.at(at + (-3)))
                    dve.wait_ge(scores.sem, scores.at(at + 1))
                    if mask is not None:
                        nc.vector.tensor_tensor(pr, S[s % 2][:, :, 0:nk], b, ALU.add).then_inc(logits.sem, 1)
                        dve.wait_ge(logits.sem, logits.at(at * 3 + 1))
                        src, b = pr, mask(t, nk)
                    else:
                        src = S[s % 2][:, :, 0:nk]
                    nc.vector.memset(stat(s, 1), 0.0)
                    for x in range(2):
                        nc.vector.tensor_tensor_reduce(out=pr[:, x, :], in0=src[:, x, :], in1=b[:, x, :], scale=1.0, scalar=CUT,
                                                       op0=ALU.add, op1=ALU.max,
                                                       accum_out=stat(s, 0)[:, x:x + 1]).then_inc(logits.sem, 1)
                    dve.wait_ge(logits.sem, logits.at((at + 1) * n_logits))
                    if sink is not None:
                        sk = sink[:, sel(i), half]
                        nc.vector.tensor_tensor(stat(s, 0), stat(s, 0), sk, ALU.max).then_inc(peaks.sem, 1)
                        dve.wait_ge(peaks.sem, peaks.at(at + 1))
                    nc.vector.tensor_scalar(stat(s, 1), stat(s, 0), -1.0, None, ALU.mult).then_inc(shifts.sem, 1)
                    if sink is not None:
                        dve.wait_ge(shifts.sem, shifts.at(at * 2 + 1))
                        nc.vector.tensor_tensor(stat(s, 3), sk, stat(s, 1), ALU.add).then_inc(shifts.sem, 1)

                def divide(i, s):
                    half, t = step(s)
                    _, nk, _ = keys(t)
                    at = i * NS + s
                    dve.wait_ge(probs.sem, probs.at((at + 1) * n_probs))
                    done = 0
                    if sink is not None:
                        nc.vector.tensor_tensor(stat(s, 2), stat(s, 2), stat(s, 4), ALU.add).then_inc(dens.sem, 1)
                        done += 1
                        dve.wait_ge(dens.sem, dens.at(at * n_dens + done))
                    nc.vector.reciprocal(stat(s, 5), stat(s, 2)).then_inc(dens.sem, 1)
                    done += 1
                    dve.wait_ge(dens.sem, dens.at(at * n_dens + done))
                    if gate is not None:
                        nc.vector.tensor_tensor(stat(s, 5), stat(s, 5), gate(sel(i, s), half, t),
                                                ALU.mult).then_inc(dens.sem, 1)
                        done += 1
                        dve.wait_ge(dens.sem, dens.at(at * n_dens + done))
                    for x in range(2):
                        pr = probs_of[s % 4][:, x, 0:nk]
                        nc.vector.tensor_scalar(pr, pr, st[:, s % 4, 5, x:x + 1], None, ALU.mult).then_inc(ready.sem, 1)

                def finish(i, s):
                    half, t = step(s)
                    r = slice(64 * half, 64 * half + 64)
                    o = out[r, sel(i, s), t * P:(t + 1) * P]
                    got = O[s % 2][r, :].rearrange("p (x q) -> p x q", x=2)
                    dve.wait_ge(mixed.sem, mixed.at(i * NS + (s + 1)))
                    if add:
                        nc.vector.tensor_tensor(o, got, o, ALU.add).then_inc(outs.sem, 1)
                    elif times is not None:
                        nc.vector.tensor_tensor(o, got, times[r, sel(i, s), t * P:(t + 1) * P], ALU.mult).then_inc(outs.sem, 1)
                    else:
                        nc.vector.tensor_copy(o, got).then_inc(outs.sem, 1)

                def body(i, j, first, last):
                    if not last:
                        logit(i, j)
                    if (not first or j >= 1) and j - 1 < NS:
                        divide(i, j - 1)
                    if not first or j >= FINISH:
                        finish(i, j - FINISH)

                pipeline(dve, body)

            @block.scalar
            def _(act):
                def exp(i, s):
                    _, nk, _ = keys(step(s)[1])
                    act.wait_ge(shifts.sem, shifts.at((i * NS + (s + 1)) * n_shifts))
                    for x in range(2):
                        pr = probs_of[s % 4][:, x, 0:nk]
                        nc.scalar.activation(pr, pr, ACT.Exp, bias=st[:, s % 4, 1, x:x + 1],
                                             accum_out=st[:, s % 4, 2, x:x + 1]).then_inc(probs.sem, 1)
                    if sink is not None:
                        nc.scalar.activation(stat(s, 4), stat(s, 3), ACT.Exp).then_inc(probs.sem, 1)

                def keep(i, s):
                    _, _, blocks = keys(step(s)[1])
                    r, w = blocks[0][1], 2 * P * len(blocks)
                    act.wait_ge(mixed.sem, mixed.at(i * NS + (s - 1)))
                    act.wait_ge(turned.sem, turned.at(i * NS + (s + 1)))
                    nc.scalar.activation(turned_of[s % 2][0:r, 0:w], T[s % 2][0:r, 0:w], ACT.Copy).then_inc(kept.sem, 1)

                def stage_values(i, half):
                    act.wait_ge(mixed.sem, mixed.at(i * NS + (4 * half + 4 - NS)))
                    src = v[:, :, rows(i * 256, 256)].rearrange("p t (x e d) -> p t x e d", x=2, e=2)
                    nc.scalar.activation(vs[:, :, :, half, :], src[:, :, :, half, :], ACT.Copy).then_inc(v_staged.sem, 1)

                def body(i, j, first, last):
                    if j == 0:
                        act.wait_ge(scores.sem, scores.at(i * NS))
                        nc.scalar.activation(qs[:, :, :], q[:, sel(i), :], ACT.Copy, scale=HD ** -0.5).then_inc(staged.sem, 1)
                        if not grouped:
                            nc.scalar.activation(ks[:, :, :], k[:, sel(i), :], ACT.Copy).then_inc(staged.sem, 1)
                    if not last:
                        exp(i, j)
                    if (not first or j >= TURN) and j - TURN < NS:
                        keep(i, j - TURN)
                    if not grouped and j in (0, 4):
                        stage_values(i, j // 4)

                pipeline(act, body)
        total = LOOPS * NS
        staged.advance(n_staged * LOOPS)
        if not grouped:
            v_staged.advance(2 * LOOPS)
        for sgn in landed:
            sgn.advance(16 * LOOPS)
        for sgn, k in ((logits, n_logits), (peaks, 0 if sink is None else 1), (shifts, n_shifts), (probs, n_probs), (dens, n_dens),
                       (ready, 2), (scores, 1), (turned, 1), (kept, 1), (mixed, 1), (outs, 1)):
            sgn.advance(total * k)

    @staticmethod
    def causal(t):
        return 0, (t + 1) * P, [(b, P) for b in range(t + 1)]

    def odd(self):
        nc, d = self.nc, self.d
        hi, lo = self.xs_hi, self.xs_lo
        xh, xl = (lambda k: hi[:, k, :]), (lambda k: lo[:, k, :])
        with ExitStack() as c:
            oT = self.sb(c, "oT_o", [P, MT, 512])
            with ExitStack() as c2:
                qT = self.sb(c2, "qT", [P, MT, 512])
                kT = self.sb(c2, "kT", [P, MT, 512])
                vt = self.sb(c2, "vt2", [P, QT, DM])
                mask = self.sb(c2, "mask", [P, QT, 512])
                zT = self.sb(c2, "zT", [P, MT, 512])
                with ExitStack() as c3:
                    ckv = self.sb(c3, "ckv", [P, 2, 512])
                    small = self.sb(c3, "odd_small", [P, 4])
                    member, spread = self.sb(c3, "member", [P, MT, NH]), self.sb(c3, "spread", [NH, MT, P])
                    ch = self.sb(c3, "ckv_hi", [P, 2, 512], F32R)
                    cl = self.sb(c3, "ckv_lo", [P, 2, 512], F32R)
                    later = self.sb(c3, "idx_later", [P, P])
                    index = [None] + [self.sb(c3, f"idx_score{t}", [P, (t + 1) * P]) for t in range(1, QT)]
                    top = self.sb(c3, "idx_top", [P, QT, 8])
                    gq, gk, gkv = small[:, 0:1], small[:, 1:2], small[:, 2:4]
                    one = lambda ap: ap.rearrange("(p a) -> p a", a=1)
                    odd_norm = self.norm_stream(1, ("odd_loads", [
                        *((small[64 * s:64 * s + 64, k:k + 1], one(d[nm][0])) for s in range(2)
                          for k, nm in enumerate(("o_g_q", "o_g_k"))),
                        (gkv, d["o_g_kv"][0].rearrange("(m p) -> p m", p=P)), (member[:, :, :], d["c_member"]),
                        (spread[:, :, :], d["c_spread"]), (later[:, :], d["c_later"])]))

                    qi, ki, wi, wit = kT[:, 0:2, :], kT[:, 2, :], kT[:, 3, :], kT[:, 4, :].rearrange("p (t c) -> p t c", t=QT)
                    dsts = [ckv[:, 0, :], ckv[:, 1, :], qi[:, 0, :], qi[:, 1, :]]
                    self.dense("o_ckv_qi", xh, xl, self.keep(lambda i, j: dsts[2 * i + j]), odd_norm)
                    self.dense("o_ki_wi", xh, xl, self.keep(lambda i, j: (ki, wi)[j]))
                    self.turn(1, lambda m, t: wi[:, t * P:(t + 1) * P], lambda m: wit)
                    self.arrived("odd_loads")
                    self.index_scores(qi, ki, wit, later, index, mask)

                    self.dense("o_q", xh, xl, self.keep(lambda i, j: flat(qT[:, rows(i * 2 + j), :])),
                               side=self.cut_highest(index, top))
                    self.norm_heads(qT, NH, HD, member, spread, lambda m: gq)
                    latent_norm = lambda c: self.norm(
                        c, 2, lambda m: ckv[:, m, :], lambda m: gkv[:, m:m + 1], lambda m: self.xtmp[:, m % 2, :],
                        lambda m: ch[:, m, :], lambda m: cl[:, m, :])
                    self.dense("o_uk", lambda k: ch[:, k, :], lambda k: cl[:, k, :],
                               self.keep(lambda i, j: flat(kT[:, rows(i * 2 + j), :])), latent_norm)
                    self.norm_heads(kT, NH, HD, member, spread, lambda m: gk)
                    vF = oT
                    self.dense("o_uv", lambda k: ch[:, k, :],
                               lambda k: cl[:, k, :], self.keep(lambda i, j: flat(vF[:, rows(i * 2 + j), :])))
                    self.turn(MT, lambda m, t: vF[:, m, t * P:(t + 1) * P], lambda m: vt[:, :, m * P:(m + 1) * P])
                    silu = lambda j: [("act", lambda i, ps: nc.scalar.activation(flat(zT[:, rows(i * 2 + j), :]), ps, ACT.Silu))]
                    self.dense("o_z", xh, xl, [silu(0), silu(1)], side=self.cut_highest(index, top))
                    self.mask_rest(index, mask)
                self.attention(qT, kT, vt, self.causal, 512, 0, oT, False, times=zT,
                               mask=lambda t, nk: mask[:, t:t + 1, 0:nk].broadcast_to([P, 2, nk]))
            self.project_out(c, oT, "o_out")

    def index_scores(self, qi, ki, wit, later, index, mask):
        nc = self.nc
        dots, acts, acc = self.sig("idx_dots"), self.sig("idx_relu"), self.sig("idx_step")
        rl = self.xtmp
        todo = [(t, h) for t in range(1, QT) for h in range(4)]
        B = 4
        with self.block() as block:
            @block.tensor
            def _(pe):
                for n, (t, h) in enumerate(todo):
                    nk = (t + 1) * P
                    if n >= B:
                        pe.wait_ge(acts.sem, n - B + 1)
                    s = 64 * (h % 2)
                    nc.tensor.matmul(self.ps[n % B][:, 0:nk], qi[s:s + 64, h // 2, t * P:(t + 1) * P],
                                     ki[s:s + 64, 0:nk], start=True, stop=True).then_inc(dots.sem, 1)

            def head_done(n):
                return 1 + (n // 4) * 5 + n % 4 + 1

            @block.scalar
            def _(act):
                for n, (t, h) in enumerate(todo):
                    nk = (t + 1) * P
                    act.wait_ge(dots.sem, n + 1)
                    if n >= 2:
                        act.wait_ge(acc.sem, head_done(n - 2))
                    nc.scalar.activation(rl[:, n % 2, 0:nk], self.ps[n % B][:, 0:nk], ACT.Relu,
                                         scale=(64 ** -0.5) * (4 ** -0.5)).then_inc(acts.sem, 1)

            @block.vector
            def _(dve):
                done = 1
                nc.vector.memset(mask[:, 0, :], 0.0).then_inc(acc.sem, 1)
                for n, (t, h) in enumerate(todo):
                    nk = (t + 1) * P
                    s = index[t][:, :]
                    dve.wait_ge(acts.sem, n + 1)
                    dve.wait_ge(acc.sem, done)
                    wt = wit[:, t, h:h + 1]
                    if h == 0:
                        ins = nc.vector.tensor_scalar(s, rl[:, n % 2, 0:nk], wt, None, ALU.mult)
                    else:
                        ins = nc.vector.scalar_tensor_tensor(s, rl[:, n % 2, 0:nk], wt, s, ALU.mult, ALU.add)
                    ins.then_inc(acc.sem, 1)
                    done += 1
                    if h == 3:
                        dve.wait_ge(acc.sem, done)
                        nc.vector.tensor_tensor(index[t][:, t * P:nk], index[t][:, t * P:nk], later[:, :],
                                                ALU.add).then_inc(acc.sem, 1)
                        done += 1

    def cut_highest(self, index, top):
        nc, found, marked = self.nc, self.sig("idx_found"), self.sig("idx_marked")
        fb, mb = found.base, marked.base
        found.advance(MT * 3)
        marked.advance(MT * 3)

        def side(dve, n):
            for t in range(1, QT):
                dve.wait_ge(marked.sem, n * 3 + (mb + t - 3))
                nc.vector.max(top[:, t, :], index[t][:, :]).then_inc(found.sem, 1)
            for t in range(1, QT):
                dve.wait_ge(found.sem, n * 3 + (fb + t))
                nc.vector.match_replace(index[t][:, :], top[:, t, :], index[t][:, :], CUT).then_inc(marked.sem, 1)
        return side

    def mask_rest(self, index, mask):
        nc, done = self.nc, self.sig("idx_masked")
        with self.block() as block:
            @block.vector
            def _(dve):
                for t in range(1, QT):
                    nc.vector.tensor_scalar(index[t][:, :], index[t][:, :], CUT, 1.0, ALU.is_equal,
                                            ALU.subtract).then_inc(done.sem, 1)
                for t in range(1, QT):
                    dve.wait_ge(done.sem, t)
                    nc.vector.tensor_scalar(mask[:, t, 0:(t + 1) * P], index[t][:, :], -NEG, None, ALU.mult)

    def project_out(self, c, oT, name, bias=None):
        o_hi = self.sb(c, f"o_hi{self.stage_n}", [P, MT, 512], F32R)
        o_lo = self.sb(c, f"o_lo{self.stage_n}", [P, MT, 512], F32R)
        self.stage_n += 1
        split = self.split_tiles(MT, lambda m: oT[:, m, :], lambda m: o_hi[:, m, :], lambda m: o_lo[:, m, :])
        self.add_to_residual(name, lambda k: o_hi[:, k, :], lambda k: o_lo[:, k, :], bias, split)

    def windowed(self):
        nc, d = self.nc, self.d
        hi, lo = self.xs_hi, self.xs_lo
        xh, xl = (lambda k: hi[:, k, :]), (lambda k: lo[:, k, :])
        with ExitStack() as c:
            oT = self.sb(c, "oT_w", [P, MT, 512])
            small = self.sb(c, "win_small", [P, 40])
            bq, bk, bv, bo, sink = small[:, 0:8], small[:, 8:10], small[:, 10:11], small[:, 11:19], small[:, 20:36]
            b = d["a_b_qkv_2"][0]
            col = lambda ap: ap.rearrange("(m p) -> p m", p=ap.shape[0] if ap.shape[0] < P else P)
            window_norm = self.norm_stream(2, ("window_loads", [(bq, col(b[0:1024])), (bv, col(b[1152:1280])), (bo, col(d["a_b_o_2"][0])),
                       (sink, d["a_sinks_2"].broadcast_to([P, NH]))]
                      + [(small[64 * s:64 * s + 64, 8 + g:9 + g], col(b[1024 + 64 * g:1088 + 64 * g]))
                         for s in range(2) for g in range(2)]), wait_loads=True)
            with ExitStack() as c2:
                qT = self.sb(c2, "qT_w", [P, MT, 512])
                kT = self.sb(c2, "kT_w", [P, 2, 512])
                vF = self.sb(c2, "vF_w", [P, 512])
                vt = self.sb(c2, "vt_w", [P, QT, P])
                step = lambda j: [("act", lambda i, ps: nc.scalar.activation(
                    flat(qT[:, rows(i * 2 + j), :]), ps, ACT.Identity, bias=bq[:, rows(i * 2 + j)]))]
                self.dense("a_q", xh, xl, [step(0), step(1)], window_norm)
                dst = [(kT[:, 0, :], bk[:, 0:1]), (kT[:, 1, :], bk[:, 1:2]), (vF[:, :], bv), (vF[:, :], bv)]
                step2 = lambda j: [("act", lambda i, ps: nc.scalar.activation(dst[2 * i + j][0], ps, ACT.Identity,
                                                                              bias=dst[2 * i + j][1]))]
                self.dense("a_kv", xh, xl, [step2(0), step2(1)])
                self.turn(1, lambda m, t: vF[:, t * P:(t + 1) * P], lambda m: vt[:, :, :])

                def keys(t):
                    return (0, P, [(0, P)]) if t == 0 else ((t - 1) * P, 2 * P, [(t - 1, P), (t, P)])
                self.attention(qT, kT, lambda b, r, x: vt[0:r, b, x * HD:(x + 1) * HD], keys, 256, 1, oT, True,
                               sink=sink.rearrange("p (a e) -> p a e", e=2))
            self.project_out(c, oT, "a_out", bias=bo)

    def feed_forward(self, layer):
        nc, d = self.nc, self.d
        w, wd = d["ffn_w_gu_2"][layer], d["ffn_w_down_2"][layer]
        hi, lo = self.xs_hi, self.xs_lo
        T = DFF // P
        with ExitStack() as c:
            a_hi = self.sb(c, f"a_hi{layer}", [P, T, 512], F32R)
            a_lo = self.sb(c, f"a_lo{layer}", [P, T, 512], F32R)
            tmp = self.sb(c, f"ff_tmp{layer}", [P, 2, 512])
            gate = [("act", lambda i, ps: nc.scalar.activation(tmp[:, 0, :], ps, ACT.Silu))]
            up = [("dve", lambda i, ps: nc.vector.tensor_tensor(tmp[:, 1, :], ps, tmp[:, 0, :], ALU.mult)),
                  ("act", lambda i, ps: nc.scalar.activation(flat(a_hi[:, rows(i), :]), tmp[:, 1, :], ACT.Copy)),
                  ("dve", lambda i, ps: nc.vector.tensor_tensor(flat(a_lo[:, rows(i), :]), tmp[:, 1, :],
                                                                flat(a_hi[:, rows(i), :]).bitcast(F32), ALU.subtract))]
            self.dense(f"ff_gu{layer}", lambda k: hi[:, k, :], lambda k: lo[:, k, :], [gate, up],
                       self.norm_stream(4 + layer))
            self.add_to_residual(f"ff_down{layer}", lambda k: a_hi[:, k, :], lambda k: a_lo[:, k, :])

    def sparse(self):
        nc, d = self.nc, self.d
        hi, lo = self.xs_hi, self.xs_lo
        xh, xl = (lambda k: hi[:, k, :]), (lambda k: lo[:, k, :])
        with ExitStack() as c:
            oT = self.sb(c, "oT_s", [P, MT, 512])
            with ExitStack() as c2:
                qT = self.sb(c2, "qT_s", [P, MT, 512])
                kT = self.sb(c2, "kT_s", [P, 2, 2, 512])
                vt = self.sb(c2, "vt_s", [P, 2, QT, P])
                gt = self.sb(c2, "gt_s", [P, QT, P])
                kcT = self.sb(c2, "kcT", [P, 2, 32])
                vc = self.sb(c2, "vc", [32, 2, HD])
                seen = self.sb(c2, "seen", [P, 1])
                with ExitStack() as c3:
                    w1 = self.sb(c3, "cmp_w1", [P, 2, 16, 256])
                    w2 = self.sb(c3, "cmp_w2", [P, 2, 2, P])
                    pos = self.sb(c3, "cmp_pos", [P, 2, 16])
                    w2d = d["b_cmp_w2_2"][0].rearrange("s (m p) c -> s p m c", p=P)
                    sparse_norm = self.norm_stream(3, ("compress_loads", [(seen[:, :], d["c_seen"])] + [pair for s in range(2) for pair in (
                        (pos[:, s], d["b_cmp_pos_2"][0, s].rearrange("(j e) c -> (e c) j", e=2)),
                        (w1[:, s], d["b_cmp_w1_2"][0, s].rearrange("(j p) c -> p j c", p=P)),
                        (w2[:, s, :, 0:HD], w2d[s]), (w2[:, s, :, HD:P], w2d[s]))]))
                    self.dense("b_q", xh, xl, self.keep(lambda i, j: flat(qT[:, rows(i * 2 + j), :])), sparse_norm)
                    cT = self.sb(c3, "cmpT", [P, 2, 2, 512])
                    vF = self.sb(c3, "vF_s", [P, 3, 512])
                    dsts = [dst[:, h, :] for dst in (cT[:, 0], cT[:, 1], kT[:, 0], kT[:, 1]) for h in range(2)]
                    dsts += [vF[:, 0, :], vF[:, 1, :], vF[:, 2, :], vF[:, 2, :]]

                    def step(j):
                        def f(i, ps):
                            return nc.scalar.activation(dsts[2 * i + j], ps, ACT.Sigmoid if 2 * i + j >= 10 else ACT.Copy)
                        return [("act", f)]
                    self.dense("b_rest", xh, xl, [step(0), step(1)])
                    outs = [vt[:, 0], vt[:, 1], gt[:, :, :]]
                    self.turn(3, lambda m, t: vF[:, m, t * P:(t + 1) * P], lambda m: outs[m])
                    self.arrived("compress_loads")
                    self.compress(c3, cT, w1, w2, pos, kcT, vc)
                self.scale_rows(gt[:, 0, :], seen)
                gates = gt[:, :, 80:128].rearrange("p t (a e g) -> p t a e g", e=2, g=3)
                gate = lambda g: lambda pairs, half, t: gates[:, t, pairs, half, g]

                def cmp_keys(t):
                    n = 8 * t + 7
                    return 0, n, [(0, n)]
                self.attention(qT, kcT, lambda b, r, x: vc[0:r, x, :], cmp_keys, 512, 2, oT, True, gate=gate(0),
                               bias_at=lambda t, nk: slice(415 - P * t, 416 - P * t + 16 * (nk - 1), 16))
                for s in range(2):
                    self.attention(qT, kT[:, s], lambda b, r, x: vt[0:r, s, b, x * HD:(x + 1) * HD], self.causal, 512,
                                   2, oT, True, add=True, gate=gate(1 + s))
            self.project_out(c, oT, "b_out")

    def scale_rows(self, gt, seen):
        nc, done = self.nc, self.sig("rows_scaled")
        with self.block() as block:
            @block.vector
            def _(dve):
                g = gt[:, 80:128].rearrange("p (h g) -> p h g", g=3)[:, :, 0]
                nc.vector.tensor_scalar(g, g, seen[:, 0:1], None, ALU.mult).then_inc(done.sem, 1)

    def compress(self, c, cT, w1, w2, pos, kcT, vc):
        nc = self.nc
        N = 2 * NCMP
        blk = self.sb(c, "cmp_blk", [P, 2, 16, N])
        hid = self.sb(c, "cmp_hid", [P, 2, 2 * N])
        arg = self.sb(c, "cmp_arg", [P, 2, 2 * N])
        built, made, step = self.sig("cmp_built"), self.sig("cmp_made"), self.sig("cmp_step")
        second = self.sig("cmp_second")
        h0, a0 = hid[:, :, :], arg[:, :, :]
        with self.block() as block:
            @block.vector
            def _(dve):
                for s in range(2):
                    for half in range(2):
                        r = slice(64 * half, 64 * half + 64)
                        for h in range(2):
                            x = cT[r, s, h, :].rearrange("p (b j e) -> p e j b", j=8, e=2)
                            for b in range(2):
                                ins = nc.vector.tensor_tensor(
                                    blk[r, s, 8 * b:8 * b + 8, NCMP * h:NCMP * (h + 1)], x[:, half, :, b:b + NCMP],
                                    pos[r, s, 8 * b:8 * b + 8].rearrange("p (j a) -> p j a", a=1).broadcast_to([64, 8, NCMP]),
                                    ALU.add)
                    ins.then_inc(built.sem, 1)
                dve.wait_ge(made.sem, 2)
                nc.vector.tensor_copy(h0, self.banks[:, 0:2, 0:2 * N]).then_inc(step.sem, 1)
                dve.wait_ge(step.sem, 1)
                nc.vector.tensor_tensor(a0, h0, h0, ALU.mult).then_inc(step.sem, 1)
                dve.wait_ge(step.sem, 2)
                nc.vector.tensor_scalar(a0, a0, 0.044715, 1.0, ALU.mult, ALU.add).then_inc(step.sem, 1)
                dve.wait_ge(step.sem, 3)
                nc.vector.tensor_tensor(a0, a0, h0, ALU.mult).then_inc(step.sem, 1)
                dve.wait_ge(step.sem, 5)
                nc.vector.tensor_tensor(h0, a0, h0, ALU.mult).then_inc(step.sem, 1)
                dve.wait_ge(second.sem, 1)
                nc.vector.tensor_copy(kcT[:, :, 0:NCMP], self.ps[2][:, 0:N].rearrange("p (h n) -> p h n", h=2))
                nc.vector.tensor_copy(vc[0:NCMP, :, :], self.ps[3][0:NCMP, 0:2 * HD].rearrange("p (h n) -> p h n", h=2))

            @block.scalar
            def _(act):
                act.wait_ge(step.sem, 4)
                nc.scalar.activation(a0, a0, ACT.Sigmoid, scale=2 * math.sqrt(2 / math.pi)).then_inc(step.sem, 1)

            @block.tensor
            def _(pe):
                for s in range(2):
                    pe.wait_ge(built.sem, s + 1)
                    for m in range(2):
                        for j in range(16):
                            ins = nc.tensor.matmul(self.ps[s][:, m * N:(m + 1) * N], w1[:, s, j, m * P:(m + 1) * P],
                                                   blk[:, s, j, :], start=(j == 0), stop=(j == 15))
                    ins.then_inc(made.sem, 1)
                pe.wait_ge(step.sem, 6)
                for m in range(2):
                    nc.tensor.matmul(self.ps[2][:, 0:N], w2[:, 0, m, :], hid[:, 0, m * N:(m + 1) * N], start=(m == 0), stop=(m == 1))
                for h in range(2):
                    for m in range(2):
                        ins = nc.tensor.matmul(self.ps[3][0:NCMP, HD * h:HD * (h + 1)],
                                               hid[:, 1, m * N + NCMP * h:m * N + NCMP * (h + 1)], w2[:, 1, m, 0:HD],
                                               start=(m == 0), stop=(m == 1))
                ins.then_inc(second.sem, 1)

    def finish(self, out, final=True):
        nc = self.nc
        stored = self.sig("stored")
        with ExitStack() as c:
            y = self.sb(c, "y", [P, MT, 512])
            tok = self.sb(c, "tok", [P, QT, DM])
            if final:
                self.run(lambda c2: self.norm(c2, MT, lambda m: self.hT[:, m, :], lambda m: self.gains[:, 6, m:m + 1],
                                              lambda m: y[:, m, :], squares=self.squares))
            src = y if final else self.hT
            self.turn(MT, lambda m, t: src[:, m, t * P:(t + 1) * P], lambda m: tok[:, :, m * P:(m + 1) * P])
            with self.block() as block:
                @block.sync
                def _(sp):
                    sp.dma_start(out[0].rearrange("(t p) c -> p t c", p=P), tok[:, :, :]).then_inc(stored.sem, 16)
                    sp.wait_ge(stored.sem, 16)


def build(nc, dram, out, layers=6):
    with ExitStack() as ctx:
        k = Kernel(nc, dram, ctx)
        k.setup()
        for stage in (k.even, k.odd, k.windowed, lambda: k.feed_forward(0), k.sparse, lambda: k.feed_forward(1))[:layers]:
            stage()
        k.finish(out, layers == 6)


def _buckets(dist, max_dist):
    rel = np.maximum(dist, 0)
    f = np.maximum(rel, 1).astype(np.float32)
    large = 16 + (np.log(f / np.float32(16)) / np.float32(math.log(max_dist / 16)) * np.float32(16)).astype(np.int32)
    return np.where(rel < 16, rel, np.minimum(large, 31))


def _one_hot(max_dist, valid):
    dist = 511 - np.arange(BIAS_L)
    hot = np.zeros((33, BIAS_L), np.float32)
    ok = valid(dist)
    hot[_buckets(dist, max_dist)[ok], np.nonzero(ok)[0]] = 1.0
    hot[32, ~ok] = NEG
    return hot


def _constants():
    pos = np.arange(SEQ)
    cnt = np.stack([1.0 / np.minimum(pos + 1, w).astype(np.float32) for w in (2, 4, 8, 16)]).astype(np.float32)
    feature = np.arange(P)[:, None] + P * np.arange(MT)[None, :]
    member = (feature[:, :, None] // HD == np.arange(NH)).astype(np.float32)
    member4 = (feature[:, :, None] // 256 == np.arange(4)).astype(np.float32)
    return {
        "c_ident": np.eye(P, dtype=np.float32),
        "c_one": np.ones((1, NH), np.float32),
        "c_member": member, "c_spread": member.transpose(2, 1, 0).copy(),
        "c_member4": member4, "c_spread4": member4.transpose(2, 1, 0).copy(),
        "c_pool": np.broadcast_to(cnt, (P, 4, SEQ)).copy(),
        "c_tri": np.triu(np.ones((P, P), np.float32)),
        "c_later": np.where(np.arange(P)[None, :] > np.arange(P)[:, None], BEYOND, 0).astype(np.float32),
        "c_seen": (np.arange(P) >= 31).astype(np.float32).reshape(P, 1),
        "c_hot": np.stack([_one_hot(128, lambda x: x >= 0), _one_hot(1024, lambda x: (x >= 0) & (x < 128)),
                           _one_hot(1024, lambda x: x >= 0)]),
    }


def kernel(**inputs):
    import concourse.bacc as bacc
    from concourse.bass_utils import run_bass_kernel_spmd as run

    nc = bacc.Bacc("TRN2", target_bir_lowering=False, num_devices=1)
    arrays = {n: np.ascontiguousarray(a) for n, a in inputs.items()}
    arrays.update(_constants())
    dram = {n: nc.dram_tensor(f"in_{n}", a.shape, F32, kind="ExternalInput").ap() for n, a in arrays.items()}
    dram["s_rows"] = nc.dram_tensor("s_rows", (2, 4, 512), F32, kind="Internal").ap()
    dram["s_bias"] = nc.dram_tensor("s_bias", (3, NH, BIAS_L), F32, kind="Internal").ap()
    dram["s_skew"] = nc.dram_tensor("s_skew", (3, NH, P, BIAS_L), F32, kind="Internal").ap()
    out = nc.dram_tensor("out", (1, SEQ, DM), F32, kind="ExternalOutput").ap()
    build(nc, dram, out, LAYERS)
    r = run(nc, [{f"in_{n}": a for n, a in arrays.items()}], core_ids=[0])
    return r.results[0]["out"]


LAYERS = 6
```
